# Optimizing a Trainium2 kernel written in Bass

```python
import math
import jax
import jax.numpy as jnp
from jax import lax
import numpy as np

D_MODEL = 1024
BATCH = 1
SEQ = 256
DEPTH = 2

GRID_W = 64
CTX_LEN = 256
N_MIXERS = 2
N_ATTN_LAYERS = (DEPTH + 1) // 2
N_LRU_LAYERS = DEPTH // 2
HEAD_DIM = 64
N_HEADS = 16
N_KV_HEADS = 4
GROUP = N_HEADS // N_KV_HEADS
WINDOW = 128
ATTN_BLOCK = 128
ROPE_THETA = 10000.0
D_RNN = 1280
LRU_BLOCKS = 16
LRU_BLOCK_W = D_RNN // LRU_BLOCKS
CONV_W = 4
CONV_LEFT = 2
LRU_C = 8.0
N_EXPERTS = 64
TOP_K = 8
N_GROUPS = 8
TOPK_GROUPS = 4
D_EXPERT = 256
ROUTED_SCALE = 2.5
MOE_BLOCK = 128
RMS_EPS = 1e-6

kernel_name = 'hybrid_swa_sink_rglru_moe_dit'

def rms_norm(x, g):
    xf = x.astype(jnp.float32)
    y = xf * lax.rsqrt(jnp.mean(xf * xf, axis=-1, keepdims=True) + RMS_EPS)
    return (y * g.astype(jnp.float32)).astype(x.dtype)

def modulate(h, shift, scale):
    return h * (1 + scale) + shift

def swiglu(t, wg, wu, wd):
    return (jax.nn.silu(t @ wg) * (t @ wu)) @ wd

def rope_angles(n_tokens):
    rows = n_tokens // GRID_W
    row = jnp.repeat(jnp.arange(rows), GRID_W).astype(jnp.float32)
    col = jnp.tile(jnp.arange(GRID_W), rows).astype(jnp.float32)
    n_freq = HEAD_DIM // 4
    inv = jnp.exp(-math.log(ROPE_THETA) * jnp.arange(n_freq, dtype=jnp.float32) / n_freq)
    return row[:, None] * inv, col[:, None] * inv

def rotate_axis(u, ang):
    u1, u2 = jnp.split(u, 2, axis=-1)
    shape = (1, ang.shape[0]) + (1,) * (u.ndim - 3) + (ang.shape[-1],)
    cos = jnp.cos(ang).reshape(shape)
    sin = jnp.sin(ang).reshape(shape)
    return jnp.concatenate([u1 * cos - u2 * sin, u2 * cos + u1 * sin], axis=-1)

def rope_2d(u, ang_row, ang_col):
    ur, uc = jnp.split(u, 2, axis=-1)
    return jnp.concatenate([rotate_axis(ur, ang_row), rotate_axis(uc, ang_col)], axis=-1)

def softmax_with_sink(s, sink):
    full = jnp.concatenate([s, jnp.broadcast_to(sink, s.shape[:-1] + (1,))], axis=-1)
    return jax.nn.softmax(full, axis=-1)[..., :-1]

def window_gqa_mixer(h, hc, w_qkv, w_o, sink, ang_row, ang_col, need_ctx):
    f32 = jnp.float32
    B, S, _ = h.shape
    qd = N_HEADS * HEAD_DIM
    kd = N_KV_HEADS * HEAD_DIM
    scale = HEAD_DIM ** -0.5

    def project(t):
        L = t.shape[1]
        p = (t @ w_qkv).astype(f32)
        q = p[..., :qd].reshape(B, L, N_KV_HEADS, GROUP, HEAD_DIM)
        k = p[..., qd:qd + kd].reshape(B, L, N_KV_HEADS, HEAD_DIM)
        v = p[..., qd + kd:].reshape(B, L, N_KV_HEADS, HEAD_DIM)
        return q, k, v

    q, k, v = project(h)
    qc, kc, vc = project(hc)
    q = rope_2d(q, ang_row, ang_col) * scale
    k = rope_2d(k, ang_row, ang_col)
    qc = qc * scale
    sink_b = sink.astype(f32).reshape(1, N_KV_HEADS, GROUP, 1, 1)

    pad = ((0, 0), (WINDOW, WINDOW), (0, 0), (0, 0))
    k_pad = jnp.pad(k, pad)
    v_pad = jnp.pad(v, pad)
    span = ATTN_BLOCK + 2 * WINDOW
    n_blocks = S // ATTN_BLOCK
    q_off = jnp.arange(ATTN_BLOCK)
    k_off = jnp.arange(span) - WINDOW

    def block(n):
        start = n * ATTN_BLOCK
        qb = lax.dynamic_slice_in_dim(q, start, ATTN_BLOCK, axis=1)
        kb = lax.dynamic_slice_in_dim(k_pad, start, span, axis=1)
        vb = lax.dynamic_slice_in_dim(v_pad, start, span, axis=1)
        ipos = start + q_off
        jpos = start + k_off
        valid = (jnp.abs(jpos[None, :] - ipos[:, None]) <= WINDOW) & (jpos[None, :] >= 0) & (jpos[None, :] < S)
        s_loc = jnp.where(valid, jnp.einsum('bqkgd,bskd->bkgqs', qb, kb), -jnp.inf)
        s_ctx = jnp.einsum('bqkgd,bckd->bkgqc', qb, kc)
        p = softmax_with_sink(jnp.concatenate([s_loc, s_ctx], axis=-1), sink_b)
        return (jnp.einsum('bkgqs,bskd->bqkgd', p[..., :span], vb)
                + jnp.einsum('bkgqc,bckd->bqkgd', p[..., span:], vc))

    o = lax.map(block, jnp.arange(n_blocks))
    o = jnp.moveaxis(o, 0, 1).reshape(B, S, qd)
    y = o.astype(h.dtype) @ w_o
    yc = None
    if need_ctx:
        s = jnp.einsum('bqkgd,bskd->bkgqs', qc, kc)
        p = softmax_with_sink(s, sink_b)
        oc = jnp.einsum('bkgqs,bskd->bqkgd', p, vc).reshape(B, hc.shape[1], qd)
        yc = oc.astype(hc.dtype) @ w_o
    return y, yc

def depthwise_conv(t, w, b):
    L = t.shape[1]
    tp = jnp.pad(t, ((0, 0), (CONV_LEFT, CONV_W - 1 - CONV_LEFT), (0, 0)))
    out = tp[:, 0:L] * w[0] + b
    for j in range(1, CONV_W):
        out = out + tp[:, j:j + L] * w[j]
    return out

def rglru_gates(u, wa, ba, wx, bx, lam):
    f32 = jnp.float32
    uf = u.astype(f32)
    ub = uf.reshape(uf.shape[:-1] + (LRU_BLOCKS, LRU_BLOCK_W))
    r = jax.nn.sigmoid(jnp.einsum('blnc,ncd->blnd', ub, wa.astype(f32)).reshape(uf.shape) + ba.astype(f32))
    i_g = jax.nn.sigmoid(jnp.einsum('blnc,ncd->blnd', ub, wx.astype(f32)).reshape(uf.shape) + bx.astype(f32))
    log_a = -LRU_C * r * jax.nn.softplus(-lam.astype(f32))
    a = jnp.exp(log_a)
    b = jnp.sqrt(-jnp.expm1(2.0 * log_a)) * (i_g * uf)
    return a, b

def _lin_combine(left, right):
    a_l, b_l = left
    a_r, b_r = right
    return a_l * a_r, a_r * b_l + b_r

def linear_recurrence(a, b, h0, reverse):
    if reverse:
        b = b.at[:, -1].add(a[:, -1] * h0)
    else:
        b = b.at[:, 0].add(a[:, 0] * h0)
    return lax.associative_scan(_lin_combine, (a, b), reverse=reverse, axis=1)[1]

def rglru_mixer(h, hc, w_in, conv_w, conv_b, wa, ba, wx, bx, lam, w_out, need_ctx):
    f32 = jnp.float32
    B = h.shape[0]
    proj = h @ w_in
    gate = jax.nn.gelu(proj[..., :D_RNN]).astype(f32)
    u = depthwise_conv(proj[..., D_RNN:], conv_w, conv_b)
    proj_c = hc @ w_in
    u_c = depthwise_conv(proj_c[..., D_RNN:], conv_w, conv_b)
    zero = jnp.zeros((B, D_RNN), f32)
    h_lat = []
    h_ctx = []
    for d, reverse in ((0, False), (1, True)):
        a_c, b_c = rglru_gates(u_c, wa[d], ba[d], wx[d], bx[d], lam[d])
        hs_c = linear_recurrence(a_c, b_c, zero, reverse)
        final_c = hs_c[:, 0] if reverse else hs_c[:, -1]
        a, b = rglru_gates(u, wa[d], ba[d], wx[d], bx[d], lam[d])
        h_lat.append(linear_recurrence(a, b, final_c, reverse))
        h_ctx.append(hs_c)
    y = ((h_lat[0] + h_lat[1]) * gate).astype(h.dtype) @ w_out
    yc = None
    if need_ctx:
        gate_c = jax.nn.gelu(proj_c[..., :D_RNN]).astype(f32)
        yc = ((h_ctx[0] + h_ctx[1]) * gate_c).astype(hc.dtype) @ w_out
    return y, yc

def moe_ffn(t, router_w, router_bias, w_gate, w_up, w_down, s_gate, s_up, s_down):
    f32 = jnp.float32
    T, D = t.shape
    scores = jax.nn.sigmoid(t.astype(f32) @ router_w.astype(f32))
    sel = scores + router_bias.astype(f32)
    per_group = N_EXPERTS // N_GROUPS
    group_score = lax.top_k(sel.reshape(T, N_GROUPS, per_group), 2)[0].sum(-1)
    _, top_groups = lax.top_k(group_score, TOPK_GROUPS)
    group_mask = jax.nn.one_hot(top_groups, N_GROUPS, dtype=f32).sum(1) > 0
    expert_mask = jnp.repeat(group_mask, per_group, axis=1)
    _, idx = lax.top_k(jnp.where(expert_mask, sel, -jnp.inf), TOP_K)
    w = jnp.take_along_axis(scores, idx, axis=1)
    w = w / jnp.sum(w, axis=-1, keepdims=True) * ROUTED_SCALE

    A = T * TOP_K
    e_flat = idx.reshape(A)
    tok_flat = jnp.arange(A, dtype=jnp.int32) // TOP_K
    order = jnp.argsort(e_flat)
    e_sorted = e_flat[order]
    tok_sorted = tok_flat[order]
    w_sorted = w.reshape(A)[order]
    counts = jnp.bincount(e_flat, length=N_EXPERTS)
    padded = (counts + MOE_BLOCK - 1) // MOE_BLOCK * MOE_BLOCK
    pad_end = jnp.cumsum(padded)
    pad_start = pad_end - padded
    start = jnp.cumsum(counts) - counts
    dest = pad_start[e_sorted] + jnp.arange(A, dtype=jnp.int32) - start[e_sorted]
    n_blocks = -(-A // MOE_BLOCK) + N_EXPERTS
    P = n_blocks * MOE_BLOCK
    tok_buf = jnp.full((P,), T, jnp.int32).at[dest].set(tok_sorted)
    w_buf = jnp.zeros((P,), f32).at[dest].set(w_sorted)
    block_expert = jnp.minimum(
        jnp.searchsorted(pad_end, jnp.arange(n_blocks, dtype=jnp.int32) * MOE_BLOCK, side='right'),
        N_EXPERTS - 1)
    t_pad = jnp.concatenate([t, jnp.zeros((1, D), t.dtype)], axis=0)

    def expert_block(args):
        tok_b, w_b, e = args
        yb = swiglu(t_pad[tok_b], w_gate[e], w_up[e], w_down[e])
        return yb.astype(f32) * w_b[:, None]

    y = lax.map(expert_block, (tok_buf.reshape(n_blocks, MOE_BLOCK),
                               w_buf.reshape(n_blocks, MOE_BLOCK), block_expert))
    routed = jnp.zeros((T + 1, D), f32).at[tok_buf].add(y.reshape(P, D))[:T]
    shared = swiglu(t, s_gate, s_up, s_down).astype(f32)
    return (routed + shared).astype(t.dtype)

def setup_inputs(seed: int = 0) -> dict:
    key = jax.random.key(seed)
    ks = jax.random.split(key, 32)
    f32 = jnp.float32

    def nrm(k, shape, scale):
        return jax.random.normal(k, shape, f32) * scale

    qkv_cols = (N_HEADS + 2 * N_KV_HEADS) * HEAD_DIM
    u = jax.random.uniform(ks[18], (N_LRU_LAYERS, 2, D_RNN), f32, 0.9, 0.999)
    return {
        'x': nrm(ks[0], (BATCH, SEQ, D_MODEL), 1.0),
        'c': nrm(ks[1], (BATCH, D_MODEL), 1.0),
        'ctx': nrm(ks[2], (BATCH, CTX_LEN, D_MODEL), 1.0),
        'c_ctx': nrm(ks[3], (D_MODEL,), 1.0),
        'ada_w': nrm(ks[4], (DEPTH, D_MODEL, 6 * D_MODEL), 0.5 * D_MODEL ** -0.5),
        'ada_b': nrm(ks[5], (DEPTH, 6 * D_MODEL), 0.02),
        'norm1_g': 1.0 + nrm(ks[6], (DEPTH, D_MODEL), 0.05),
        'norm2_g': 1.0 + nrm(ks[7], (DEPTH, D_MODEL), 0.05),
        'attn_w_qkv': nrm(ks[8], (N_ATTN_LAYERS, D_MODEL, qkv_cols), D_MODEL ** -0.5),
        'attn_w_o': nrm(ks[9], (N_ATTN_LAYERS, N_HEADS * HEAD_DIM, D_MODEL), (N_HEADS * HEAD_DIM) ** -0.5),
        'attn_sink': nrm(ks[10], (N_ATTN_LAYERS, N_HEADS), 0.5),
        'lru_w_in': nrm(ks[11], (N_LRU_LAYERS, D_MODEL, 2 * D_RNN), D_MODEL ** -0.5),
        'lru_conv_w': nrm(ks[12], (N_LRU_LAYERS, CONV_W, D_RNN), CONV_W ** -0.5),
        'lru_conv_b': nrm(ks[13], (N_LRU_LAYERS, D_RNN), 0.02),
        'lru_wa': nrm(ks[14], (N_LRU_LAYERS, 2, LRU_BLOCKS, LRU_BLOCK_W, LRU_BLOCK_W), LRU_BLOCK_W ** -0.5),
        'lru_ba': nrm(ks[15], (N_LRU_LAYERS, 2, D_RNN), 0.02),
        'lru_wx': nrm(ks[16], (N_LRU_LAYERS, 2, LRU_BLOCKS, LRU_BLOCK_W, LRU_BLOCK_W), LRU_BLOCK_W ** -0.5),
        'lru_bx': nrm(ks[17], (N_LRU_LAYERS, 2, D_RNN), 0.02),
        'lru_lam': jnp.log(u) - jnp.log1p(-u),
        'lru_w_out': nrm(ks[19], (N_LRU_LAYERS, D_RNN, D_MODEL), D_RNN ** -0.5),
        'moe_router_w': nrm(ks[20], (DEPTH, D_MODEL, N_EXPERTS), D_MODEL ** -0.5),
        'moe_router_bias': nrm(ks[21], (DEPTH, N_EXPERTS), 0.01),
        'moe_w_gate': nrm(ks[22], (DEPTH, N_EXPERTS, D_MODEL, D_EXPERT), D_MODEL ** -0.5),
        'moe_w_up': nrm(ks[23], (DEPTH, N_EXPERTS, D_MODEL, D_EXPERT), D_MODEL ** -0.5),
        'moe_w_down': nrm(ks[24], (DEPTH, N_EXPERTS, D_EXPERT, D_MODEL), D_EXPERT ** -0.5),
        'shared_w_gate': nrm(ks[25], (DEPTH, D_MODEL, D_EXPERT), D_MODEL ** -0.5),
        'shared_w_up': nrm(ks[26], (DEPTH, D_MODEL, D_EXPERT), D_MODEL ** -0.5),
        'shared_w_down': nrm(ks[27], (DEPTH, D_EXPERT, D_MODEL), D_EXPERT ** -0.5),
        'final_g': 1.0 + nrm(ks[28], (D_MODEL,), 0.05),
    }

def reference(x, c, ctx, c_ctx, ada_w, ada_b, norm1_g, norm2_g, attn_w_qkv, attn_w_o, attn_sink,
              lru_w_in, lru_conv_w, lru_conv_b, lru_wa, lru_ba, lru_wx, lru_bx, lru_lam, lru_w_out,
              moe_router_w, moe_router_bias, moe_w_gate, moe_w_up, moe_w_down,
              shared_w_gate, shared_w_up, shared_w_down, final_g):
    B, S, D = x.shape
    C = ctx.shape[1]
    ang_row, ang_col = rope_angles(S)
    for i in range(DEPTH):
        mod = jax.nn.silu(c) @ ada_w[i] + ada_b[i]
        mod_c = jax.nn.silu(c_ctx) @ ada_w[i] + ada_b[i]
        sh1, sc1, g1, sh2, sc2, g2 = [m[:, None, :] for m in jnp.split(mod, 6, axis=-1)]
        csh1, csc1, cg1, csh2, csc2, cg2 = jnp.split(mod_c, 6, axis=-1)
        need_ctx = i < DEPTH - 1

        h = modulate(rms_norm(x, norm1_g[i]), sh1, sc1)
        hc = modulate(rms_norm(ctx, norm1_g[i]), csh1, csc1)
        j = i // N_MIXERS
        if i % N_MIXERS == 0:
            y, yc = window_gqa_mixer(h, hc, attn_w_qkv[j], attn_w_o[j], attn_sink[j], ang_row, ang_col, need_ctx)
        else:
            y, yc = rglru_mixer(h, hc, lru_w_in[j], lru_conv_w[j], lru_conv_b[j], lru_wa[j], lru_ba[j],
                                lru_wx[j], lru_bx[j], lru_lam[j], lru_w_out[j], need_ctx)
        x = x + g1 * y
        h2 = modulate(rms_norm(x, norm2_g[i]), sh2, sc2)
        moe_args = (moe_router_w[i], moe_router_bias[i], moe_w_gate[i], moe_w_up[i], moe_w_down[i],
                    shared_w_gate[i], shared_w_up[i], shared_w_down[i])
        if need_ctx:
            ctx = ctx + cg1 * yc
            h2c = modulate(rms_norm(ctx, norm2_g[i]), csh2, csc2)
            f = moe_ffn(jnp.concatenate([h2.reshape(B * S, D), h2c.reshape(B * C, D)], axis=0), *moe_args)
            x = x + g2 * f[:B * S].reshape(B, S, D)
            ctx = ctx + cg2 * f[B * S:].reshape(B, C, D)
        else:
            f = moe_ffn(h2.reshape(B * S, D), *moe_args)
            x = x + g2 * f.reshape(B, S, D)
    return rms_norm(x, final_g)


_drawn_inputs = setup_inputs


def setup_inputs(seed=0):
    import zlib

    import numpy as np

    out = dict(_drawn_inputs(seed))
    spreads = {}
    factors = {'attn_sink': 8.0, 'lru_ba': 8.0, 'lru_bx': 6.261}
    for name, (base, spread) in spreads.items():
        noise = np.random.default_rng([zlib.crc32(name.encode()), seed]).standard_normal(out[name].shape)
        drawn = base * np.exp(spread * noise) if base else spread * noise
        out[name] = jnp.asarray(drawn.astype(out[name].dtype))
    for name, factor in factors.items():
        out[name] = (out[name] * factor).astype(out[name].dtype)
    return out
```

```python
import math

import concourse.bass as bass
from concourse import mybir
from contextlib import ExitStack

F32 = mybir.dt.float32
BF16 = mybir.dt.bfloat16
I32 = mybir.dt.int32
U32 = mybir.dt.uint32
ALU = mybir.AluOpType
ACT = mybir.ActivationFunctionType
AX = mybir.AxisListType

P = 128
D = 1024
KD = D // P
SEQ = 256
CTX = 256
TOK = SEQ + CTX
LAT_TILES = SEQ // P
TILES = TOK // P
NMOD = 6
SH1, SC1, GATE1, SH2, SC2, GATE2 = range(NMOD)
EPS = 1e-6
GRID_W = 64
ROPE_THETA = 10000.0

HEADS = 16
KV = 4
GROUP = HEADS // KV
HD = 64
QD = HEADS * HD
KVD = KV * HD
QKV = QD + 2 * KVD
WINDOW = 128
SCALE = HD ** -0.5
NEG = -1e30

RNN = 1280
RB = 16
RW = RNN // RB
TAPS = 4
LEFT = 2

EXPERTS = 64
TOPK = 8
GROUPS = 8
PER_GROUP = EXPERTS // GROUPS
TOP_GROUPS = 4
FE = 256
KF = FE // P
ROUTED_SCALE = 2.5
FAR = 8192.0


def max_blocks(tiles):
    extra = (tiles * P * TOPK - EXPERTS) // P
    return (EXPERTS + extra + 1) // 2 * 2


NBMAX = max_blocks(TILES) + 6

_FIELDS = [("ident", P), ("before", P), ("iota", P), ("mask", LAT_TILES * SEQ), ("before_e", EXPERTS + 1),
           ("upto_e", EXPERTS), ("lower_g", GROUPS * GROUPS), ("tok", TILES), ("negbase", NBMAX),
           ("iota_b", NBMAX), ("rope_c", LAT_TILES * HD), ("rope_s", LAT_TILES * HD)]
FIELD = {}
_at = 0
for _name, _width in _FIELDS:
    FIELD[_name] = (_at, _at + _width)
    _at += _width
TABLE_W = _at


class Chain:

    def __init__(self, eng, sem):
        self.eng, self.sem, self.n = eng, sem, 0

    def done(self, ins):
        self.n += 1
        ins.then_inc(self.sem, 1)
        return self.n

    def link(self, ins):
        self.eng.wait_ge(self.sem, self.done(ins))


class Core:

    def __init__(self, nc, stack, ins, table, out):
        self.nc, self.stack, self.ins, self.out = nc, stack, ins, out
        self.table_dram = table
        self.mod_rows = nc.dram_tensor("mod_rows", (2, 2, NMOD * D), F32, kind="Internal").ap()
        self.h2_rows = nc.dram_tensor("h2_rows", (TOK, D), F32, kind="Internal").ap()
        self.y_rows = nc.dram_tensor("y_rows", (TOK * TOPK, D), F32, kind="Internal").ap()

        self.sems = []

    def sem(self, name):
        self.sems.append(self.nc.alloc_semaphore(name=name))
        return self.sems[-1]

    def recycle_semaphores(self):
        self.nc.clear_and_free_semaphores(self.sems)
        self.nc.all_engine_barrier()
        self.sems = []

    def field(self, name, rows=P):
        a, b = FIELD[name]
        return self.table[0:rows, a:b]


def ada_phase(g):
    nc, ins = g.nc, g.ins
    HALF = NMOD * D // 2
    BUFS = 5
    NB = HALF // 512
    with ExitStack() as st:
        sb = lambda n, s, d=F32: st.enter_context(nc.sbuf_tensor(n, s, d))
        wbuf = sb("ada_wbuf", [P, BUFS, HALF])
        craw = sb("ada_craw", [P, 2, KD])
        cs = sb("ada_cs", [P, KD, 2])
        row = sb("ada_row", [2, 2, NMOD * D])
        bias = sb("ada_bias", [2, 2, NMOD * D])
        gains = sb("ada_gains", [2, 2, 2, D])
        w_ready = [g.sem(f"ada_w_ready{i}") for i in range(BUFS)]
        c_ready, c_silu, used = g.sem("ada_c_ready"), g.sem("ada_c_silu"), g.sem("ada_used")
        evac, row_ready, small = g.sem("ada_evac"), g.sem("ada_row_ready"), g.sem("ada_small")
        stored, chain_s, x_in = g.sem("ada_stored"), g.sem("ada_chain"), g.sem("x_in")
        tiles = [(l, h, k) for l in range(2) for h in range(2) for k in range(KD)]

        with nc.Block() as block:
            @block.sync
            def _(sp):
                sp.dma_start(craw[:, 0, :], ins["c"].rearrange("o (p k) -> p (o k)", k=KD)).then_inc(c_ready, 16)
                sp.dma_start(craw[:, 1, :], ins["c_ctx"].rearrange("(p k) -> p k", k=KD)).then_inc(c_ready, 16)
                for n, (l, h, k) in enumerate(tiles):
                    if n >= BUFS:
                        sp.wait_ge(used, n - BUFS + 1)
                    src = ins["ada_w"][l].rearrange("(p k) n -> p k n", k=KD)[:, k, h * HALF:(h + 1) * HALF]
                    sp.dma_start(wbuf[:, n % BUFS, :], src).then_inc(w_ready[n % BUFS], 16)

            @block.gpsimd
            def _(pool):
                pool.dma_start(g.table[:], g.table_dram).then_inc(x_in, 16)
                for l in range(2):
                    pool.dma_start(bias[:, l, :], ins["ada_b"][l].partition_broadcast(2)).then_inc(small, 16)
                    pool.dma_start(gains[:, l, 0, :], ins["norm1_g"][l].partition_broadcast(2)).then_inc(small, 16)
                    pool.dma_start(gains[:, l, 1, :], ins["norm2_g"][l].partition_broadcast(2)).then_inc(small, 16)
                pool.dma_start(g.x[:, 0:LAT_TILES, :], ins["x"][0].rearrange("(t p) d -> p t d", p=P)).then_inc(x_in, 16)
                pool.dma_start(g.x[:, LAT_TILES:TILES, :], ins["ctx"][0].rearrange("(t p) d -> p t d", p=P)).then_inc(x_in, 16)
                pool.wait_ge(x_in, 48)

            @block.scalar
            def _(act):
                act.wait_ge(c_ready, 32)
                for s in range(2):
                    act.activation(cs[:, :, s], craw[:, s, :], ACT.Silu).then_inc(c_silu, 1)
                for l in range(2):
                    act.wait_ge(row_ready, l + 1)
                    act.dma_start(g.mod_rows[l], row[:, l, :]).then_inc(stored, 16)
                act.wait_ge(stored, 32)

            @block.tensor
            def _(pe):
                pe.wait_ge(c_silu, 2)
                for n, (l, h, k) in enumerate(tiles):
                    pe.wait_ge(w_ready[n % BUFS], 16 * (n // BUFS + 1))
                    if k == 0 and n:
                        pe.wait_ge(evac, n // KD)
                    for j in range(NB):
                        last = pe.matmul(g.ps[0:2, j, :], cs[:, k, :], wbuf[:, n % BUFS, j * 512:(j + 1) * 512],
                                         start=(k == 0), stop=(k == KD - 1))
                    last.then_inc(used, 1)

            @block.vector
            def _(dve):
                chain = Chain(dve, chain_s)
                dve.wait_ge(small, 96)
                for l in range(2):
                    for h in range(2):
                        dve.wait_ge(used, KD * (2 * l + h + 1))
                        part = slice(h * HALF, (h + 1) * HALF)
                        dve.tensor_tensor(row[:, l, part], g.ps[0:2, 0:NB, :].rearrange("p a b -> p (a b)"),
                                          bias[:, l, part], ALU.add).then_inc(evac, 1)
                    dve.wait_ge(evac, 2 * l + 2)
                    for i, sc in enumerate((SC1, SC2)):
                        r = row[:, l, sc * D:(sc + 1) * D]
                        chain.link(dve.scalar_tensor_tensor(r, r, 1.0, gains[:, l, i, :], ALU.add, ALU.mult))
                    dve.sem_inc(row_ready, 1)


class Norm:

    def __init__(self, g, tag, sb, tiles, shift, gain):
        self.g, self.tiles, self.shift, self.gain = g, tiles, shift, gain
        self.h = sb(tag + "_h", [P, 2, D])
        self.hT = sb(tag + "_hT", [P, KD, tiles * P])
        self.sumsq = sb(tag + "_sumsq", [P, tiles])
        self.root = sb(tag + "_root", [P, tiles])
        self.rstd = sb(tag + "_rstd", [P, tiles])
        self.junk = sb(tag + "_sq", [P, D])
        self.squares, self.roots, self.h_ready = g.sem(tag + "_squares"), g.sem(tag + "_roots"), g.sem(tag + "_h_ready")
        self.turned, self.hT_act, self.hT_dve = g.sem(tag + "_turned"), g.sem(tag + "_hT_act"), g.sem(tag + "_hT_dve")
        self.scaled = g.sem(tag + "_scaled")

    def act_stats(self, act):
        for t in range(self.tiles):
            act.activation(self.junk[:], self.g.x[:, t, :], ACT.Square, accum_out=self.sumsq[:, t:t + 1]).then_inc(self.squares, 1)
            act.wait_ge(self.squares, t + 1)
        act.activation(self.root[:], self.sumsq[:], ACT.Sqrt, bias=self.g.eps[:, 0:1], scale=1.0 / D).then_inc(self.roots, 1)

    def act_evacuate(self, act, t):
        act.wait_ge(self.turned, t + 1)
        act.activation(self.hT[:, 0:KD // 2, t * P:(t + 1) * P],
                       self.g.ps[:, 0, :].rearrange("p (k c) -> p k c", c=P), ACT.Copy).then_inc(self.hT_act, 1)

    def dve_rstd(self, dve):
        dve.wait_ge(self.roots, 1)
        dve.reciprocal(self.rstd[:], self.root[:]).then_inc(self.scaled, 1)
        dve.wait_ge(self.scaled, 1)

    def dve_h(self, dve, t, stored=None):
        if t >= 2:
            dve.wait_ge(self.turned, t - 1)
            if stored is not None:
                dve.wait_ge(stored[t % 2], 16 * (t // 2))
        h = self.h[:, t % 2, :]
        dve.scalar_tensor_tensor(h, self.g.x[:, t, :], self.rstd[:, t:t + 1], self.gain(t), ALU.mult, ALU.mult).then_inc(self.scaled, 1)
        dve.wait_ge(self.scaled, t + 2)
        dve.tensor_tensor(h, h, self.shift(t), ALU.add).then_inc(self.h_ready, 1)

    def dve_evacuate(self, dve, t):
        dve.wait_ge(self.turned, t + 1)
        dve.tensor_copy(self.hT[:, KD // 2:KD, t * P:(t + 1) * P],
                        self.g.ps[:, 1, :].rearrange("p (k c) -> p k c", c=P)).then_inc(self.hT_dve, 1)

    def pe_turn(self, pe, t):
        pe.wait_ge(self.h_ready, t + 1)
        if t:
            pe.wait_ge(self.hT_act, t)
            pe.wait_ge(self.hT_dve, t)
        for k in range(KD):
            last = pe.transpose(self.g.ps[:, k // 4, (k % 4) * P:(k % 4 + 1) * P], self.h[:, t % 2, k::KD], self.g.ident)
        last.then_inc(self.turned, 1)

    def wait_hT(self, eng, t):
        eng.wait_ge(self.hT_act, t + 1)
        eng.wait_ge(self.hT_dve, t + 1)




def qkv_phase(g, qT, kT, v):
    nc, ins = g.nc, g.ins
    PAIRS = HEADS // 2
    with ExitStack() as st:
        sb = lambda n, s, d=F32: st.enter_context(nc.sbuf_tensor(n, s, d))
        w = sb("w_qkv", [P, KD, QKV])
        norm = Norm(g, "n1", sb, TILES, lambda t: g.mod(t, SH1), lambda t: g.mod(t, SC1))
        qk = sb("qk", [P, TILES, QD + KVD])
        rot = sb("rot", [P, QD + KVD])
        w_ready, projected, qk_ready = g.sem("qkv_w_ready"), g.sem("qkv_projected"), g.sem("qk_ready")
        qk_evac, v_evac, chain_s = g.sem("qkv_qk_evac"), g.sem("qkv_v_evac"), g.sem("qkv_chain")
        turned, turned_a, turned_v = g.sem("qk_turned"), g.sem("qk_turned_act"), g.sem("qk_turned_dve")
        spans = [(0, 512), (512, QD), (QD, QD + KVD), (QD + KVD, QKV)]
        chunks = [("q", m) for m in range(PAIRS)] + [("k", m) for m in range(KV // 2)]

        with nc.Block() as block:
            @block.sync
            def _(sp):
                sp.dma_start(w[:], ins["attn_w_qkv"][0].rearrange("(p k) n -> p k n", k=KD)).then_inc(w_ready, 16)

            def out_of(m):
                kind, i = chunks[m]
                return (qT if kind == "q" else kT)[:, i, :]

            @block.scalar
            def _(act):
                norm.act_stats(act)
                for t in range(TILES):
                    norm.act_evacuate(act, t)
                for t in range(TILES):
                    act.wait_ge(projected, t + 1)
                    act.activation(v[:, t, :], g.ps[:, 5, 0:KVD], ACT.Copy).then_inc(v_evac, 1)
                for m in range(1, len(chunks), 2):
                    act.wait_ge(turned, m + 1)
                    act.activation(out_of(m), g.ps[:, 6 + m % 2, :], ACT.Copy).then_inc(turned_a, 1)

            @block.vector
            def _(dve):
                chain = Chain(dve, chain_s)
                norm.dve_rstd(dve)
                for t in range(TILES):
                    norm.dve_h(dve, t)
                    norm.dve_evacuate(dve, t)
                for t in range(TILES):
                    dve.wait_ge(projected, t + 1)
                    flat = g.ps[:, 2:5, :].rearrange("p a b -> p (a b)")[:, 0:QD + KVD]
                    if t >= LAT_TILES:
                        dve.tensor_copy(qk[:, t, :], flat).then_inc(qk_evac, 1)
                        continue
                    heads = lambda a: a.rearrange("p (h d) -> p h d", d=HD)
                    halves = lambda a: a.rearrange("p (h x s f) -> p h x s f", x=2, s=2, f=HD // 4)
                    c0 = FIELD["rope_c"][0] + t * HD
                    s0 = FIELD["rope_s"][0] + t * HD
                    nh = HEADS + KV
                    cos = g.table[:, c0:c0 + HD][:, None, :].to_broadcast([P, nh, HD])
                    sin = g.table[:, s0:s0 + HD].rearrange("p (x s f) -> p x s f", x=2, s=2)
                    dve.tensor_tensor(heads(qk[:, t, :]), heads(flat), cos, ALU.mult).then_inc(chain_s, 1)
                    for s in range(2):
                        dve.tensor_tensor(halves(rot[:])[:, :, :, s, :], halves(flat)[:, :, :, 1 - s, :],
                                          sin[:, None, :, s, :].to_broadcast([P, nh, 2, HD // 4]), ALU.mult).then_inc(chain_s, 1)
                    dve.wait_ge(chain_s, 3 * (t + 1))
                    dve.tensor_tensor(qk[:, t, :], qk[:, t, :], rot[:], ALU.add).then_inc(qk_evac, 1)
                    dve.wait_ge(qk_evac, t + 1)
                for m in range(0, len(chunks), 2):
                    dve.wait_ge(turned, m + 1)
                    dve.tensor_copy(out_of(m), g.ps[:, 6 + m % 2, :]).then_inc(turned_v, 1)

            @block.tensor
            def _(pe):
                for t in range(TILES):
                    norm.pe_turn(pe, t)
                pe.wait_ge(w_ready, 16)
                for t in range(TILES):
                    norm.wait_hT(pe, t)
                    if t:
                        pe.wait_ge(qk_evac, t)
                        pe.wait_ge(v_evac, t)
                    for k in range(KD):
                        for j, (c0, c1) in enumerate(spans):
                            cols = w[:, k, c0:c1]
                            if j < 2:
                                cols = cols.rearrange("p (s g d) -> p g s d", s=2, g=GROUP)
                            last = pe.matmul(g.ps[:, 2 + j, 0:c1 - c0], norm.hT[:, k, t * P:(t + 1) * P], cols,
                                             start=(k == 0), stop=(k == KD - 1))
                    last.then_inc(projected, 1)
                pe.wait_ge(qk_evac, TILES)
                for m, (kind, i) in enumerate(chunks):
                    if m >= 2:
                        pe.wait_ge(turned_a if m % 2 else turned_v, m // 2)
                    for t in range(TILES):
                        src = qk[:, t, (QD if kind == "k" else 0) + i * P:(QD if kind == "k" else 0) + (i + 1) * P]
                        last = pe.transpose(g.ps[:, 6 + m % 2, t * P:(t + 1) * P], src, g.ident)
                    last.then_inc(turned, 1)


def attention_phase(g, qT, kT, v, o):
    nc, ins = g.nc, g.ins
    units = [(t, m, s) for t in range(TILES) for m in range(HEADS // 2) for s in range(2)]
    head = lambda m, s: (2 * (m // GROUP) + s) * GROUP + m % GROUP
    first_key = lambda t: 0 if t < LAT_TILES else SEQ
    with ExitStack() as st:
        sb = lambda n, s, d=F32: st.enter_context(nc.sbuf_tensor(n, s, d))
        prob = sb("prob", [P, 2, TOK])
        probT = sb("probT", [P, 2, TOK])
        sink = sb("sink", [P, HEADS])
        negsink = sb("negsink", [P, HEADS])
        top = sb("top", [P, len(units)])
        nbias = sb("nbias", [P, TILES, HEADS])
        rowsum = sb("rowsum", [P, TILES, HEADS])
        sinkexp = sb("sinkexp", [P, TILES, HEADS])
        sink_in, scored, biased, exped = g.sem("sink_in"), g.sem("scored"), g.sem("biased"), g.sem("exped")
        turned, evac_a, evac_v, mixed = g.sem("prob_turned"), g.sem("probT_act"), g.sem("probT_dve"), g.sem("mixed")
        chain_s, o_evac, sink_arg, sink_exp = g.sem("att_chain"), g.sem("o_evac"), g.sem("sink_arg"), g.sem("sink_exp")

        with nc.Block() as block:
            @block.sync
            def _(sp):
                sp.dma_start(sink[:], ins["attn_sink"][0].partition_broadcast(P)).then_inc(sink_in, 16)

            @block.tensor
            def _(pe):
                def scores(u):
                    t, m, s = units[u]
                    if u >= 2:
                        pe.wait_ge(exped, u - 1)
                    rows = slice(HD * s, HD * (s + 1))
                    query = qT[rows, m, t * P:(t + 1) * P]
                    if t < LAT_TILES:
                        pe.matmul(g.ps[:, u % 2, 0:SEQ], query, kT[rows, m // GROUP, 0:SEQ], start=True, stop=False)
                        pe.matmul(g.ps[:, u % 2, 0:SEQ], g.ident_bf[:], g.mask_bf[:, t * SEQ:(t + 1) * SEQ], start=False, stop=True)
                    last = pe.matmul(g.ps[:, u % 2, SEQ:TOK], query, kT[rows, m // GROUP, SEQ:TOK], start=True, stop=True)
                    last.then_inc(scored, 1)

                def turn(u):
                    t, m, s = units[u]
                    pe.wait_ge(exped, u + 1)
                    if u >= 2:
                        pe.wait_ge(evac_a if u % 2 else evac_v, u // 2)
                    for j in range(first_key(t) // P, TILES):
                        last = pe.transpose(g.ps[:, 2 + u % 2, j * P:(j + 1) * P], prob[:, u % 2, j * P:(j + 1) * P], g.ident)
                    last.then_inc(turned, 1)

                def mix(u):
                    t, m, s = units[u]
                    hd = head(m, s)
                    kvh = hd // GROUP
                    pe.wait_ge(evac_a if u % 2 else evac_v, u // 2 + 1)
                    if t >= 2 and m == 0 and s == 0:
                        pe.wait_ge(o_evac, t - 1)
                    bank = 4 + 2 * (t % 2) + hd // 8
                    j0 = first_key(t) // P
                    for j in range(j0, TILES):
                        last = pe.matmul(g.ps[:, bank, (hd % 8) * HD:(hd % 8 + 1) * HD], probT[:, u % 2, j * P:(j + 1) * P],
                                         v[:, j, kvh * HD:(kvh + 1) * HD], start=(j == j0), stop=(j == TILES - 1))
                    last.then_inc(mixed, 1)

                scores(0)
                for u in range(len(units)):
                    if u + 1 < len(units):
                        scores(u + 1)
                    turn(u)
                    if u:
                        mix(u - 1)
                mix(len(units) - 1)

            @block.vector
            def _(dve):
                chain = Chain(dve, chain_s)
                dve.wait_ge(sink_in, 16)
                chain.link(dve.tensor_scalar(negsink[:], sink[:], -1.0, None, ALU.mult))

                def finish(t):
                    dve.wait_ge(biased, HEADS * (t + 1))
                    chain.link(dve.tensor_tensor(sinkexp[:, t, :], nbias[:, t, :], sink[:], ALU.add))
                    dve.sem_inc(sink_arg, 1)
                    dve.wait_ge(sink_exp, t + 1)
                    dve.wait_ge(exped, HEADS * (t + 1))
                    chain.link(dve.tensor_tensor(rowsum[:, t, :], rowsum[:, t, :], sinkexp[:, t, :], ALU.add))
                    chain.link(dve.reciprocal(rowsum[:, t, :], rowsum[:, t, :]))
                    dve.wait_ge(mixed, HEADS * (t + 1))
                    b = 4 + 2 * (t % 2)
                    dve.tensor_tensor(o[:, t, :].rearrange("p (h d) -> p h d", d=HD),
                                      g.ps[:, b:b + 2, :].rearrange("p a (h d) -> p (a h) d", d=HD),
                                      rowsum[:, t, :, None].to_broadcast([P, HEADS, HD]), ALU.mult).then_inc(o_evac, 1)

                for u, (t, m, s) in enumerate(units):
                    hd = head(m, s)
                    dve.wait_ge(scored, u + 1)
                    chain.link(dve.reduce_max(top[:, u:u + 1], g.ps[:, u % 2, first_key(t):TOK], AX.X))
                    dve.tensor_scalar(nbias[:, t, hd:hd + 1], top[:, u:u + 1], -SCALE, negsink[:, hd:hd + 1],
                                      ALU.mult, ALU.min).then_inc(biased, 1)
                    if u >= 1 and (u - 1) % 2 == 0:
                        w = u - 1
                        dve.wait_ge(turned, w + 1)
                        if w >= 2:
                            dve.wait_ge(mixed, w - 1)
                        k0 = first_key(units[w][0])
                        dve.tensor_copy(probT[:, w % 2, k0:TOK], g.ps[:, 2 + w % 2, k0:TOK]).then_inc(evac_v, 1)
                    if u % HEADS == 3 and t:
                        finish(t - 1)
                finish(TILES - 1)

            @block.scalar
            def _(act):
                def copy(w):
                    act.wait_ge(turned, w + 1)
                    if w >= 2:
                        act.wait_ge(mixed, w - 1)
                    k0 = first_key(units[w][0])
                    act.activation(probT[:, w % 2, k0:TOK], g.ps[:, 2 + w % 2, k0:TOK], ACT.Copy).then_inc(evac_a, 1)

                def sink_terms(t):
                    act.wait_ge(sink_arg, t + 1)
                    act.activation(sinkexp[:, t, :], sinkexp[:, t, :], ACT.Exp).then_inc(sink_exp, 1)

                for u, (t, m, s) in enumerate(units):
                    hd = head(m, s)
                    k0 = first_key(t)
                    act.wait_ge(biased, u + 1)
                    if u >= 2:
                        act.wait_ge(turned, u - 1)
                    act.activation(prob[:, u % 2, k0:TOK], g.ps[:, u % 2, k0:TOK], ACT.Exp, bias=nbias[:, t, hd:hd + 1],
                                   scale=SCALE, accum_out=rowsum[:, t, hd:hd + 1]).then_inc(exped, 1)
                    if u >= 1 and (u - 1) % 2 == 1:
                        copy(u - 1)
                    if u % HEADS == 3 and t:
                        sink_terms(t - 1)
                copy(len(units) - 1)
                sink_terms(TILES - 1)


def project_phase(g, tag, w_dram, kp, nk, tiles, srcT=None, src=None):
    nc = g.nc
    with ExitStack() as st:
        sb = lambda n, s, d=F32: st.enter_context(nc.sbuf_tensor(n, s, d))
        w = sb(tag + "_w", [kp, nk, D])
        if srcT is None:
            srcT = sb(tag + "_srcT", [P, KD, tiles * P])
        gated = sb(tag + "_gated", [P, 2, D])
        w_ready, turned, done = g.sem(tag + "_w_ready"), g.sem(tag + "_turned"), g.sem(tag + "_done")
        turned_a, turned_v = g.sem(tag + "_turned_act"), g.sem(tag + "_turned_dve")
        gated_s, added = g.sem(tag + "_gated_s"), g.sem(tag + "_added")

        with nc.Block() as block:
            @block.sync
            def _(sp):
                sp.dma_start(w[:], w_dram).then_inc(w_ready, 16)

            @block.tensor
            def _(pe):
                if src is not None:
                    for t in range(tiles):
                        if t:
                            pe.wait_ge(turned_a, t)
                            pe.wait_ge(turned_v, t)
                        for k in range(KD):
                            last = pe.transpose(g.ps[:, k // 4, (k % 4) * P:(k % 4 + 1) * P], src[:, t, k::KD], g.ident)
                        last.then_inc(turned, 1)
                pe.wait_ge(w_ready, 16)
                for t in range(tiles):
                    if src is not None:
                        pe.wait_ge(turned_a, t + 1)
                        pe.wait_ge(turned_v, t + 1)
                    if t >= 2:
                        pe.wait_ge(gated_s, t - 1)
                    for k in range(nk):
                        for j in range(2):
                            last = pe.matmul(g.ps[:, 4 + 2 * (t % 2) + j, :], srcT[:, k, t * P:(t + 1) * P],
                                             w[:, k, j * 512:(j + 1) * 512], start=(k == 0), stop=(k == nk - 1))
                    last.then_inc(done, 1)

            @block.scalar
            def _(act):
                if src is not None:
                    for t in range(tiles):
                        act.wait_ge(turned, t + 1)
                        act.activation(srcT[:, 0:KD // 2, t * P:(t + 1) * P],
                                       g.ps[:, 0, :].rearrange("p (k c) -> p k c", c=P), ACT.Copy).then_inc(turned_a, 1)

            @block.vector
            def _(dve):
                if src is not None:
                    for t in range(tiles):
                        dve.wait_ge(turned, t + 1)
                        dve.tensor_copy(srcT[:, KD // 2:KD, t * P:(t + 1) * P],
                                        g.ps[:, 1, :].rearrange("p (k c) -> p k c", c=P)).then_inc(turned_v, 1)
                for t in range(tiles):
                    dve.wait_ge(done, t + 1)
                    if t >= 2:
                        dve.wait_ge(added, t - 1)
                    y = g.ps[:, 4 + 2 * (t % 2):6 + 2 * (t % 2), :].rearrange("p a b -> p (a b)")
                    dve.tensor_tensor(gated[:, t % 2, :], y, g.mod(t, GATE1), ALU.mult).then_inc(gated_s, 1)
                    dve.wait_ge(gated_s, t + 1)
                    dve.tensor_tensor(g.x[:, t, :], g.x[:, t, :], gated[:, t % 2, :], ALU.add).then_inc(added, 1)


class Routes:

    def __init__(self, sb, layer, tiles):
        n = f"l{layer}_"
        self.slot = sb(n + "slot", [P, tiles, EXPERTS])
        self.entry = sb(n + "entry", [P, tiles, EXPERTS, 3])
        self.expert = sb(n + "expert", [1, NBMAX], I32)
        self.count = sb(n + "count", [1, 1], I32)


def route_phase(g, layer, tiles, routes):
    nc, ins = g.nc, g.ins
    tag = f"r{layer}"
    E = EXPERTS
    with ExitStack() as st:
        sb = lambda n, s, d=F32: st.enter_context(nc.sbuf_tensor(f"{tag}_{n}", s, d))
        sem = lambda n: g.sem(f"{tag}_{n}")
        norm = Norm(g, f"n2_{layer}", lambda n, s, d=F32: st.enter_context(nc.sbuf_tensor(n, s, d)), tiles,
                    lambda t: g.mod(t, SH2), lambda t: g.mod(t, SC2))
        wr = sb("wr", [P, KD, E])
        wgu = sb("wgu", [P, 2, KD, FE])
        wd = sb("wd", [P, KF, D])
        rbias = sb("rbias", [P, E])
        act_g = sb("act_g", [P, FE])
        hid = sb("hid", [P, FE])
        hidT = sb("hidT", [P, KF, P])
        gated = sb("gated", [P, D])
        score = sb("score", [P, tiles, E])
        sel = sb("sel", [P, tiles, E])
        best = sb("best", [P, tiles, GROUPS, 8])
        gscore = sb("gscore", [P, tiles, GROUPS])
        beats = sb("beats", [P, tiles, GROUPS, GROUPS])
        ties = sb("ties", [P, tiles, GROUPS, GROUPS])
        rank = sb("rank", [P, tiles, GROUPS])
        pen = sb("pen", [P, tiles, GROUPS])
        top8 = sb("top8", [P, tiles, 8])
        chosen = sb("chosen", [P, tiles, E])
        chosen_bf = sb("chosen_bf", [P, tiles, E], BF16)
        weight = sb("weight", [P, tiles, E])
        wsum = sb("wsum", [P, tiles])
        kth = sb("kth", [P, tiles, E])
        nblk = sb("nblk", [E, 1])
        over = sb("over", [E, TILES])
        blkend = sb("blkend", [E, 1])
        covers = sb("covers", [E, NBMAX])
        blkstart = sb("blkstart", [P, E + 1])
        w_in, h_stored = sem("w_in"), [sem("h_stored0"), sem("h_stored1")]
        routed, scored, gu_done, silued, hid_s = sem("routed"), sem("scored"), sem("gu_done"), sem("silued"), sem("hid_s")
        turned, hidT_s, y_done, gated_s = sem("hid_turned"), sem("hidT_s"), sem("y_done"), sem("gated_s")
        chain_s, masks, pos_done, nblk_s, ends = sem("chain"), sem("masks"), sem("pos_done"), sem("nblk_s"), sem("ends")
        covers_s, owners, blkend_s, xadd = sem("covers_s"), sem("owners"), sem("blkend_s"), sem("xadd")

        with nc.Block() as block:
            @block.sync
            def _(sp):
                sp.dma_start(wr[:], ins["moe_router_w"][layer].rearrange("(p k) e -> p k e", k=KD)).then_inc(w_in, 16)
                sp.dma_start(rbias[:], ins["moe_router_bias"][layer].partition_broadcast(P)).then_inc(w_in, 16)
                sp.dma_start(wgu[:, 0, :, :], ins["shared_w_gate"][layer].rearrange("(p k) f -> p k f", k=KD)).then_inc(w_in, 16)
                sp.dma_start(wgu[:, 1, :, :], ins["shared_w_up"][layer].rearrange("(p k) f -> p k f", k=KD)).then_inc(w_in, 16)
                sp.dma_start(wd[:], ins["shared_w_down"][layer].rearrange("(p j) d -> p j d", j=KF)).then_inc(w_in, 16)
                for t in range(tiles):
                    sp.wait_ge(norm.h_ready, t + 1)
                    sp.dma_start(g.h2_rows[t * P:(t + 1) * P, :], norm.h[:, t % 2, :]).then_inc(h_stored[t % 2], 16)
                for i in range(2):
                    sp.wait_ge(h_stored[i], 16 * (tiles // 2))

            @block.tensor
            def _(pe):
                for t in range(tiles):
                    norm.pe_turn(pe, t)
                pe.wait_ge(w_in, 80)
                for t in range(tiles):
                    norm.wait_hT(pe, t)
                    for k in range(KD):
                        last = pe.matmul(g.ps[:, 7, t * E:(t + 1) * E], norm.hT[:, k, t * P:(t + 1) * P], wr[:, k, :],
                                         start=(k == 0), stop=(k == KD - 1))
                last.then_inc(routed, 1)
                for t in range(tiles):
                    if t:
                        pe.wait_ge(hid_s, t)
                    for k in range(KD):
                        last = pe.matmul(g.ps[:, 4, :].rearrange("p (a f) -> p a f", a=2), norm.hT[:, k, t * P:(t + 1) * P],
                                         wgu[:, :, k, :], start=(k == 0), stop=(k == KD - 1))
                    last.then_inc(gu_done, 1)
                    pe.wait_ge(hid_s, t + 1)
                    if t:
                        pe.wait_ge(hidT_s, t)
                    for j in range(KF):
                        last = pe.transpose(g.ps[:, 2, j * P:(j + 1) * P], hid[:, j::KF], g.ident)
                    last.then_inc(turned, 1)
                    pe.wait_ge(hidT_s, t + 1)
                    if t:
                        pe.wait_ge(gated_s, t)
                    for j in range(KF):
                        for n in range(2):
                            last = pe.matmul(g.ps[:, 5 + n, :], hidT[:, j, :], wd[:, j, n * 512:(n + 1) * 512],
                                             start=(j == 0), stop=(j == KF - 1))
                    last.then_inc(y_done, 1)
                pe.wait_ge(masks, 1)
                for t in range(tiles):
                    for t0 in range(t + 1):
                        pe.matmul(g.ps[:, 3, t * E:(t + 1) * E], g.before_bf[:] if t0 == t else g.ones_bf[:],
                                  chosen_bf[:, t0, :], start=(t0 == 0), stop=(t0 == t))
                for t in range(tiles):
                    last = pe.matmul(g.ps[0:E, 4, 0:1], chosen_bf[:, t, :], g.ones_bf[:, 0:1], start=(t == 0), stop=(t == tiles - 1))
                last.then_inc(pos_done, 1)
                pe.wait_ge(nblk_s, 1)
                pe.matmul(g.ps[:, 5, 0:E + 1], nblk[:, 0:1].to_broadcast([E, P]), g.field("before_e", E), start=True, stop=True)
                pe.matmul(g.ps[0:E, 6, 0:1], g.field("upto_e", E), nblk[:], start=True, stop=True).then_inc(ends, 1)
                pe.wait_ge(covers_s, 1)
                pe.matmul(g.ps[:, 4, 0:NBMAX], g.ones[0:E, :], covers[:], start=True, stop=True).then_inc(owners, 1)

            @block.scalar
            def _(act):
                norm.act_stats(act)
                for t in range(tiles):
                    norm.act_evacuate(act, t)
                act.wait_ge(routed, 1)
                act.activation(score[:], g.ps[:, 7, 0:tiles * E].rearrange("p (t e) -> p t e", e=E), ACT.Sigmoid).then_inc(scored, 1)
                for t in range(tiles):
                    act.wait_ge(gu_done, t + 1)
                    act.activation(act_g[:], g.ps[:, 4, 0:FE], ACT.Silu).then_inc(silued, 1)
                    act.wait_ge(turned, t + 1)
                    act.activation(hidT[:], g.ps[:, 2, 0:FE].rearrange("p (j c) -> p j c", c=P), ACT.Copy).then_inc(hidT_s, 1)

            @block.vector
            def _(dve):
                chain = Chain(dve, chain_s)
                norm.dve_rstd(dve)
                for t in range(tiles):
                    norm.dve_h(dve, t, stored=h_stored)
                    norm.dve_evacuate(dve, t)
                for t in range(tiles):
                    dve.wait_ge(silued, t + 1)
                    dve.tensor_tensor(hid[:], act_g[:], g.ps[:, 4, FE:2 * FE], ALU.mult).then_inc(hid_s, 1)
                    dve.wait_ge(y_done, t + 1)
                    if t:
                        dve.wait_ge(xadd, t)
                    dve.tensor_tensor(gated[:], g.ps[:, 5:7, :].rearrange("p a b -> p (a b)"), g.mod(t, GATE2), ALU.mult).then_inc(gated_s, 1)
                    dve.wait_ge(gated_s, t + 1)
                    dve.tensor_tensor(g.x[:, t, :], g.x[:, t, :], gated[:], ALU.add).then_inc(xadd, 1)

                dve.wait_ge(scored, 1)
                dve.wait_ge(w_in, 80)
                by_group = lambda a: a.rearrange("p t (g e) -> p t g e", e=PER_GROUP)
                chain.link(dve.tensor_tensor(sel[:], score[:], rbias[:, None, :].to_broadcast([P, tiles, E]), ALU.add))
                for t in range(tiles):
                    for gr in range(GROUPS):
                        last = dve.max(best[:, t, gr, :], sel[:, t, gr * PER_GROUP:(gr + 1) * PER_GROUP])
                        n = chain.done(last)
                dve.wait_ge(chain_s, n)
                chain.link(dve.tensor_tensor(gscore[:], best[:, :, :, 0], best[:, :, :, 1], ALU.add))
                mine = gscore[:, :, :, None].to_broadcast([P, tiles, GROUPS, GROUPS])
                other = gscore[:, :, None, :].to_broadcast([P, tiles, GROUPS, GROUPS])
                lower = g.field("lower_g").rearrange("p (a b) -> p a b", b=GROUPS)
                chain.done(dve.tensor_tensor(beats[:], other, mine, ALU.is_gt))
                chain.link(dve.tensor_tensor(ties[:], other, mine, ALU.is_equal))
                chain.link(dve.tensor_tensor(ties[:], ties[:], lower[:, None, :, :].to_broadcast([P, tiles, GROUPS, GROUPS]), ALU.mult))
                chain.link(dve.tensor_tensor(beats[:], beats[:], ties[:], ALU.add))
                chain.link(dve.tensor_reduce(rank[:], beats[:], AX.X, ALU.add))
                chain.link(dve.tensor_scalar(rank[:], rank[:], float(TOP_GROUPS), None, ALU.is_lt))
                chain.link(dve.tensor_scalar(pen[:], rank[:], -NEG, NEG, ALU.mult, ALU.add))
                wide = lambda a: a[:, :, :, None].to_broadcast([P, tiles, GROUPS, PER_GROUP])
                chain.link(dve.tensor_tensor(by_group(sel[:]), by_group(sel[:]), wide(rank[:]), ALU.mult))
                chain.link(dve.tensor_tensor(by_group(sel[:]), by_group(sel[:]), wide(pen[:]), ALU.add))
                for t in range(tiles):
                    n = chain.done(dve.max(top8[:, t, :], sel[:, t, :]))
                dve.wait_ge(chain_s, n)
                for t in range(tiles):
                    n = chain.done(dve.match_replace(chosen[:, t, :], top8[:, t, :], sel[:, t, :], -3e38))
                dve.wait_ge(chain_s, n)
                chain.link(dve.tensor_scalar(chosen[:], chosen[:], -2e38, None, ALU.is_lt))
                dve.tensor_copy(chosen_bf[:], chosen[:]).then_inc(masks, 1)
                chain.link(dve.tensor_tensor(weight[:], score[:], chosen[:], ALU.mult))
                chain.link(dve.tensor_reduce(wsum[:], weight[:], AX.X, ALU.add))
                chain.link(dve.reciprocal(wsum[:], wsum[:]))
                chain.link(dve.tensor_scalar(wsum[:], wsum[:], ROUTED_SCALE, None, ALU.mult))
                chain.done(dve.tensor_tensor(routes.entry[:, :, :, 1], weight[:], wsum[:, :, None].to_broadcast([P, tiles, E]), ALU.mult))
                for t in range(tiles):
                    n = chain.done(dve.tensor_tensor_scan(kth[:, t, :], g.ones[:, 0:E], chosen[:, t, :], 0.0, ALU.mult, ALU.add))
                tok = g.field("tok")[:, 0:tiles]
                chain.done(dve.tensor_scalar(routes.entry[:, :, :, 0], tok[:, :, None].to_broadcast([P, tiles, E]), -FAR, None, ALU.add))
                dve.wait_ge(chain_s, n)
                for t in range(tiles):
                    chain.link(dve.tensor_scalar(wsum[:, t:t + 1], tok[:, t:t + 1], float(TOPK), -1.0 - FAR, ALU.mult, ALU.add))
                    chain.done(dve.tensor_scalar(routes.entry[:, t, :, 2], kth[:, t, :], wsum[:, t:t + 1], None, ALU.add))
                dve.wait_ge(pos_done, 1)
                for j in range(1, tiles):
                    chain.link(dve.tensor_scalar(over[:, j:j + 1], g.ps[0:E, 4, 0:1], float(P * j), None, ALU.is_gt))
                if tiles > 2:
                    chain.link(dve.tensor_reduce(over[:, 0:1], over[:, 1:tiles], AX.X, ALU.add))
                src = over[:, 0:1] if tiles > 2 else over[:, 1:2]
                dve.tensor_scalar(nblk[:], src, 1.0, None, ALU.add).then_inc(nblk_s, 1)
                dve.wait_ge(ends, 1)
                chain.done(dve.tensor_copy(blkstart[:], g.ps[:, 5, 0:E + 1]))
                chain.link(dve.tensor_copy(blkend[:], g.ps[0:E, 6, 0:1]))
                dve.tensor_scalar(covers[:], g.field("iota_b", E), blkend[:, 0:1], None, ALU.is_ge).then_inc(covers_s, 1)
                chain.done(dve.tensor_scalar(routes.count[:], blkstart[0:1, E:E + 1], -1.0, None, ALU.add))
                chain.link(dve.tensor_scalar(blkstart[:, 0:E], blkstart[:, 0:E], float(P), 1.0, ALU.mult, ALU.add))
                pos = g.ps[:, 3, 0:tiles * E].rearrange("p (t e) -> p t e", e=E)
                chain.link(dve.tensor_tensor(routes.slot[:], pos, blkstart[:, None, 0:E].to_broadcast([P, tiles, E]), ALU.add))
                chain.link(dve.tensor_tensor(routes.slot[:], routes.slot[:], chosen[:], ALU.mult))
                chain.link(dve.tensor_scalar(routes.slot[:], routes.slot[:], -1.0, None, ALU.add))
                dve.wait_ge(owners, 1)
                chain.link(dve.tensor_scalar(routes.expert[:], g.ps[0:1, 4, 0:NBMAX], float(E - 1), None, ALU.min))


def expert_phase(g, layer, tiles, routes):
    nc, ins = g.nc, g.ins
    tag = f"m{layer}"
    last_token, last_row = tiles * P - 1, tiles * P * TOPK - 1
    with ExitStack() as st:
        sb = lambda n, s, d=F32: st.enter_context(nc.sbuf_tensor(f"{tag}_{n}", s, d))
        sem = lambda n: g.sem(f"{tag}_{n}")
        wgu = sb("wgu", [P, 2, 2, KD, FE])
        wd = sb("wd", [P, 2, KF, D])
        xg = [sb(f"xg{q}", [P, D]) for q in range(2)]
        xT = sb("xT", [P, 2, KD, P])
        onehot = sb("onehot", [P, 2, tiles, P])
        meta = sb("meta", [P, NBMAX, 3])
        gidx = [sb(f"gidx{q}", [P, 1], U32) for q in range(2)]
        sidx = [sb(f"sidx{q}", [P, 1], U32) for q in range(2)]
        act_g = sb("act_g", [P, FE])
        hid = sb("hid", [P, FE])
        hidT = sb("hidT", [P, KF, P])
        ysb = [sb(f"ysb{q}", [P, D]) for q in range(2)]
        pair = lambda n: [sem(n + "0"), sem(n + "1")]
        wgu_in, wd_in, gathered, scattered = pair("wgu_in"), pair("wd_in"), pair("gathered"), pair("scattered")
        onehot_s, meta_done, idx_s, xT_turned, xT_a, xT_v = (sem(n) for n in ("onehot_s", "meta_done", "idx_s", "xT_turned", "xT_a", "xT_v"))
        gu_done, silued, hid_s, hid_turned, hidT_s = (sem(n) for n in ("gu_done", "silued", "hid_s", "hid_turned", "hidT_s"))
        y_done, y_a, y_v, sidx_s, zeroed, issue, meta_v = (sem(n) for n in ("y_done", "y_a", "y_v", "sidx_s", "zeroed", "issue", "meta_v"))
        GU, YB, XB, HB, MB = 0, 1, 3, 5, 6

        gate_w = ins["moe_w_gate"][layer].rearrange("e (p k) f -> e p k f", k=KD)
        up_w = ins["moe_w_up"][layer].rearrange("e (p k) f -> e p k f", k=KD)
        down_w = ins["moe_w_down"][layer].rearrange("e (p j) d -> e p j d", j=KF)

        def last_pair(eng):
            return eng.value_load(routes.count[0:1, 0:1], min_val=EXPERTS - 1, max_val=max_blocks(tiles) - 1) >> 1

        def owner(eng, b):
            return eng.value_load(routes.expert[0:1, bass.ds(b, 1)], min_val=0, max_val=EXPERTS - 1)

        with nc.Block() as block:
            @block.sync
            def _(sp):
                def gate_up(i, q):
                    b = 2 * i + q
                    e = owner(sp, b)
                    if not (isinstance(i, int) and i == 0):
                        sp.wait_ge(gu_done, b - 1)
                        sp.sem_inc(issue, 1)
                    for a, w in enumerate((gate_w, up_w)):
                        sp.dma_start(wgu[:, q, a, :, :], w[bass.ds(e, 1)].rearrange("o p k f -> p (o k) f")).then_inc(wgu_in[q], 16)

                def down(i, q):
                    b = 2 * i + q
                    e = owner(sp, b)
                    if not (isinstance(i, int) and i == 0):
                        sp.wait_ge(y_done, b - 1)
                        sp.sem_inc(issue, 1)
                    sp.dma_start(wd[:, q, :, :], down_w[bass.ds(e, 1)].rearrange("o p j d -> p (o j) d")).then_inc(wd_in[q], 16)

                final = last_pair(sp)
                gate_up(0, 0)
                down(0, 0)
                gate_up(0, 1)
                gate_up(1, 0)
                down(0, 1)
                gate_up(1, 1)
                down(1, 0)
                with sp.Fori(2, final + 1) as i:
                    gate_up(i, 0)
                    down(i - 1, 1)
                    gate_up(i, 1)
                    down(i, 0)
                down(final, 1)

            @block.gpsimd
            def _(pool):
                def gather(i, q):
                    b = 2 * i + q
                    pool.wait_ge(idx_s, b + 1)
                    if not (isinstance(i, int) and i == 0):
                        pool.wait_ge(xT_turned, b - 1)
                    pool.sem_inc(issue, 1)
                    pool.indirect_dma_start(xg[q][:], None, g.h2_rows[0:tiles * P, :], bass.IndirectOffsetOnAxis(ap=gidx[q][:, 0:1], axis=0),
                                            bounds_check=last_token, oob_is_err=False).then_inc(gathered[q], 16)

                def scatter(i, q):
                    b = 2 * i + q
                    pool.wait_ge(y_a, b + 1)
                    pool.wait_ge(y_v, b + 1)
                    pool.wait_ge(sidx_s, b + 1)
                    pool.sem_inc(issue, 1)
                    pool.indirect_dma_start(g.y_rows[0:tiles * P * TOPK, :], bass.IndirectOffsetOnAxis(ap=sidx[q][:, 0:1], axis=0), ysb[q][:], None,
                                            bounds_check=last_row, oob_is_err=False).then_inc(scattered[q], 16)

                for q in range(2):
                    pool.memset(xg[q][:], 0.0).then_inc(zeroed, 1)
                pool.wait_ge(zeroed, 2)
                final = last_pair(pool)
                gather(0, 0)
                gather(0, 1)
                gather(1, 0)
                scatter(0, 0)
                gather(1, 1)
                with pool.Fori(1, final + 1) as i:
                    scatter(i - 1, 1)
                    gather(i + 1, 0)
                    scatter(i, 0)
                    gather(i + 1, 1)
                scatter(final, 1)
                for q in range(2):
                    pool.wait_ge(scattered[q], 16 * final + 16)
                    pool.sem_inc(issue, 1)
                    pool.wait_ge(gathered[q], 16 * final + 32)
                    pool.sem_inc(issue, 1)

            @block.tensor
            def _(pe):
                def slots(i, q):
                    b = 2 * i + q
                    e = owner(pe, b)
                    pe.wait_ge(onehot_s, b + 1)
                    if not (isinstance(i, int) and i == 0):
                        pe.wait_ge(idx_s, b - 1)
                    for t in range(tiles):
                        last = pe.matmul(g.ps[:, MB + q, 0:3], onehot[:, q, t, :],
                                         routes.entry[:, t, bass.ds(e, 1), :].rearrange("p o c -> p (o c)"),
                                         start=(t == 0), stop=(t == tiles - 1))
                    last.then_inc(meta_done, 1)

                def turn_tokens(i, q, first=False):
                    b = 2 * i + q
                    pe.wait_ge(gathered[q], 16 * (i + 1))
                    if not first:
                        pe.wait_ge(xT_a, b)
                        pe.wait_ge(xT_v, b)
                    for k in range(KD):
                        last = pe.transpose(g.ps[:, XB + k // 4, (k % 4) * P:(k % 4 + 1) * P], xg[q][:, k::KD], g.ident)
                    last.then_inc(xT_turned, 1)

                def down(i, q, first=False):
                    b = 2 * i + q
                    pe.wait_ge(hidT_s, b + 1)
                    pe.wait_ge(wd_in[q], 16 * (i + 1))
                    if not first:
                        pe.wait_ge(y_a, b)
                        pe.wait_ge(y_v, b)
                    for j in range(KF):
                        for n in range(2):
                            last = pe.matmul(g.ps[:, YB + n, :], hidT[:, j, :], wd[:, q, j, n * 512:(n + 1) * 512],
                                             start=(j == 0), stop=(j == KF - 1))
                    last.then_inc(y_done, 1)

                def step(i, q):
                    b = 2 * i + q
                    first = isinstance(i, int) and i == 0 and q == 0
                    pe.wait_ge(xT_a, b + 1)
                    pe.wait_ge(xT_v, b + 1)
                    pe.wait_ge(wgu_in[q], 32 * (i + 1))
                    if not first:
                        pe.wait_ge(hid_s, b)
                    for k in range(KD):
                        last = pe.matmul(g.ps[:, GU, :].rearrange("p (a f) -> p a f", a=2), xT[:, q, k, :],
                                         wgu[:, q, :, k, :], start=(k == 0), stop=(k == KD - 1))
                    last.then_inc(gu_done, 1)
                    if not first:
                        down(i - 1 + q, 1 - q, first=(isinstance(i, int) and i == 0 and q == 1))
                    turn_tokens(i + q, 1 - q)
                    pe.wait_ge(hid_s, b + 1)
                    if not first:
                        pe.wait_ge(hidT_s, b)
                    for j in range(KF):
                        last = pe.transpose(g.ps[:, HB, j * P:(j + 1) * P], hid[:, j::KF], g.ident)
                    last.then_inc(hid_turned, 1)
                    slots(i + 1, q)

                slots(0, 0)
                slots(0, 1)
                turn_tokens(0, 0, first=True)
                final = last_pair(pe)
                step(0, 0)
                step(0, 1)
                with pe.Fori(1, final + 1) as i:
                    step(i, 0)
                    step(i, 1)
                down(final, 1)

            @block.scalar
            def _(act):
                def tokens(i, q):
                    b = 2 * i + q
                    act.wait_ge(xT_turned, b + 1)
                    act.activation(xT[:, q, 0:KD // 2, :], g.ps[:, XB, :].rearrange("p (k c) -> p k c", c=P), ACT.Copy).then_inc(xT_a, 1)

                def y_half(i, q, wait=True):
                    b = 2 * i + q
                    act.wait_ge(y_done, b + 1)
                    if wait:
                        act.wait_ge(scattered[q], 16 * i)
                    act.activation(ysb[q][:, 0:512], g.ps[:, YB, :], ACT.Copy).then_inc(y_a, 1)

                def step(i, q):
                    b = 2 * i + q
                    peeled = isinstance(i, int)
                    act.wait_ge(gu_done, b + 1)
                    if not (peeled and q == 0):
                        act.wait_ge(hid_s, b)
                    act.activation(act_g[:], g.ps[:, GU, 0:FE], ACT.Silu).then_inc(silued, 1)
                    if not (peeled and q == 0):
                        y_half(i - 1 + q, 1 - q, wait=not peeled and q == 1 or not peeled)
                    tokens(i + q, 1 - q)
                    act.wait_ge(hid_turned, b + 1)
                    act.activation(hidT[:], g.ps[:, HB, 0:FE].rearrange("p (j c) -> p j c", c=P), ACT.Copy).then_inc(hidT_s, 1)

                tokens(0, 0)
                final = last_pair(act)
                step(0, 0)
                step(0, 1)
                act.wait_ge(gu_done, 3)
                act.wait_ge(hid_s, 2)
                act.activation(act_g[:], g.ps[:, GU, 0:FE], ACT.Silu).then_inc(silued, 1)
                y_half(0, 1, wait=False)
                tokens(1, 1)
                act.wait_ge(hid_turned, 3)
                act.activation(hidT[:], g.ps[:, HB, 0:FE].rearrange("p (j c) -> p j c", c=P), ACT.Copy).then_inc(hidT_s, 1)
                act.wait_ge(gu_done, 4)
                act.wait_ge(hid_s, 3)
                act.activation(act_g[:], g.ps[:, GU, 0:FE], ACT.Silu).then_inc(silued, 1)
                y_half(1, 0)
                tokens(2, 0)
                act.wait_ge(hid_turned, 4)
                act.activation(hidT[:], g.ps[:, HB, 0:FE].rearrange("p (j c) -> p j c", c=P), ACT.Copy).then_inc(hidT_s, 1)
                with act.Fori(2, final + 1) as i:
                    step(i, 0)
                    step(i, 1)
                y_half(final, 1)

            @block.vector
            def _(dve):
                def pick(i, q, wait=True):
                    b = 2 * i + q
                    e = owner(dve, b)
                    if wait:
                        dve.wait_ge(meta_done, b - 1)
                    for t in range(tiles):
                        last = dve.tensor_scalar(onehot[:, q, t, :], g.field("iota"), routes.slot[:, t, bass.ds(e, 1)],
                                                 g.table[:, bass.ds(b + FIELD["negbase"][0], 1)], ALU.subtract, ALU.is_equal)
                    last.then_inc(onehot_s, 1)

                def indices(i, q, wait=True):
                    b = 2 * i + q
                    dve.wait_ge(meta_done, b + 1)
                    if wait:
                        dve.wait_ge(gathered[q], 16 * i)
                    dve.tensor_copy(meta[:, bass.ds(b, 1), :].rearrange("p o c -> p (o c)"), g.ps[:, MB + q, 0:3]).then_inc(meta_v, 1)
                    dve.tensor_scalar(gidx[q][:], g.ps[:, MB + q, 0:1], FAR, None, ALU.add).then_inc(idx_s, 1)

                def tokens(i, q):
                    b = 2 * i + q
                    dve.wait_ge(xT_turned, b + 1)
                    dve.tensor_copy(xT[:, q, KD // 2:KD, :], g.ps[:, XB + 1, :].rearrange("p (k c) -> p k c", c=P)).then_inc(xT_v, 1)

                def y_half(i, q, wait=True):
                    b = 2 * i + q
                    if wait:
                        dve.wait_ge(scattered[q], 16 * i)
                    dve.tensor_scalar(sidx[q][:], meta[:, bass.ds(b, 1), 2], FAR, None, ALU.add).then_inc(sidx_s, 1)
                    dve.wait_ge(y_done, b + 1)
                    dve.tensor_copy(ysb[q][:, 512:D], g.ps[:, YB + 1, :]).then_inc(y_v, 1)

                def step(i, q, first_y=False):
                    b = 2 * i + q
                    first = isinstance(i, int) and i == 0 and q == 0
                    dve.wait_ge(silued, b + 1)
                    dve.wait_ge(meta_v, b + 1)
                    if not first:
                        dve.wait_ge(hid_turned, b)
                    dve.scalar_tensor_tensor(hid[:], act_g[:], meta[:, bass.ds(b, 1), 1], g.ps[:, GU, FE:2 * FE],
                                             ALU.mult, ALU.mult).then_inc(hid_s, 1)
                    if not first:
                        y_half(i - 1 + q, 1 - q, wait=not first_y)
                    tokens(i + q, 1 - q)
                    pick(i + 1 + q, 1 - q)
                    indices(i + 1, q)

                pick(0, 0, wait=False)
                pick(0, 1, wait=False)
                indices(0, 0, wait=False)
                indices(0, 1, wait=False)
                pick(1, 0)
                tokens(0, 0)
                final = last_pair(dve)
                step(0, 0)
                step(0, 1, first_y=True)
                step(1, 0, first_y=True)
                step(1, 1)
                with dve.Fori(2, final + 1) as i:
                    step(i, 0)
                    step(i, 1)
                y_half(final, 1)


def combine_phase(g, layer, tiles):
    nc = g.nc
    tag = f"c{layer}"
    H = D // 2
    jobs = [(t, h) for t in range(tiles) for h in range(2)]
    with ExitStack() as st:
        sb = lambda n, s, d=F32: st.enter_context(nc.sbuf_tensor(f"{tag}_{n}", s, d))
        rows = sb("rows", [P, 2, TOPK, H])
        total = sb("total", [P, 2, H])
        rows_in = [g.sem(f"{tag}_rows_in{q}") for q in range(2)]
        summed, chain_s = g.sem(f"{tag}_summed"), g.sem(f"{tag}_chain")
        src = g.y_rows[0:tiles * P * TOPK, :].rearrange("(t p k) d -> t p k d", p=P, k=TOPK)
        with nc.Block() as block:
            @block.sync
            def _(sp):
                for n, (t, h) in enumerate(jobs):
                    if n >= 2:
                        sp.wait_ge(summed, n - 1)
                    sp.dma_start(rows[:, n % 2, :, :], src[t][:, :, h * H:(h + 1) * H]).then_inc(rows_in[n % 2], 16)

            @block.vector
            def _(dve):
                chain = Chain(dve, chain_s)
                for n, (t, h) in enumerate(jobs):
                    q = n % 2
                    x = g.x[:, t, h * H:(h + 1) * H]
                    dve.wait_ge(rows_in[q], 16 * (n // 2 + 1))
                    dve.tensor_reduce(total[:, q, :], rows[:, q, :, :].rearrange("p k d -> p d k"), AX.X, ALU.add).then_inc(summed, 1)
                    dve.wait_ge(summed, n + 1)
                    chain.link(dve.tensor_tensor(total[:, q, :], total[:, q, :], g.mod(t, GATE2)[:, h * H:(h + 1) * H], ALU.mult))
                    chain.link(dve.tensor_tensor(x, x, total[:, q, :], ALU.add))


BA, BX, LAM, CW, CB = 0, 2, 4, 6, 10


def lru_in_phase(g, par, uc, gate):
    nc, ins = g.nc, g.ins
    CH = 640
    PAD = SEQ + TAPS - 1
    with ExitStack() as st:
        sb = lambda n, s, d=F32: st.enter_context(nc.sbuf_tensor(n, s, d))
        norm = Norm(g, "n3", sb, TILES, lambda t: g.mod(t, SH1), lambda t: g.mod(t, SC1))
        w = sb("lru_w_in_sb", [P, 2, KD, CH])
        ut = sb("lru_ut", [P, TILES, RNN])
        upad = sb("lru_upad", [RW, 2, 2, PAD])
        praw = sb("lru_praw", [96, 2, RW])
        w_ready = [g.sem(f"li_w_ready{q}") for q in range(2)]
        par_in, par_turned, par_s = g.sem("li_par_in"), g.sem("li_par_turned"), g.sem("li_par_s")
        done, evac, turned, padded = g.sem("li_done"), g.sem("li_evac"), g.sem("li_turned"), g.sem("li_padded")
        conv, padz, chain_s = g.sem("li_conv"), g.sem("li_padz"), g.sem("li_chain")
        jobs = [(c, t) for c in (2, 3) for t in range(TILES)] + [(c, t) for c in (0, 1) for t in range(LAT_TILES)]
        order = [2, 3, 0, 1]
        last_job = {c: max(n for n, (cc, _) in enumerate(jobs) if cc == c) for c in order}

        with nc.Block() as block:
            @block.sync
            def _(sp):
                src = ins["lru_w_in"][0].rearrange("(p k) n -> p k n", k=KD)
                for i, c in enumerate(order):
                    if i >= 2:
                        sp.wait_ge(done, last_job[order[i - 2]] + 1)
                    sp.dma_start(w[:, i % 2, :, :], src[:, :, c * CH:(c + 1) * CH]).then_inc(w_ready[i % 2], 16)

            @block.gpsimd
            def _(pool):
                for i, name in enumerate(("lru_ba", "lru_bx", "lru_lam")):
                    pool.dma_start(praw[32 * i:32 * i + 32, 0, :], ins[name][0].rearrange("d (n c) -> (d n) c", c=RW)).then_inc(par_in, 16)
                pool.dma_start(praw[0:64, 1, :], ins["lru_conv_w"][0].rearrange("j (n c) -> (j n) c", c=RW)).then_inc(par_in, 16)
                pool.dma_start(praw[64:80, 1, :], ins["lru_conv_b"][0].rearrange("(n c) -> n c", c=RW)).then_inc(par_in, 16)
                pool.memset(upad[:], 0.0).then_inc(padz, 1)

            @block.tensor
            def _(pe):
                pe.wait_ge(par_in, 80)
                pe.transpose(g.ps[0:RW, 6, 0:96], praw[:, 0, :], g.ident[0:96, 0:96])
                pe.transpose(g.ps[0:RW, 6, 96:176], praw[0:80, 1, :], g.ident[0:80, 0:80]).then_inc(par_turned, 1)
                for t in range(TILES):
                    norm.pe_turn(pe, t)

                def block_turn(n):
                    if n >= 2:
                        pe.wait_ge(padded, n - 1)
                    for t in range(TILES):
                        last = pe.transpose(g.ps[0:RW, 4 + n % 2, t * P:(t + 1) * P], ut[:, t, n * RW:(n + 1) * RW], g.ident)
                    last.then_inc(turned, 1)

                for n, (c, t) in enumerate(jobs):
                    if t == 0:
                        i = order.index(c)
                        pe.wait_ge(w_ready[i % 2], 16 * (i // 2 + 1))
                    norm.wait_hT(pe, TILES - 1 if n == 1 else t)
                    if n >= 2:
                        pe.wait_ge(evac, n - 1)
                    b = 2 if n % 2 == 0 else 0
                    for k in range(KD):
                        for j in range(2):
                            last = pe.matmul(g.ps[:, b + j, 0:CH // 2], norm.hT[:, k, t * P:(t + 1) * P],
                                             w[:, order.index(c) % 2, k, j * (CH // 2):(j + 1) * (CH // 2)],
                                             start=(k == 0), stop=(k == KD - 1))
                    last.then_inc(done, 1)
                    if 4 <= n < 8:
                        if n == 4:
                            pe.wait_ge(evac, 4)
                        for m in range(2):
                            block_turn(2 * (n - 4) + m)
                    if n >= 8:
                        if n == 8:
                            pe.wait_ge(evac, 8)
                        for m in range(2):
                            block_turn(8 + 2 * (n - 8) + m)

            @block.scalar
            def _(act):
                norm.act_stats(act)
                for t in range(TILES):
                    norm.act_evacuate(act, t)
                for n, (c, t) in enumerate(jobs):
                    act.wait_ge(done, n + 1)
                    b = 2 if n % 2 == 0 else 0
                    dst, c0, f = (ut, (c - 2) * CH, ACT.Copy) if c >= 2 else (gate, c * CH, ACT.Gelu_apprx_tanh)
                    act.activation(dst[:, t, c0:c0 + CH].rearrange("p (j c) -> p j c", j=2), g.ps[:, b:b + 2, 0:CH // 2], f).then_inc(evac, 1)

            @block.vector
            def _(dve):
                chain = Chain(dve, chain_s)
                dve.wait_ge(par_turned, 1)
                dve.tensor_copy(par[:], g.ps[0:RW, 6, 0:176]).then_inc(par_s, 1)
                dve.wait_ge(par_s, 1)
                norm.dve_rstd(dve)
                for t in range(TILES):
                    norm.dve_h(dve, t)
                    norm.dve_evacuate(dve, t)
                dve.wait_ge(padz, 1)
                col = lambda s, n: par[:, s * RB + n:s * RB + n + 1]
                for n in range(RB):
                    q = n % 2
                    dve.wait_ge(turned, n + 1)
                    dve.tensor_copy(upad[:, q, :, LEFT:LEFT + SEQ], g.ps[0:RW, 4 + q, :].rearrange("p (s c) -> p s c", s=2)).then_inc(padded, 1)
                    dve.wait_ge(padded, n + 1)
                    u = uc[:, n, :].rearrange("p (s c) -> p s c", s=2)
                    chain.link(dve.tensor_scalar(u, upad[:, q, :, 0:SEQ], col(CW, n), col(CB, n), ALU.mult, ALU.add))
                    for j in range(1, TAPS):
                        chain.link(dve.scalar_tensor_tensor(u, upad[:, q, :, j:j + SEQ], col(CW + j, n), u, ALU.mult, ALU.add))


def lru_scan_phase(g, par, uc, gate, hsum):
    nc, ins = g.nc, g.ins
    HB = RB // 2
    groups = [(d, h) for d in range(2) for h in range(2)]
    with ExitStack() as st:
        sb = lambda n, s, d=F32: st.enter_context(nc.sbuf_tensor("ls_" + n, s, d))
        sem = lambda n: g.sem("ls_" + n)
        wa = sb("wa", [RW, 2 * RB, RW])
        wx = sb("wx", [RW, 2 * RB, RW])
        z, w1, dd, lnw, m0 = (sb(n, [RW, 2 * RB]) for n in ("z", "w1", "dd", "lnw", "m0"))
        pos8, neg8 = sb("pos8", [RW, 2 * RB]), sb("neg8", [RW, 2 * RB])
        r = sb("r", [RW, HB, TOK])
        bu = sb("bu", [RW, HB, TOK])
        a = sb("a", [RW, HB, TOK])
        ig = sb("ig", [RW, 2, TOK])
        sq = sb("sq", [RW, 2, TOK])
        hc = sb("hc", [RW, 2, CTX])
        back = sb("back", [RW, 2, SEQ])
        w_in, w_done, zs, ln_s, chain_s = sem("w_in"), sem("w_done"), sem("zs"), sem("ln_s"), sem("chain")
        rates, sig, bus, exps, sqs, omts, roots, scans = (sem(n) for n in ("rates", "sig", "bus", "exps", "sqs", "omts", "roots", "scans"))
        gturned, gated, acts = sem("gturned"), sem("gated"), sem("acts")
        lam = par[:, LAM * RB:(LAM + 2) * RB]
        blocks = [(d, h, n) for d, h in groups for n in range(HB)]

        with nc.Block() as block:
            @block.sync
            def _(sp):
                for dst, name in ((wa, "lru_wa"), (wx, "lru_wx")):
                    sp.dma_start(dst[:], ins[name][0].rearrange("d n c f -> c (d n) f")).then_inc(w_in, 16)

            @block.tensor
            def _(pe):
                pe.wait_ge(w_in, 32)
                for j, (d, h, n) in enumerate(blocks):
                    ch = h * HB + n
                    if j >= 2:
                        pe.wait_ge(sig, 2 * (j - 1))
                    b = 2 * (j % 2)
                    pe.matmul(g.ps[0:RW, b, :], wa[:, d * RB + ch, :], uc[:, ch, :], start=True, stop=True)
                    pe.matmul(g.ps[0:RW, b + 1, :], wx[:, d * RB + ch, :], uc[:, ch, :], start=True, stop=True).then_inc(w_done, 1)
                for n in range(RB):
                    if n >= 2:
                        pe.wait_ge(gated, n - 1)
                    for t in range(LAT_TILES):
                        last = pe.transpose(g.ps[0:RW, 4 + n % 2, t * P:(t + 1) * P], gate[:, t, n * RW:(n + 1) * RW], g.ident)
                    last.then_inc(gturned, 1)

            @block.scalar
            def _(act):
                act.activation(z[:], lam, ACT.Abs).then_inc(acts, 1)
                act.wait_ge(acts, 1)
                act.activation(z[:], z[:], ACT.Exp, scale=-1.0).then_inc(zs, 1)
                act.wait_ge(zs, 2)
                act.activation(lnw[:], w1[:], ACT.Ln).then_inc(ln_s, 1)
                for gi, (d, h) in enumerate(groups):
                    base = gi * HB
                    for n in range(HB):
                        j = base + n
                        ch = h * HB + n
                        act.wait_ge(w_done, j + 1)
                        if gi:
                            act.wait_ge(scans, j - HB + 1)
                        act.activation(r[:, n, :], g.ps[0:RW, 2 * (j % 2), :], ACT.Sigmoid, bias=par[:, (BA + d) * RB + ch:(BA + d) * RB + ch + 1]).then_inc(sig, 1)
                        if j >= 2:
                            act.wait_ge(bus, j - 1)
                        act.activation(ig[:, j % 2, :], g.ps[0:RW, 2 * (j % 2) + 1, :], ACT.Sigmoid, bias=par[:, (BX + d) * RB + ch:(BX + d) * RB + ch + 1]).then_inc(sig, 1)
                    if gi == 0:
                        act.wait_ge(rates, 1)
                    act.wait_ge(sig, 2 * (base + HB))
                    for n in range(HB):
                        j = base + n
                        c = d * RB + h * HB + n
                        act.activation(a[:, n, :], r[:, n, :], ACT.Exp, scale=neg8[:, c:c + 1]).then_inc(exps, 1)
                        act.wait_ge(exps, 2 * j + 1)
                        act.activation(r[:, n, :], r[:, n, :], ACT.Tanh, scale=pos8[:, c:c + 1]).then_inc(exps, 1)
                    for n in range(HB):
                        j = base + n
                        act.wait_ge(omts, j + 1)
                        act.activation(r[:, n, :], r[:, n, :], ACT.Sqrt).then_inc(roots, 1)

            @block.gpsimd
            def _(pool):
                for j in range(len(blocks)):
                    n = j % HB
                    pool.wait_ge(exps, 2 * j + 1)
                    if j >= 2:
                        pool.wait_ge(omts, j - 1)
                    pool.tensor_tensor(sq[:, j % 2, :], a[:, n, :], a[:, n, :], ALU.mult).then_inc(sqs, 1)

            @block.vector
            def _(dve):
                chain = Chain(dve, chain_s)
                dve.wait_ge(zs, 1)
                dve.tensor_scalar(w1[:], z[:], 1.0, None, ALU.add).then_inc(zs, 1)
                dve.wait_ge(zs, 2)
                chain.link(dve.tensor_scalar(dd[:], w1[:], -1.0, None, ALU.add))
                chain.link(dve.tensor_scalar(m0[:], dd[:], 0.0, None, ALU.is_equal))
                chain.link(dve.tensor_tensor(dd[:], dd[:], m0[:], ALU.add))
                chain.link(dve.reciprocal(dd[:], dd[:]))
                dve.wait_ge(ln_s, 1)
                chain.link(dve.tensor_tensor(lnw[:], lnw[:], m0[:], ALU.add))
                chain.link(dve.tensor_tensor(lnw[:], lnw[:], dd[:], ALU.mult))
                chain.link(dve.tensor_tensor(lnw[:], lnw[:], z[:], ALU.mult))
                chain.link(dve.tensor_scalar(m0[:], lam, -1.0, 0.0, ALU.mult, ALU.max))
                chain.link(dve.tensor_tensor(m0[:], m0[:], lnw[:], ALU.add))
                chain.link(dve.tensor_scalar(pos8[:], m0[:], 8.0, None, ALU.mult))
                dve.tensor_scalar(neg8[:], m0[:], -8.0, None, ALU.mult).then_inc(rates, 1)
                for gi, (d, h) in enumerate(groups):
                    base = gi * HB
                    for n in range(HB):
                        j = base + n
                        dve.wait_ge(sig, 2 * j + 2)
                        dve.tensor_tensor(bu[:, n, :], ig[:, j % 2, :], uc[:, h * HB + n, :], ALU.mult).then_inc(bus, 1)
                    for n in range(HB):
                        j = base + n
                        dve.wait_ge(exps, 2 * j + 2)
                        dve.wait_ge(sqs, j + 1)
                        dve.scalar_tensor_tensor(r[:, n, :], sq[:, j % 2, :], 1.0, r[:, n, :], ALU.add, ALU.mult).then_inc(omts, 1)
                    for n in range(HB):
                        j = base + n
                        ch = h * HB + n
                        dve.wait_ge(roots, j + 1)
                        dve.wait_ge(bus, j + 1)
                        chain.link(dve.tensor_tensor(bu[:, n, :], bu[:, n, :], r[:, n, :], ALU.mult))
                        lat, ctx = slice(0, SEQ), slice(SEQ, TOK)
                        if d == 0:
                            chain.link(dve.tensor_tensor_scan(hc[:, j % 2, :], a[:, n, ctx], bu[:, n, ctx], 0.0, ALU.mult, ALU.add))
                            chain.done(dve.tensor_tensor_scan(hsum[:, ch, :], a[:, n, lat], bu[:, n, lat], hc[:, j % 2, CTX - 1:CTX], ALU.mult, ALU.add))
                            dve.wait_ge(chain_s, chain.n)
                        else:
                            rev = lambda x: x[:, ::-1]
                            chain.link(dve.tensor_tensor_scan(rev(hc[:, j % 2, :]), rev(a[:, n, ctx]), rev(bu[:, n, ctx]), 0.0, ALU.mult, ALU.add))
                            chain.link(dve.tensor_tensor_scan(rev(back[:, j % 2, :]), rev(a[:, n, lat]), rev(bu[:, n, lat]), hc[:, j % 2, 0:1], ALU.mult, ALU.add))
                            chain.link(dve.tensor_tensor(hsum[:, ch, :], hsum[:, ch, :], back[:, j % 2, :], ALU.add))
                        dve.sem_inc(scans, 1)
                for n in range(RB):
                    dve.wait_ge(gturned, n + 1)
                    dve.tensor_tensor(hsum[:, n, :], hsum[:, n, :], g.ps[0:RW, 4 + n % 2, 0:SEQ], ALU.mult).then_inc(gated, 1)


def load_mod_phase(g, layer, dsts):
    nc = g.nc
    mod_in = g.sem(f"mod_in{layer}")
    with nc.Block() as block:
        @block.sync
        def _(sp):
            for dst, stream, n in dsts:
                sp.dma_start(dst, g.mod_rows[layer, stream, 0:n * D].partition_broadcast(P).rearrange("p (m d) -> p m d", d=D)).then_inc(mod_in, 16)
            sp.wait_ge(mod_in, 16 * len(dsts))

        if layer == 0:
            @block.vector
            def _(dve):
                dve.tensor_copy(g.ident_bf[:], g.ident)
                dve.tensor_copy(g.mask_bf[:], g.field("mask"))
                dve.tensor_copy(g.before_bf[:], g.field("before"))
                dve.memset(g.ones_bf[:], 1.0)
                dve.memset(g.ones[:], 1.0)
                dve.memset(g.eps[:], EPS)


def final_phase(g):
    nc = g.nc
    with ExitStack() as st:
        sb = lambda n, s, d=F32: st.enter_context(nc.sbuf_tensor("f_" + n, s, d))
        gain = sb("gain", [P, D])
        y = sb("y", [P, LAT_TILES, D])
        sumsq, root, junk = sb("sumsq", [P, LAT_TILES]), sb("root", [P, LAT_TILES]), sb("junk", [P, D])
        gain_in, squares, rooted, recip, ready, stored = (g.sem("f_" + n) for n in ("gain_in", "squares", "rooted", "recip", "ready", "stored"))
        with nc.Block() as block:
            @block.sync
            def _(sp):
                sp.dma_start(gain[:], g.ins["final_g"].partition_broadcast(P)).then_inc(gain_in, 16)
                for t in range(LAT_TILES):
                    sp.wait_ge(ready, t + 1)
                    sp.dma_start(g.out[0, t * P:(t + 1) * P, :], y[:, t, :]).then_inc(stored, 16)
                sp.wait_ge(stored, 16 * LAT_TILES)

            @block.scalar
            def _(act):
                for t in range(LAT_TILES):
                    act.activation(junk[:], g.x[:, t, :], ACT.Square, accum_out=sumsq[:, t:t + 1]).then_inc(squares, 1)
                    act.wait_ge(squares, t + 1)
                act.activation(root[:], sumsq[:], ACT.Sqrt, bias=g.eps[:, 0:1], scale=1.0 / D).then_inc(rooted, 1)

            @block.vector
            def _(dve):
                dve.wait_ge(rooted, 1)
                dve.reciprocal(root[:], root[:]).then_inc(recip, 1)
                dve.wait_ge(recip, 1)
                dve.wait_ge(gain_in, 16)
                for t in range(LAT_TILES):
                    dve.scalar_tensor_tensor(y[:, t, :], g.x[:, t, :], root[:, t:t + 1], gain[:], ALU.mult, ALU.mult).then_inc(ready, 1)


def backbone(nc, ins, table, out):
    with ExitStack() as stack:
        g = Core(nc, stack, ins, table, out)
        sb = lambda n, s, d=F32: stack.enter_context(nc.sbuf_tensor(n, s, d))
        g.table = sb("table", [P, TABLE_W])
        g.x = sb("x_stream", [P, TILES, D])
        g.ident_bf, g.before_bf, g.ones_bf = (sb(n, [P, P], BF16) for n in ("ident_bf", "before_bf", "ones_bf"))
        g.mask_bf = sb("mask_bf", [P, LAT_TILES * SEQ], BF16)
        g.ones = sb("ones", [P, P])
        g.eps = sb("eps", [P, 1])
        g.ps = stack.enter_context(nc.psum_tensor("ps", [P, 8, 512], F32))
        g.ident = g.field("ident")
        ada_phase(g)

        with ExitStack() as layer:
            sb = lambda n, s, d=F32: layer.enter_context(nc.sbuf_tensor(n, s, d))
            mods = sb("mods0", [P, 2, NMOD, D])
            g.mod = lambda t, m: mods[:, t // LAT_TILES, m, :]
            load_mod_phase(g, 0, [(mods[:, s, :, :], s, NMOD) for s in range(2)])
            with ExitStack() as att:
                sb = lambda n, s, d=F32: att.enter_context(nc.sbuf_tensor(n, s, d))
                qT = sb("qT", [P, HEADS // 2, TOK])
                kT = sb("kT", [P, KV // 2, TOK])
                v = sb("v", [P, TILES, KVD])
                qkv_phase(g, qT, kT, v)
                o = sb("o", [P, TILES, QD])
                attention_phase(g, qT, kT, v, o)
                project_phase(g, "ao", ins["attn_w_o"][0].rearrange("(p k) n -> p k n", k=KD), P, KD, TILES, src=o)
            with ExitStack() as moe:
                routes = Routes(lambda n, s, d=F32: moe.enter_context(nc.sbuf_tensor(n, s, d)), 0, TILES)
                route_phase(g, 0, TILES, routes)
                expert_phase(g, 0, TILES, routes)
            combine_phase(g, 0, TILES)
        g.recycle_semaphores()

        with ExitStack() as layer:
            sb = lambda n, s, d=F32: layer.enter_context(nc.sbuf_tensor(n, s, d))
            mod_lat = sb("mod1_lat", [P, NMOD, D])
            mod_ctx = sb("mod1_ctx", [P, 2, D])
            g.mod = lambda t, m: (mod_lat if t < LAT_TILES else mod_ctx)[:, m, :]
            load_mod_phase(g, 1, [(mod_lat[:], 0, NMOD), (mod_ctx[:], 1, 2)])
            with ExitStack() as lru:
                sb = lambda n, s, d=F32: lru.enter_context(nc.sbuf_tensor(n, s, d))
                hsum = sb("hsum", [RW, RB, SEQ])
                with ExitStack() as inner:
                    sb = lambda n, s, d=F32: inner.enter_context(nc.sbuf_tensor(n, s, d))
                    par = sb("par", [RW, 11 * RB])
                    uc = sb("uc", [RW, RB, TOK])
                    gate = sb("gate", [P, LAT_TILES, RNN])
                    lru_in_phase(g, par, uc, gate)
                    lru_scan_phase(g, par, uc, gate, hsum)
                project_phase(g, "lo", ins["lru_w_out"][0].rearrange("(n c) d -> c n d", c=RW), RW, RB, LAT_TILES, srcT=hsum)
            with ExitStack() as moe:
                routes = Routes(lambda n, s, d=F32: moe.enter_context(nc.sbuf_tensor(n, s, d)), 1, LAT_TILES)
                route_phase(g, 1, LAT_TILES, routes)
                expert_phase(g, 1, LAT_TILES, routes)
            combine_phase(g, 1, LAT_TILES)
        final_phase(g)


_INS = ["x", "c", "ctx", "c_ctx", "ada_w", "ada_b", "norm1_g", "norm2_g", "attn_w_qkv", "attn_w_o", "attn_sink",
        "lru_w_in", "lru_conv_w", "lru_conv_b", "lru_wa", "lru_ba", "lru_wx", "lru_bx", "lru_lam", "lru_w_out",
        "moe_router_w", "moe_router_bias", "moe_w_gate", "moe_w_up", "moe_w_down",
        "shared_w_gate", "shared_w_up", "shared_w_down", "final_g"]


def shape_table():
    import numpy as np

    f = np.float32
    tab = np.zeros((P, TABLE_W), f)

    def put(name, a):
        lo, hi = FIELD[name]
        a = np.asarray(a, f)
        tab[0:a.shape[0], lo:hi] = a

    r = np.arange(P)
    e = np.arange(EXPERTS)
    put("ident", np.eye(P))
    put("before", r[:, None] < r[None, :])
    put("iota", np.tile(r, (P, 1)))
    q, k = np.arange(SEQ), np.arange(SEQ)
    mask = np.where(np.abs(q[:, None] - k[None, :]) <= WINDOW, 0.0, NEG)
    put("mask", mask.reshape(LAT_TILES, P, SEQ).transpose(1, 0, 2).reshape(P, -1))
    put("before_e", np.concatenate([e[:, None] < e[None, :], np.ones((EXPERTS, 1), bool)], 1))
    put("upto_e", e[:, None] <= e[None, :])
    gg = np.arange(GROUPS)
    put("lower_g", np.tile((gg[None, :] < gg[:, None]).reshape(1, -1), (P, 1)))
    put("tok", r[:, None] + P * np.arange(TILES)[None, :])
    put("negbase", np.tile(-P * np.arange(NBMAX), (P, 1)))
    put("iota_b", np.tile(np.arange(NBMAX), (P, 1)))
    nf = HD // 4
    inv = np.exp(f(-math.log(ROPE_THETA)) * np.arange(nf, dtype=f) / f(nf)).astype(f)
    tok = np.arange(SEQ)
    row = (tok // GRID_W).astype(f)[:, None] * inv
    col = (tok % GRID_W).astype(f)[:, None] * inv
    cos = np.concatenate([np.cos(row), np.cos(row), np.cos(col), np.cos(col)], 1)
    sin = np.concatenate([-np.sin(row), np.sin(row), -np.sin(col), np.sin(col)], 1)
    tiled = lambda a: a.reshape(LAT_TILES, P, HD).transpose(1, 0, 2).reshape(P, -1)
    put("rope_c", tiled(cos))
    put("rope_s", tiled(sin))
    return tab


def kernel(**inputs):
    import numpy as _np
    import concourse.bacc as _bacc
    from concourse import mybir as _mybir
    from concourse.bass_utils import run_bass_kernel_spmd as _run

    nc = _bacc.Bacc("TRN2", target_bir_lowering=False, num_devices=1)
    arrays, ins = {}, {}
    for name in _INS:
        a = _np.ascontiguousarray(inputs[name])
        arrays[f"in_{name}"] = a
        ins[name] = nc.dram_tensor(f"in_{name}", a.shape, _mybir.dt.from_np(a.dtype), kind="ExternalInput").ap()
    arrays["in_table"] = shape_table()
    table = nc.dram_tensor("in_table", arrays["in_table"].shape, F32, kind="ExternalInput").ap()
    out = nc.dram_tensor("out_0", (1, SEQ, D), F32, kind="ExternalOutput").ap()
    backbone(nc, ins, table, out)
    r = _run(nc, [arrays], core_ids=[0])
    return r.results[0]["out_0"]
```

```python
import math

import concourse.bass as bass
from concourse import mybir
from contextlib import ExitStack

F32 = mybir.dt.float32
BF16 = mybir.dt.bfloat16
I32 = mybir.dt.int32
U32 = mybir.dt.uint32
ALU = mybir.AluOpType
ACT = mybir.ActivationFunctionType
AX = mybir.AxisListType

P = 128
D = 1024
KD = D // P
SEQ = 256
CTX = 256
TOK = SEQ + CTX
LAT_TILES = SEQ // P
TILES = TOK // P
NMOD = 6
SH1, SC1, GATE1, SH2, SC2, GATE2 = range(NMOD)
EPS = 1e-6
GRID_W = 64
ROPE_THETA = 10000.0

HEADS = 16
KV = 4
GROUP = HEADS // KV
HD = 64
QD = HEADS * HD
KVD = KV * HD
QKV = QD + 2 * KVD
WINDOW = 128
SCALE = HD ** -0.5
NEG = -1e30

RNN = 1280
RB = 16
RW = RNN // RB
RP = 96
TAPS = 4
LEFT = 2

EXPERTS = 64
TOPK = 8
GROUPS = 8
PER_GROUP = EXPERTS // GROUPS
TOP_GROUPS = 4
FE = 256
KF = FE // P
ROUTED_SCALE = 2.5
FAR = 8192.0


def slots_of(tiles):
    return tiles * P // 4


def max_blocks(tiles):
    extra = (tiles * P * TOPK - EXPERTS) // slots_of(tiles)
    return (EXPERTS + extra + 1) // 2 * 2


NBMAX = max_blocks(TILES) + 8

_FIELDS = [("ident", P), ("before", P), ("iota", P), ("mask", LAT_TILES * SEQ), ("before_e", EXPERTS + 1),
           ("upto_e", EXPERTS), ("lower_g", GROUPS * GROUPS), ("tok", TILES), ("negbase0", NBMAX), ("negbase1", NBMAX),
           ("iota_b", NBMAX), ("rope_c", LAT_TILES * HD), ("rope_s", LAT_TILES * HD)]
FIELD = {}
_at = 0
for _name, _width in _FIELDS:
    FIELD[_name] = (_at, _at + _width)
    _at += _width
TABLE_W = _at


class Chain:

    def __init__(self, eng, sem):
        self.eng, self.sem, self.n = eng, sem, 0

    def done(self, ins):
        self.n += 1
        ins.then_inc(self.sem, 1)
        return self.n

    def link(self, ins):
        self.eng.wait_ge(self.sem, self.done(ins))


class Core:

    def __init__(self, nc, stack, ins, table, out):
        self.nc, self.stack, self.ins, self.out = nc, stack, ins, out
        self.table_dram = table
        self.mod_rows = nc.dram_tensor("mod_rows", (2, 2, NMOD * D), F32, kind="Internal").ap()
        self.h2_rows = nc.dram_tensor("h2_rows", (TOK, D), F32, kind="Internal").ap()
        self.y_rows = nc.dram_tensor("y_rows", (TOK * TOPK, D), F32, kind="Internal").ap()

        self.sems = []

    def sem(self, name):
        self.sems.append(self.nc.alloc_semaphore(name=name))
        return self.sems[-1]

    def recycle_semaphores(self):
        self.nc.clear_and_free_semaphores(self.sems)
        self.nc.all_engine_barrier()
        self.sems = []

    def field(self, name, rows=P):
        a, b = FIELD[name]
        return self.table[0:rows, a:b]


def ada_phase(g):
    nc, ins = g.nc, g.ins
    HALF = NMOD * D // 2
    BUFS = 5
    NB = HALF // 512
    with ExitStack() as st:
        sb = lambda n, s, d=F32: st.enter_context(nc.sbuf_tensor(n, s, d))
        wbuf = sb("ada_wbuf", [P, BUFS, HALF])
        craw = sb("ada_craw", [P, 2, KD])
        cs = sb("ada_cs", [P, KD, 2])
        row = sb("ada_row", [2, 2, NMOD * D])
        bias = sb("ada_bias", [2, 2, NMOD * D])
        gains = sb("ada_gains", [2, 2, 2, D])
        w_ready = [g.sem(f"ada_w_ready{i}") for i in range(BUFS)]
        c_ready, c_silu, used = g.sem("ada_c_ready"), g.sem("ada_c_silu"), g.sem("ada_used")
        evac, row_ready, small = g.sem("ada_evac"), g.sem("ada_row_ready"), g.sem("ada_small")
        stored, chain_s, x_in = g.sem("ada_stored"), g.sem("ada_chain"), g.sem("x_in")
        tiles = [(l, h, k) for l in range(2) for h in range(2) for k in range(KD)]

        with nc.Block() as block:
            @block.sync
            def _(sp):
                sp.dma_start(craw[:, 0, :], ins["c"].rearrange("o (p k) -> p (o k)", k=KD)).then_inc(c_ready, 16)
                sp.dma_start(craw[:, 1, :], ins["c_ctx"].rearrange("(p k) -> p k", k=KD)).then_inc(c_ready, 16)
                for n, (l, h, k) in enumerate(tiles):
                    if n >= BUFS:
                        sp.wait_ge(used, n - BUFS + 1)
                    src = ins["ada_w"][l].rearrange("(p k) n -> p k n", k=KD)[:, k, h * HALF:(h + 1) * HALF]
                    sp.dma_start(wbuf[:, n % BUFS, :], src).then_inc(w_ready[n % BUFS], 16)

            @block.gpsimd
            def _(pool):
                pool.dma_start(g.table[:], g.table_dram).then_inc(x_in, 16)
                for l in range(2):
                    pool.dma_start(bias[:, l, :], ins["ada_b"][l].partition_broadcast(2)).then_inc(small, 16)
                    pool.dma_start(gains[:, l, 0, :], ins["norm1_g"][l].partition_broadcast(2)).then_inc(small, 16)
                    pool.dma_start(gains[:, l, 1, :], ins["norm2_g"][l].partition_broadcast(2)).then_inc(small, 16)
                pool.dma_start(g.x[:, 0:LAT_TILES, :], ins["x"][0].rearrange("(t p) d -> p t d", p=P)).then_inc(x_in, 16)
                pool.dma_start(g.x[:, LAT_TILES:TILES, :], ins["ctx"][0].rearrange("(t p) d -> p t d", p=P)).then_inc(x_in, 16)
                pool.wait_ge(x_in, 48)

            @block.scalar
            def _(act):
                act.wait_ge(c_ready, 32)
                for s in range(2):
                    act.activation(cs[:, :, s], craw[:, s, :], ACT.Silu).then_inc(c_silu, 1)
                for l in range(2):
                    act.wait_ge(row_ready, l + 1)
                    act.dma_start(g.mod_rows[l], row[:, l, :]).then_inc(stored, 16)
                act.wait_ge(stored, 32)

            @block.tensor
            def _(pe):
                pe.wait_ge(c_silu, 2)
                for n, (l, h, k) in enumerate(tiles):
                    pe.wait_ge(w_ready[n % BUFS], 16 * (n // BUFS + 1))
                    if k == 0 and n:
                        pe.wait_ge(evac, n // KD)
                    for j in range(NB):
                        last = pe.matmul(g.ps[0:2, j, :], cs[:, k, :], wbuf[:, n % BUFS, j * 512:(j + 1) * 512],
                                         start=(k == 0), stop=(k == KD - 1))
                    last.then_inc(used, 1)

            @block.vector
            def _(dve):
                chain = Chain(dve, chain_s)
                dve.wait_ge(small, 96)
                for l in range(2):
                    for h in range(2):
                        dve.wait_ge(used, KD * (2 * l + h + 1))
                        part = slice(h * HALF, (h + 1) * HALF)
                        dve.tensor_tensor(row[:, l, part], g.ps[0:2, 0:NB, :].rearrange("p a b -> p (a b)"),
                                          bias[:, l, part], ALU.add).then_inc(evac, 1)
                    dve.wait_ge(evac, 2 * l + 2)
                    for i, sc in enumerate((SC1, SC2)):
                        r = row[:, l, sc * D:(sc + 1) * D]
                        chain.link(dve.scalar_tensor_tensor(r, r, 1.0, gains[:, l, i, :], ALU.add, ALU.mult))
                    dve.sem_inc(row_ready, 1)


class Norm:

    def __init__(self, g, tag, sb, tiles, shift, gain):
        self.g, self.tiles, self.shift, self.gain = g, tiles, shift, gain
        self.h = sb(tag + "_h", [P, 2, D])
        self.hT = sb(tag + "_hT", [P, KD, tiles * P])
        self.sumsq = sb(tag + "_sumsq", [P, tiles])
        self.root = sb(tag + "_root", [P, tiles])
        self.rstd = sb(tag + "_rstd", [P, tiles])
        self.junk = sb(tag + "_sq", [P, D], BF16)
        self.squares, self.roots, self.h_ready = g.sem(tag + "_squares"), g.sem(tag + "_roots"), g.sem(tag + "_h_ready")
        self.turned, self.hT_act, self.hT_dve = g.sem(tag + "_turned"), g.sem(tag + "_hT_act"), g.sem(tag + "_hT_dve")
        self.scaled = g.sem(tag + "_scaled")

    def act_stats(self, act):
        for t in range(self.tiles):
            act.activation(self.junk[:], self.g.x[:, t, :], ACT.Square, accum_out=self.sumsq[:, t:t + 1]).then_inc(self.squares, 1)
            act.wait_ge(self.squares, t + 1)
        act.activation(self.root[:], self.sumsq[:], ACT.Sqrt, bias=self.g.eps[:, 0:1], scale=1.0 / D).then_inc(self.roots, 1)

    def act_evacuate(self, act, t):
        act.wait_ge(self.turned, t + 1)
        act.activation(self.hT[:, 0:KD // 2, t * P:(t + 1) * P],
                       self.g.ps[:, 0, :].rearrange("p (k c) -> p k c", c=P), ACT.Copy).then_inc(self.hT_act, 1)

    def dve_rstd(self, dve):
        dve.wait_ge(self.roots, 1)
        dve.reciprocal(self.rstd[:], self.root[:]).then_inc(self.scaled, 1)
        dve.wait_ge(self.scaled, 1)

    def dve_h(self, dve, t, stored=None):
        if t >= 2:
            dve.wait_ge(self.turned, t - 1)
            if stored is not None:
                dve.wait_ge(stored[t % 2], 16 * (t // 2))
        h = self.h[:, t % 2, :]
        dve.scalar_tensor_tensor(h, self.g.x[:, t, :], self.rstd[:, t:t + 1], self.gain(t), ALU.mult, ALU.mult).then_inc(self.scaled, 1)
        dve.wait_ge(self.scaled, t + 2)
        dve.tensor_tensor(h, h, self.shift(t), ALU.add).then_inc(self.h_ready, 1)

    def dve_evacuate(self, dve, t):
        dve.wait_ge(self.turned, t + 1)
        dve.tensor_copy(self.hT[:, KD // 2:KD, t * P:(t + 1) * P],
                        self.g.ps[:, 1, :].rearrange("p (k c) -> p k c", c=P)).then_inc(self.hT_dve, 1)

    def pe_turn(self, pe, t):
        pe.wait_ge(self.h_ready, t + 1)
        if t:
            pe.wait_ge(self.hT_act, t)
            pe.wait_ge(self.hT_dve, t)
        for k in range(KD):
            last = pe.transpose(self.g.ps[:, k // 4, (k % 4) * P:(k % 4 + 1) * P], self.h[:, t % 2, k::KD], self.g.ident)
        last.then_inc(self.turned, 1)

    def wait_hT(self, eng, t):
        eng.wait_ge(self.hT_act, t + 1)
        eng.wait_ge(self.hT_dve, t + 1)




def qkv_phase(g, qT, kT, v):
    nc, ins = g.nc, g.ins
    PAIRS = HEADS // 2
    with ExitStack() as st:
        sb = lambda n, s, d=F32: st.enter_context(nc.sbuf_tensor(n, s, d))
        w = sb("w_qkv", [P, KD, QKV])
        norm = Norm(g, "n1", sb, TILES, lambda t: g.mod(t, SH1), lambda t: g.mod(t, SC1))
        qk = sb("qk", [P, TILES, QD + KVD])
        rot = sb("rot", [P, QD + KVD])
        w_ready, projected, qk_ready = g.sem("qkv_w_ready"), g.sem("qkv_projected"), g.sem("qk_ready")
        qk_evac, v_evac, chain_s = g.sem("qkv_qk_evac"), g.sem("qkv_v_evac"), g.sem("qkv_chain")
        turned, turned_a, turned_v = g.sem("qk_turned"), g.sem("qk_turned_act"), g.sem("qk_turned_dve")
        kz = g.sem("k_zeroed")
        spans = [(0, 512), (512, QD), (QD, QD + KVD), (QD + KVD, QKV)]
        chunks = [("q", m) for m in range(PAIRS)] + [("k", m) for m in range(KV // 2)]

        with nc.Block() as block:
            @block.sync
            def _(sp):
                sp.dma_start(w[:], ins["attn_w_qkv"][0].rearrange("(p k) n -> p k n", k=KD)).then_inc(w_ready, 16)

            def evacuate(copy, m, done):
                kind, i = chunks[m]
                ps = g.ps[:, 6 + m % 2, :]
                if kind == "q":
                    copy(qT[:, i, :], ps).then_inc(done, 1)
                else:
                    copy(kT[0:HD, i, 0, :], ps[0:HD, :]).then_inc(done, 1)
                    copy(kT[HD:P, i, 1, :], ps[HD:P, :]).then_inc(done, 1)

            @block.scalar
            def _(act):
                norm.act_stats(act)
                for t in range(TILES):
                    norm.act_evacuate(act, t)
                for t in range(TILES):
                    act.wait_ge(projected, t + 1)
                    act.activation(v[:, t, :], g.ps[:, 5, 0:KVD], ACT.Copy).then_inc(v_evac, 1)
                act.wait_ge(kz, 1)
                for m in range(1, len(chunks), 2):
                    act.wait_ge(turned, m + 1)
                    evacuate(lambda o, i: act.activation(o, i, ACT.Copy), m, turned_a)

            @block.vector
            def _(dve):
                chain = Chain(dve, chain_s)
                norm.dve_rstd(dve)
                for t in range(TILES):
                    norm.dve_h(dve, t)
                    norm.dve_evacuate(dve, t)
                for t in range(TILES):
                    dve.wait_ge(projected, t + 1)
                    flat = g.ps[:, 2:5, :].rearrange("p a b -> p (a b)")[:, 0:QD + KVD]
                    if t >= LAT_TILES:
                        dve.tensor_copy(qk[:, t, :], flat).then_inc(qk_evac, 1)
                        continue
                    heads = lambda a: a.rearrange("p (h d) -> p h d", d=HD)
                    halves = lambda a: a.rearrange("p (h x s f) -> p h x s f", x=2, s=2, f=HD // 4)
                    c0 = FIELD["rope_c"][0] + t * HD
                    s0 = FIELD["rope_s"][0] + t * HD
                    nh = HEADS + KV
                    cos = g.table[:, c0:c0 + HD][:, None, :].to_broadcast([P, nh, HD])
                    sin = g.table[:, s0:s0 + HD].rearrange("p (x s f) -> p x s f", x=2, s=2)
                    dve.tensor_tensor(heads(qk[:, t, :]), heads(flat), cos, ALU.mult).then_inc(chain_s, 1)
                    for s in range(2):
                        dve.tensor_tensor(halves(rot[:])[:, :, :, s, :], halves(flat)[:, :, :, 1 - s, :],
                                          sin[:, None, :, s, :].to_broadcast([P, nh, 2, HD // 4]), ALU.mult).then_inc(chain_s, 1)
                    dve.wait_ge(chain_s, 3 * (t + 1))
                    dve.tensor_tensor(qk[:, t, :], qk[:, t, :], rot[:], ALU.add).then_inc(qk_evac, 1)
                    dve.wait_ge(qk_evac, t + 1)
                dve.wait_ge(kz, 1)
                for m in range(0, len(chunks), 2):
                    dve.wait_ge(turned, m + 1)
                    evacuate(dve.tensor_copy, m, turned_v)

            @block.gpsimd
            def _(pool):
                pool.memset(kT[:], 0.0).then_inc(kz, 1)

            @block.tensor
            def _(pe):
                for t in range(TILES):
                    norm.pe_turn(pe, t)
                pe.wait_ge(w_ready, 16)
                for t in range(TILES):
                    norm.wait_hT(pe, t)
                    if t:
                        pe.wait_ge(qk_evac, t)
                        pe.wait_ge(v_evac, t)
                    for k in range(KD):
                        for j, (c0, c1) in enumerate(spans):
                            cols = w[:, k, c0:c1]
                            if j < 2:
                                cols = cols.rearrange("p (s g d) -> p g s d", s=2, g=GROUP)
                            last = pe.matmul(g.ps[:, 2 + j, 0:c1 - c0], norm.hT[:, k, t * P:(t + 1) * P], cols,
                                             start=(k == 0), stop=(k == KD - 1))
                    last.then_inc(projected, 1)
                pe.wait_ge(qk_evac, TILES)
                for m, (kind, i) in enumerate(chunks):
                    if m >= 2:
                        pe.wait_ge(turned_a if m % 2 else turned_v, m // 2)
                    for t in range(TILES):
                        src = qk[:, t, (QD if kind == "k" else 0) + i * P:(QD if kind == "k" else 0) + (i + 1) * P]
                        last = pe.transpose(g.ps[:, 6 + m % 2, t * P:(t + 1) * P], src, g.ident)
                    last.then_inc(turned, 1)


def attention_phase(g, qT, kT, v, o):
    nc, ins = g.nc, g.ins
    units = [(t, m, s) for t in range(TILES) for m in range(HEADS // 2) for s in range(2)]
    head = lambda m, s: (2 * (m // GROUP) + s) * GROUP + m % GROUP
    first_key = lambda t: 0 if t < LAT_TILES else SEQ
    S_BANKS, AHEAD, LAG = 4, 3, 2
    T_BANK, O_BANK = 4, 6
    with ExitStack() as st:
        sb = lambda n, s, d=F32: st.enter_context(nc.sbuf_tensor(n, s, d))
        prob = sb("prob", [P, S_BANKS, TOK])
        probT = sb("probT", [P, 2, TOK])
        sink = sb("sink", [P, HEADS])
        negsink = sb("negsink", [P, HEADS])
        top = sb("top", [P, len(units)])
        nbias = sb("nbias", [P, TILES, HEADS])
        rowsum = sb("rowsum", [P, TILES, HEADS])
        sinkexp = sb("sinkexp", [P, TILES, HEADS])
        sink_in, scored, biased, exped = g.sem("sink_in"), g.sem("scored"), g.sem("biased"), g.sem("exped")
        turned, evac_a, evac_v, mixed = g.sem("prob_turned"), g.sem("probT_act"), g.sem("probT_dve"), g.sem("mixed")
        chain_s, o_evac, sink_arg, sink_exp = g.sem("att_chain"), g.sem("o_evac"), g.sem("sink_arg"), g.sem("sink_exp")
        HALF = HEADS // 2

        with nc.Block() as block:
            @block.sync
            def _(sp):
                sp.dma_start(sink[:], ins["attn_sink"][0].partition_broadcast(P)).then_inc(sink_in, 16)

            @block.tensor
            def _(pe):
                def scores(u):
                    t, m, s = units[u]
                    if u >= S_BANKS:
                        pe.wait_ge(exped, u - S_BANKS + 1)
                    ps = g.ps[:, u % S_BANKS, :]
                    query, jp = qT[:, m, t * P:(t + 1) * P], m // GROUP
                    if t < LAT_TILES:
                        pe.matmul(ps[:, 0:SEQ], query, kT[:, jp, s, 0:SEQ], start=True, stop=False)
                        pe.matmul(ps[:, 0:SEQ], g.ident_bf[:], g.mask_bf[:, t * SEQ:(t + 1) * SEQ], start=False, stop=True)
                    pe.matmul(ps[:, SEQ:TOK], query, kT[:, jp, s, SEQ:TOK], start=True, stop=True).then_inc(scored, 1)

                def turn(u):
                    t, m, s = units[u]
                    pe.wait_ge(exped, u + 1)
                    if u >= 2:
                        pe.wait_ge(evac_a if u % 2 else evac_v, u // 2)
                    for j in range(first_key(t) // P, TILES):
                        last = pe.transpose(g.ps[:, T_BANK + u % 2, j * P:(j + 1) * P], prob[:, u % S_BANKS, j * P:(j + 1) * P], g.ident)
                    last.then_inc(turned, 1)

                def mix(u):
                    t, m, s = units[u]
                    hd = head(m, s)
                    kvh = hd // GROUP
                    pe.wait_ge(evac_a if u % 2 else evac_v, u // 2 + 1)
                    if t and u % HALF == 0:
                        pe.wait_ge(o_evac, u // HALF - 1)
                    j0 = first_key(t) // P
                    for j in range(j0, TILES):
                        last = pe.matmul(g.ps[:, O_BANK + hd // HALF, (hd % HALF) * HD:(hd % HALF + 1) * HD],
                                         probT[:, u % 2, j * P:(j + 1) * P], v[:, j, kvh * HD:(kvh + 1) * HD],
                                         start=(j == j0), stop=(j == TILES - 1))
                    last.then_inc(mixed, 1)

                for u in range(AHEAD):
                    scores(u)
                for u in range(len(units)):
                    if u + AHEAD < len(units):
                        scores(u + AHEAD)
                    turn(u)
                    if u:
                        mix(u - 1)
                mix(len(units) - 1)

            @block.vector
            def _(dve):
                chain = Chain(dve, chain_s)
                dve.wait_ge(sink_in, 16)
                chain.link(dve.tensor_scalar(negsink[:], sink[:], -1.0, None, ALU.mult))

                def finish(n):
                    t, hs = n // 2, slice(n % 2 * HALF, (n % 2 + 1) * HALF)
                    dve.wait_ge(biased, HALF * (n + 1))
                    dve.tensor_tensor(sinkexp[:, t, hs], nbias[:, t, hs], sink[:, hs], ALU.add).then_inc(sink_arg, 1)
                    dve.wait_ge(sink_exp, n + 1)
                    dve.wait_ge(exped, HALF * (n + 1))
                    chain.link(dve.tensor_tensor(rowsum[:, t, hs], rowsum[:, t, hs], sinkexp[:, t, hs], ALU.add))
                    chain.link(dve.reciprocal(rowsum[:, t, hs], rowsum[:, t, hs]))
                    dve.wait_ge(mixed, HALF * (n + 1))
                    dve.tensor_tensor(o[:, t, n % 2 * 512:(n % 2 + 1) * 512].rearrange("p (h d) -> p h d", d=HD),
                                      g.ps[:, O_BANK + n % 2, :].rearrange("p (h d) -> p h d", d=HD),
                                      rowsum[:, t, hs, None].to_broadcast([P, HALF, HD]), ALU.mult).then_inc(o_evac, 1)

                def copy(w):
                    dve.wait_ge(turned, w + 1)
                    if w >= 2:
                        dve.wait_ge(mixed, w - 1)
                    k0 = first_key(units[w][0])
                    dve.tensor_copy(probT[:, w % 2, k0:TOK], g.ps[:, T_BANK + w % 2, k0:TOK]).then_inc(evac_v, 1)

                for u in range(len(units) + AHEAD):
                    if u < len(units):
                        t, m, s = units[u]
                        hd = head(m, s)
                        dve.wait_ge(scored, u + 1)
                        chain.link(dve.reduce_max(top[:, u:u + 1], g.ps[:, u % S_BANKS, first_key(t):TOK], AX.X))
                        dve.tensor_scalar(nbias[:, t, hd:hd + 1], top[:, u:u + 1], -SCALE, negsink[:, hd:hd + 1],
                                          ALU.mult, ALU.min).then_inc(biased, 1)
                    if u >= LAG and (u - LAG) % 2 == 0 and u - LAG < len(units):
                        copy(u - LAG)
                    if u % HALF == 4 and u >= HALF and u < len(units):
                        finish(u // HALF - 1)
                finish(len(units) // HALF - 1)

            @block.scalar
            def _(act):
                def copy(w):
                    act.wait_ge(turned, w + 1)
                    if w >= 2:
                        act.wait_ge(mixed, w - 1)
                    k0 = first_key(units[w][0])
                    act.activation(probT[:, w % 2, k0:TOK], g.ps[:, T_BANK + w % 2, k0:TOK], ACT.Copy).then_inc(evac_a, 1)

                def sink_terms(n):
                    t, hs = n // 2, slice(n % 2 * HALF, (n % 2 + 1) * HALF)
                    act.wait_ge(sink_arg, n + 1)
                    act.activation(sinkexp[:, t, hs], sinkexp[:, t, hs], ACT.Exp).then_inc(sink_exp, 1)

                for u in range(len(units) + AHEAD):
                    if u < len(units):
                        t, m, s = units[u]
                        hd = head(m, s)
                        k0 = first_key(t)
                        act.wait_ge(biased, u + 1)
                        if u >= S_BANKS:
                            act.wait_ge(turned, u - S_BANKS + 1)
                        act.activation(prob[:, u % S_BANKS, k0:TOK], g.ps[:, u % S_BANKS, k0:TOK], ACT.Exp,
                                       bias=nbias[:, t, hd:hd + 1], scale=SCALE, accum_out=rowsum[:, t, hd:hd + 1]).then_inc(exped, 1)
                    if u >= LAG and (u - LAG) % 2 == 1 and u - LAG < len(units):
                        copy(u - LAG)
                    if u % HALF == 4 and u >= HALF and u < len(units):
                        sink_terms(u // HALF - 1)
                sink_terms(len(units) // HALF - 1)


def project_phase(g, tag, w_dram, kp, nk, tiles, srcT=None, src=None):
    rows = kp if srcT is None else srcT.shape[0]
    nc = g.nc
    with ExitStack() as st:
        sb = lambda n, s, d=F32: st.enter_context(nc.sbuf_tensor(n, s, d))
        w = sb(tag + "_w", [rows, nk, D])
        if srcT is None:
            srcT = sb(tag + "_srcT", [P, KD, tiles * P])
        gated = sb(tag + "_gated", [P, 2, D])
        w_ready, turned, done = g.sem(tag + "_w_ready"), g.sem(tag + "_turned"), g.sem(tag + "_done")
        turned_a, turned_v = g.sem(tag + "_turned_act"), g.sem(tag + "_turned_dve")
        gated_s, added, padded = g.sem(tag + "_gated_s"), g.sem(tag + "_added"), g.sem(tag + "_padded")

        with nc.Block() as block:
            if rows > kp:
                @block.gpsimd
                def _(pool):
                    pool.memset(w[64:rows, :, :], 0.0).then_inc(padded, 1)

            @block.sync
            def _(sp):
                if rows > kp:
                    sp.wait_ge(padded, 1)
                sp.dma_start(w[0:kp, :, :], w_dram).then_inc(w_ready, 16)

            @block.tensor
            def _(pe):
                if src is not None:
                    for t in range(tiles):
                        if t:
                            pe.wait_ge(turned_a, t)
                            pe.wait_ge(turned_v, t)
                        for k in range(KD):
                            last = pe.transpose(g.ps[:, k // 4, (k % 4) * P:(k % 4 + 1) * P], src[:, t, k::KD], g.ident)
                        last.then_inc(turned, 1)
                pe.wait_ge(w_ready, 16)
                for t in range(tiles):
                    if src is not None:
                        pe.wait_ge(turned_a, t + 1)
                        pe.wait_ge(turned_v, t + 1)
                    if t >= 2:
                        pe.wait_ge(gated_s, t - 1)
                    for k in range(nk):
                        for j in range(2):
                            last = pe.matmul(g.ps[:, 4 + 2 * (t % 2) + j, :], srcT[:, k, t * P:(t + 1) * P],
                                             w[:, k, j * 512:(j + 1) * 512], start=(k == 0), stop=(k == nk - 1))
                    last.then_inc(done, 1)

            @block.scalar
            def _(act):
                if src is not None:
                    for t in range(tiles):
                        act.wait_ge(turned, t + 1)
                        act.activation(srcT[:, 0:KD // 2, t * P:(t + 1) * P],
                                       g.ps[:, 0, :].rearrange("p (k c) -> p k c", c=P), ACT.Copy).then_inc(turned_a, 1)

            @block.vector
            def _(dve):
                if src is not None:
                    for t in range(tiles):
                        dve.wait_ge(turned, t + 1)
                        dve.tensor_copy(srcT[:, KD // 2:KD, t * P:(t + 1) * P],
                                        g.ps[:, 1, :].rearrange("p (k c) -> p k c", c=P)).then_inc(turned_v, 1)
                for t in range(tiles):
                    dve.wait_ge(done, t + 1)
                    if t >= 2:
                        dve.wait_ge(added, t - 1)
                    y = g.ps[:, 4 + 2 * (t % 2):6 + 2 * (t % 2), :].rearrange("p a b -> p (a b)")
                    dve.tensor_tensor(gated[:, t % 2, :], y, g.mod(t, GATE1), ALU.mult).then_inc(gated_s, 1)
                    dve.wait_ge(gated_s, t + 1)
                    dve.tensor_tensor(g.x[:, t, :], g.x[:, t, :], gated[:, t % 2, :], ALU.add).then_inc(added, 1)


class Routes:

    def __init__(self, sb, layer, tiles):
        n = f"l{layer}_"
        self.slot = sb(n + "slot", [P, tiles, EXPERTS])
        self.entry = sb(n + "entry", [P, tiles, EXPERTS, 3])
        self.expert = sb(n + "expert", [1, NBMAX], I32)
        self.count = sb(n + "count", [1, 1], I32)


def route_phase(g, layer, tiles, routes):
    nc, ins = g.nc, g.ins
    tag = f"r{layer}"
    E, S = EXPERTS, slots_of(tiles)
    full = tiles * P // S
    with ExitStack() as st:
        sb = lambda n, s, d=F32: st.enter_context(nc.sbuf_tensor(f"{tag}_{n}", s, d))
        sem = lambda n: g.sem(f"{tag}_{n}")
        norm = Norm(g, f"n2_{layer}", lambda n, s, d=F32: st.enter_context(nc.sbuf_tensor(n, s, d)), tiles,
                    lambda t: g.mod(t, SH2), lambda t: g.mod(t, SC2))
        wr = sb("wr", [P, KD, E])
        wgu = sb("wgu", [P, 2, KD, FE])
        wd = sb("wd", [P, KF, D])
        rbias = sb("rbias", [P, E])
        act_g = sb("act_g", [P, FE])
        hid = sb("hid", [P, FE])
        hidT = sb("hidT", [P, KF, P])
        gated = sb("gated", [P, D])
        score = sb("score", [P, tiles, E])
        sel = sb("sel", [P, tiles, E])
        best = sb("best", [P, tiles, GROUPS, 8])
        gscore = sb("gscore", [P, tiles, GROUPS])
        beats = sb("beats", [P, tiles, GROUPS, GROUPS])
        ties = sb("ties", [P, tiles, GROUPS, GROUPS])
        rank = sb("rank", [P, tiles, GROUPS])
        pen = sb("pen", [P, tiles, GROUPS])
        top8 = sb("top8", [P, tiles, 8])
        chosen = sb("chosen", [P, tiles, E])
        chosen_bf = sb("chosen_bf", [P, tiles, E], BF16)
        weight = sb("weight", [P, tiles, E])
        wsum = sb("wsum", [P, tiles])
        kth = sb("kth", [P, tiles, E])
        nblk = sb("nblk", [E, 1])
        over = sb("over", [E, full])
        blkend = sb("blkend", [E, 1])
        covers = sb("covers", [E, NBMAX])
        blkstart = sb("blkstart", [P, E + 1])
        w_in, h_stored = sem("w_in"), [sem("h_stored0"), sem("h_stored1")]
        routed, scored, gu_done, silued, hid_s = sem("routed"), sem("scored"), sem("gu_done"), sem("silued"), sem("hid_s")
        turned, hidT_s, y_done, gated_s = sem("hid_turned"), sem("hidT_s"), sem("y_done"), sem("gated_s")
        chain_s, masks, pos_done, nblk_s, ends = sem("chain"), sem("masks"), sem("pos_done"), sem("nblk_s"), sem("ends")
        covers_s, owners, blkend_s, xadd = sem("covers_s"), sem("owners"), sem("blkend_s"), sem("xadd")

        with nc.Block() as block:
            @block.sync
            def _(sp):
                sp.dma_start(wr[:], ins["moe_router_w"][layer].rearrange("(p k) e -> p k e", k=KD)).then_inc(w_in, 16)
                sp.dma_start(rbias[:], ins["moe_router_bias"][layer].partition_broadcast(P)).then_inc(w_in, 16)
                sp.dma_start(wgu[:, 0, :, :], ins["shared_w_gate"][layer].rearrange("(p k) f -> p k f", k=KD)).then_inc(w_in, 16)
                sp.dma_start(wgu[:, 1, :, :], ins["shared_w_up"][layer].rearrange("(p k) f -> p k f", k=KD)).then_inc(w_in, 16)
                sp.dma_start(wd[:], ins["shared_w_down"][layer].rearrange("(p j) d -> p j d", j=KF)).then_inc(w_in, 16)
                for t in range(tiles):
                    sp.wait_ge(norm.h_ready, t + 1)
                    sp.dma_start(g.h2_rows[t * P:(t + 1) * P, :], norm.h[:, t % 2, :]).then_inc(h_stored[t % 2], 16)
                for i in range(2):
                    sp.wait_ge(h_stored[i], 16 * (tiles // 2))

            @block.tensor
            def _(pe):
                for t in range(tiles):
                    norm.pe_turn(pe, t)
                pe.wait_ge(w_in, 80)
                for t in range(tiles):
                    norm.wait_hT(pe, t)
                    for k in range(KD):
                        last = pe.matmul(g.ps[:, 7, t * E:(t + 1) * E], norm.hT[:, k, t * P:(t + 1) * P], wr[:, k, :],
                                         start=(k == 0), stop=(k == KD - 1))
                last.then_inc(routed, 1)
                for t in range(tiles):
                    if t:
                        pe.wait_ge(hid_s, t)
                    for k in range(KD):
                        last = pe.matmul(g.ps[:, 4, :].rearrange("p (a f) -> p a f", a=2), norm.hT[:, k, t * P:(t + 1) * P],
                                         wgu[:, :, k, :], start=(k == 0), stop=(k == KD - 1))
                    last.then_inc(gu_done, 1)
                    pe.wait_ge(hid_s, t + 1)
                    if t:
                        pe.wait_ge(hidT_s, t)
                    for j in range(KF):
                        last = pe.transpose(g.ps[:, 2, j * P:(j + 1) * P], hid[:, j::KF], g.ident)
                    last.then_inc(turned, 1)
                    pe.wait_ge(hidT_s, t + 1)
                    if t:
                        pe.wait_ge(gated_s, t)
                    for j in range(KF):
                        for n in range(2):
                            last = pe.matmul(g.ps[:, 5 + n, :], hidT[:, j, :], wd[:, j, n * 512:(n + 1) * 512],
                                             start=(j == 0), stop=(j == KF - 1))
                    last.then_inc(y_done, 1)
                pe.wait_ge(masks, 1)
                for t in range(tiles):
                    for t0 in range(t + 1):
                        pe.matmul(g.ps[:, 3, t * E:(t + 1) * E], g.before_bf[:] if t0 == t else g.ones_bf[:],
                                  chosen_bf[:, t0, :], start=(t0 == 0), stop=(t0 == t))
                for t in range(tiles):
                    last = pe.matmul(g.ps[0:E, 4, 0:1], chosen_bf[:, t, :], g.ones_bf[:, 0:1], start=(t == 0), stop=(t == tiles - 1))
                last.then_inc(pos_done, 1)
                pe.wait_ge(nblk_s, 1)
                pe.matmul(g.ps[:, 5, 0:E + 1], nblk[:, 0:1].to_broadcast([E, P]), g.field("before_e", E), start=True, stop=True)
                pe.matmul(g.ps[0:E, 6, 0:1], g.field("upto_e", E), nblk[:], start=True, stop=True).then_inc(ends, 1)
                pe.wait_ge(covers_s, 1)
                pe.matmul(g.ps[:, 4, 0:NBMAX], g.ones[0:E, :], covers[:], start=True, stop=True).then_inc(owners, 1)

            @block.scalar
            def _(act):
                norm.act_stats(act)
                for t in range(tiles):
                    norm.act_evacuate(act, t)
                act.wait_ge(routed, 1)
                act.activation(score[:], g.ps[:, 7, 0:tiles * E].rearrange("p (t e) -> p t e", e=E), ACT.Sigmoid).then_inc(scored, 1)
                for t in range(tiles):
                    act.wait_ge(gu_done, t + 1)
                    act.activation(act_g[:], g.ps[:, 4, 0:FE], ACT.Silu).then_inc(silued, 1)
                    act.wait_ge(turned, t + 1)
                    act.activation(hidT[:], g.ps[:, 2, 0:FE].rearrange("p (j c) -> p j c", c=P), ACT.Copy).then_inc(hidT_s, 1)

            @block.vector
            def _(dve):
                chain = Chain(dve, chain_s)
                norm.dve_rstd(dve)
                for t in range(tiles):
                    norm.dve_h(dve, t, stored=h_stored)
                    norm.dve_evacuate(dve, t)
                for t in range(tiles):
                    dve.wait_ge(silued, t + 1)
                    dve.tensor_tensor(hid[:], act_g[:], g.ps[:, 4, FE:2 * FE], ALU.mult).then_inc(hid_s, 1)
                    dve.wait_ge(y_done, t + 1)
                    if t:
                        dve.wait_ge(xadd, t)
                    dve.tensor_tensor(gated[:], g.ps[:, 5:7, :].rearrange("p a b -> p (a b)"), g.mod(t, GATE2), ALU.mult).then_inc(gated_s, 1)
                    dve.wait_ge(gated_s, t + 1)
                    dve.tensor_tensor(g.x[:, t, :], g.x[:, t, :], gated[:], ALU.add).then_inc(xadd, 1)

                dve.wait_ge(scored, 1)
                dve.wait_ge(w_in, 80)
                by_group = lambda a: a.rearrange("p t (g e) -> p t g e", e=PER_GROUP)
                chain.link(dve.tensor_tensor(sel[:], score[:], rbias[:, None, :].to_broadcast([P, tiles, E]), ALU.add))
                for t in range(tiles):
                    for gr in range(GROUPS):
                        last = dve.max(best[:, t, gr, :], sel[:, t, gr * PER_GROUP:(gr + 1) * PER_GROUP])
                        n = chain.done(last)
                dve.wait_ge(chain_s, n)
                chain.link(dve.tensor_tensor(gscore[:], best[:, :, :, 0], best[:, :, :, 1], ALU.add))
                mine = gscore[:, :, :, None].to_broadcast([P, tiles, GROUPS, GROUPS])
                other = gscore[:, :, None, :].to_broadcast([P, tiles, GROUPS, GROUPS])
                lower = g.field("lower_g").rearrange("p (a b) -> p a b", b=GROUPS)
                chain.done(dve.tensor_tensor(beats[:], other, mine, ALU.is_gt))
                chain.link(dve.tensor_tensor(ties[:], other, mine, ALU.is_equal))
                chain.link(dve.tensor_tensor(ties[:], ties[:], lower[:, None, :, :].to_broadcast([P, tiles, GROUPS, GROUPS]), ALU.mult))
                chain.link(dve.tensor_tensor(beats[:], beats[:], ties[:], ALU.add))
                chain.link(dve.tensor_reduce(rank[:], beats[:], AX.X, ALU.add))
                chain.link(dve.tensor_scalar(rank[:], rank[:], float(TOP_GROUPS), None, ALU.is_lt))
                chain.link(dve.tensor_scalar(pen[:], rank[:], -NEG, NEG, ALU.mult, ALU.add))
                wide = lambda a: a[:, :, :, None].to_broadcast([P, tiles, GROUPS, PER_GROUP])
                chain.link(dve.tensor_tensor(by_group(sel[:]), by_group(sel[:]), wide(rank[:]), ALU.mult))
                chain.link(dve.tensor_tensor(by_group(sel[:]), by_group(sel[:]), wide(pen[:]), ALU.add))
                for t in range(tiles):
                    n = chain.done(dve.max(top8[:, t, :], sel[:, t, :]))
                dve.wait_ge(chain_s, n)
                for t in range(tiles):
                    n = chain.done(dve.match_replace(chosen[:, t, :], top8[:, t, :], sel[:, t, :], -3e38))
                dve.wait_ge(chain_s, n)
                chain.link(dve.tensor_scalar(chosen[:], chosen[:], -2e38, None, ALU.is_lt))
                dve.tensor_copy(chosen_bf[:], chosen[:]).then_inc(masks, 1)
                chain.link(dve.tensor_tensor(weight[:], score[:], chosen[:], ALU.mult))
                chain.link(dve.tensor_reduce(wsum[:], weight[:], AX.X, ALU.add))
                chain.link(dve.reciprocal(wsum[:], wsum[:]))
                chain.link(dve.tensor_scalar(wsum[:], wsum[:], ROUTED_SCALE, None, ALU.mult))
                chain.done(dve.tensor_tensor(routes.entry[:, :, :, 1], weight[:], wsum[:, :, None].to_broadcast([P, tiles, E]), ALU.mult))
                for t in range(tiles):
                    n = chain.done(dve.tensor_tensor_scan(kth[:, t, :], g.ones[:, 0:E], chosen[:, t, :], 0.0, ALU.mult, ALU.add))
                tok = g.field("tok")[:, 0:tiles]
                chain.done(dve.tensor_scalar(routes.entry[:, :, :, 0], tok[:, :, None].to_broadcast([P, tiles, E]), -FAR, None, ALU.add))
                dve.wait_ge(chain_s, n)
                for t in range(tiles):
                    chain.link(dve.tensor_scalar(wsum[:, t:t + 1], tok[:, t:t + 1], float(TOPK), -1.0 - FAR, ALU.mult, ALU.add))
                    chain.done(dve.tensor_scalar(routes.entry[:, t, :, 2], kth[:, t, :], wsum[:, t:t + 1], None, ALU.add))
                dve.wait_ge(pos_done, 1)
                for j in range(1, full):
                    chain.link(dve.tensor_scalar(over[:, j:j + 1], g.ps[0:E, 4, 0:1], float(S * j), None, ALU.is_gt))
                chain.link(dve.tensor_reduce(over[:, 0:1], over[:, 1:full], AX.X, ALU.add))
                dve.tensor_scalar(nblk[:], over[:, 0:1], 1.0, None, ALU.add).then_inc(nblk_s, 1)
                dve.wait_ge(ends, 1)
                chain.done(dve.tensor_copy(blkstart[:], g.ps[:, 5, 0:E + 1]))
                chain.link(dve.tensor_copy(blkend[:], g.ps[0:E, 6, 0:1]))
                dve.tensor_scalar(covers[:], g.field("iota_b", E), blkend[:, 0:1], None, ALU.is_ge).then_inc(covers_s, 1)
                chain.done(dve.tensor_scalar(routes.count[:], blkstart[0:1, E:E + 1], -1.0, None, ALU.add))
                chain.link(dve.tensor_scalar(blkstart[:, 0:E], blkstart[:, 0:E], float(S), 1.0, ALU.mult, ALU.add))
                pos = g.ps[:, 3, 0:tiles * E].rearrange("p (t e) -> p t e", e=E)
                chain.link(dve.tensor_tensor(routes.slot[:], pos, blkstart[:, None, 0:E].to_broadcast([P, tiles, E]), ALU.add))
                chain.link(dve.tensor_tensor(routes.slot[:], routes.slot[:], chosen[:], ALU.mult))
                chain.link(dve.tensor_scalar(routes.slot[:], routes.slot[:], -1.0, None, ALU.add))
                dve.wait_ge(owners, 1)
                chain.link(dve.tensor_scalar(routes.expert[:], g.ps[0:1, 4, 0:NBMAX], float(E - 1), None, ALU.min))


def expert_phase(g, layer, tiles, routes):
    nc, ins = g.nc, g.ins
    tag = f"m{layer}"
    S = slots_of(tiles)
    last_token, last_row = tiles * P - 1, tiles * P * TOPK - 1
    with ExitStack() as st:
        sb = lambda n, s, d=F32: st.enter_context(nc.sbuf_tensor(f"{tag}_{n}", s, d))
        sem = lambda n: g.sem(f"{tag}_{n}")
        wgu = sb("wgu", [P, 2, 2, KD, FE])
        wd = sb("wd", [P, 2, KF, D])
        xg = [sb(f"xg{q}", [S, D]) for q in range(2)]
        xT = sb("xT", [P, 2, KD, S])
        onehot = sb("onehot", [P, 2, tiles, S])
        meta = sb("meta", [S, NBMAX, 3])
        gidx = [sb(f"gidx{q}", [S, 1], U32) for q in range(2)]
        sidx = [sb(f"sidx{q}", [S, 1], U32) for q in range(2)]
        act_g = sb("act_g", [S, FE])
        hid = sb("hid", [S, FE])
        hidT = sb("hidT", [P, KF, S])
        ysb = [sb(f"ysb{q}", [S, D]) for q in range(2)]
        pair = lambda n: [sem(n + "0"), sem(n + "1")]
        wgu_in, wd_in, gathered, scattered = pair("wgu_in"), pair("wd_in"), pair("gathered"), pair("scattered")
        onehot_s, meta_done, idx_s, xT_turned, xT_a, xT_v = (sem(n) for n in ("onehot_s", "meta_done", "idx_s", "xT_turned", "xT_a", "xT_v"))
        gu_done, silued, hid_s, hid_turned, hidT_s = (sem(n) for n in ("gu_done", "silued", "hid_s", "hid_turned", "hidT_s"))
        y_done, y_a, y_v, sidx_s, zeroed, issue, meta_v = (sem(n) for n in ("y_done", "y_a", "y_v", "sidx_s", "zeroed", "issue", "meta_v"))
        GU, YB, XB, HB, MB = 0, 1, 3, 5, 6

        gate_w = ins["moe_w_gate"][layer].rearrange("e (p k) f -> e p k f", k=KD)
        up_w = ins["moe_w_up"][layer].rearrange("e (p k) f -> e p k f", k=KD)
        down_w = ins["moe_w_down"][layer].rearrange("e (p j) d -> e p j d", j=KF)

        def last_pair(eng):
            return eng.value_load(routes.count[0:1, 0:1], min_val=EXPERTS - 1, max_val=max_blocks(tiles) - 1) >> 1

        def owner(eng, b):
            return eng.value_load(routes.expert[0:1, bass.ds(b, 1)], min_val=0, max_val=EXPERTS - 1)

        def after_wait(eng):
            eng.sem_inc(issue, 1)

        with nc.Block() as block:
            @block.sync
            def _(sp):
                def gate_up(i, q):
                    b = 2 * i + q
                    e = owner(sp, b)
                    if not (isinstance(i, int) and i == 0):
                        sp.wait_ge(gu_done, b - 1)
                        after_wait(sp)
                    for a, w in enumerate((gate_w, up_w)):
                        sp.dma_start(wgu[:, q, a, :, :], w[bass.ds(e, 1)].rearrange("o p k f -> p (o k) f")).then_inc(wgu_in[q], 16)

                def down(i, q):
                    b = 2 * i + q
                    e = owner(sp, b)
                    if not (isinstance(i, int) and i == 0):
                        sp.wait_ge(y_done, b - 1)
                        after_wait(sp)
                    sp.dma_start(wd[:, q, :, :], down_w[bass.ds(e, 1)].rearrange("o p j d -> p (o j) d")).then_inc(wd_in[q], 16)

                final = last_pair(sp)
                gate_up(0, 0)
                down(0, 0)
                gate_up(0, 1)
                gate_up(1, 0)
                down(0, 1)
                gate_up(1, 1)
                down(1, 0)
                with sp.Fori(2, final + 1) as i:
                    gate_up(i, 0)
                    down(i - 1, 1)
                    gate_up(i, 1)
                    down(i, 0)
                down(final, 1)

            @block.gpsimd
            def _(pool):
                def gather(i, q):
                    b = 2 * i + q
                    pool.wait_ge(idx_s, b + 1)
                    if not (isinstance(i, int) and i == 0):
                        pool.wait_ge(xT_turned, b - 1)
                    after_wait(pool)
                    pool.indirect_dma_start(xg[q][:], None, g.h2_rows[0:tiles * P, :], bass.IndirectOffsetOnAxis(ap=gidx[q][:, 0:1], axis=0),
                                            bounds_check=last_token, oob_is_err=False).then_inc(gathered[q], 16)

                def scatter(i, q):
                    b = 2 * i + q
                    pool.wait_ge(y_a, b + 1)
                    pool.wait_ge(y_v, b + 1)
                    pool.wait_ge(sidx_s, b + 1)
                    after_wait(pool)
                    pool.indirect_dma_start(g.y_rows[0:tiles * P * TOPK, :], bass.IndirectOffsetOnAxis(ap=sidx[q][:, 0:1], axis=0), ysb[q][:], None,
                                            bounds_check=last_row, oob_is_err=False).then_inc(scattered[q], 16)

                for q in range(2):
                    pool.memset(xg[q][:], 0.0).then_inc(zeroed, 1)
                pool.wait_ge(zeroed, 2)
                final = last_pair(pool)
                gather(0, 0)
                gather(0, 1)
                gather(1, 0)
                gather(1, 1)
                scatter(0, 0)
                gather(2, 0)
                with pool.Fori(1, final + 1) as i:
                    scatter(i - 1, 1)
                    gather(i + 1, 1)
                    scatter(i, 0)
                    gather(i + 2, 0)
                scatter(final, 1)
                for q in range(2):
                    pool.wait_ge(scattered[q], 16 * final + 16)
                    after_wait(pool)
                    pool.wait_ge(gathered[q], 16 * final + (32 if q else 48))
                    after_wait(pool)

            @block.tensor
            def _(pe):
                def slots(i, q):
                    b = 2 * i + q
                    e = owner(pe, b)
                    pe.wait_ge(onehot_s, b + 1)
                    if not (isinstance(i, int) and i == 0):
                        pe.wait_ge(idx_s, b - 1)
                    for t in range(tiles):
                        last = pe.matmul(g.ps[0:S, MB + q, 0:3], onehot[:, q, t, :],
                                         routes.entry[:, t, bass.ds(e, 1), :].rearrange("p o c -> p (o c)"),
                                         start=(t == 0), stop=(t == tiles - 1))
                    last.then_inc(meta_done, 1)

                def turn_tokens(i, q, first=False):
                    b = 2 * i + q
                    pe.wait_ge(gathered[q], 16 * (i + 1))
                    if not first:
                        pe.wait_ge(xT_a, b)
                        pe.wait_ge(xT_v, b)
                    after_wait(pe)
                    for k in range(KD):
                        last = pe.transpose(g.ps[:, XB + k // 4, (k % 4) * S:(k % 4 + 1) * S], xg[q][:, k::KD], g.ident[0:S, 0:S])
                    last.then_inc(xT_turned, 1)

                def down(i, q, first=False):
                    b = 2 * i + q
                    pe.wait_ge(hidT_s, b + 1)
                    pe.wait_ge(wd_in[q], 16 * (i + 1))
                    if not first:
                        pe.wait_ge(y_a, b)
                        pe.wait_ge(y_v, b)
                    for j in range(KF):
                        for n in range(2):
                            last = pe.matmul(g.ps[0:S, YB + n, :], hidT[:, j, :], wd[:, q, j, n * 512:(n + 1) * 512],
                                             start=(j == 0), stop=(j == KF - 1))
                    last.then_inc(y_done, 1)

                def step(i, q):
                    b = 2 * i + q
                    first = isinstance(i, int) and i == 0 and q == 0
                    pe.wait_ge(xT_a, b + 1)
                    pe.wait_ge(xT_v, b + 1)
                    pe.wait_ge(wgu_in[q], 32 * (i + 1))
                    if not first:
                        pe.wait_ge(hid_s, b)
                    for k in range(KD):
                        last = pe.matmul(g.ps[0:S, GU, :].rearrange("p (a f) -> p a f", a=2), xT[:, q, k, :],
                                         wgu[:, q, :, k, :], start=(k == 0), stop=(k == KD - 1))
                    last.then_inc(gu_done, 1)
                    turn_tokens(i + q, 1 - q)
                    if not first:
                        down(i - 1 + q, 1 - q, first=(isinstance(i, int) and i == 0 and q == 1))
                    pe.wait_ge(hid_s, b + 1)
                    if not first:
                        pe.wait_ge(hidT_s, b)
                    after_wait(pe)
                    for j in range(KF):
                        last = pe.transpose(g.ps[:, HB, j * S:(j + 1) * S], hid[:, j::KF], g.ident[0:S, 0:S])
                    last.then_inc(hid_turned, 1)
                    slots(i + 1 + q, 1 - q)

                slots(0, 0)
                slots(0, 1)
                slots(1, 0)
                turn_tokens(0, 0, first=True)
                final = last_pair(pe)
                step(0, 0)
                step(0, 1)
                with pe.Fori(1, final + 1) as i:
                    step(i, 0)
                    step(i, 1)
                down(final, 1)

            @block.scalar
            def _(act):
                def tokens(i, q):
                    b = 2 * i + q
                    act.wait_ge(xT_turned, b + 1)
                    act.activation(xT[:, q, 0:KD // 2, :], g.ps[:, XB, 0:4 * S].rearrange("p (k c) -> p k c", c=S), ACT.Copy).then_inc(xT_a, 1)

                def y_half(i, q, wait=True):
                    b = 2 * i + q
                    act.wait_ge(y_done, b + 1)
                    if wait:
                        act.wait_ge(scattered[q], 16 * i)
                    act.activation(ysb[q][:, 0:512], g.ps[0:S, YB, :], ACT.Copy).then_inc(y_a, 1)

                def step(i, q):
                    b = 2 * i + q
                    peeled = isinstance(i, int)
                    act.wait_ge(gu_done, b + 1)
                    if not (peeled and q == 0):
                        act.wait_ge(hid_s, b)
                    act.activation(act_g[:], g.ps[0:S, GU, 0:FE], ACT.Silu).then_inc(silued, 1)
                    tokens(i + q, 1 - q)
                    if not (peeled and q == 0):
                        y_half(i - 1 + q, 1 - q, wait=not peeled)
                    act.wait_ge(hid_turned, b + 1)
                    act.activation(hidT[:], g.ps[:, HB, 0:KF * S].rearrange("p (j c) -> p j c", c=S), ACT.Copy).then_inc(hidT_s, 1)

                tokens(0, 0)
                final = last_pair(act)
                step(0, 0)
                step(0, 1)
                act.wait_ge(gu_done, 3)
                act.wait_ge(hid_s, 2)
                act.activation(act_g[:], g.ps[0:S, GU, 0:FE], ACT.Silu).then_inc(silued, 1)
                tokens(1, 1)
                y_half(0, 1, wait=False)
                act.wait_ge(hid_turned, 3)
                act.activation(hidT[:], g.ps[:, HB, 0:KF * S].rearrange("p (j c) -> p j c", c=S), ACT.Copy).then_inc(hidT_s, 1)
                act.wait_ge(gu_done, 4)
                act.wait_ge(hid_s, 3)
                act.activation(act_g[:], g.ps[0:S, GU, 0:FE], ACT.Silu).then_inc(silued, 1)
                tokens(2, 0)
                y_half(1, 0)
                act.wait_ge(hid_turned, 4)
                act.activation(hidT[:], g.ps[:, HB, 0:KF * S].rearrange("p (j c) -> p j c", c=S), ACT.Copy).then_inc(hidT_s, 1)
                with act.Fori(2, final + 1) as i:
                    step(i, 0)
                    step(i, 1)
                y_half(final, 1)

            @block.vector
            def _(dve):
                def pick(i, q, wait=True):
                    b = 2 * i + q
                    e = owner(dve, b)
                    if wait:
                        dve.wait_ge(meta_done, b - 1)
                    for t in range(tiles):
                        last = dve.tensor_scalar(onehot[:, q, t, :], g.field("iota")[:, 0:S], routes.slot[:, t, bass.ds(e, 1)],
                                                 g.table[:, bass.ds(b + FIELD[f"negbase{layer}"][0], 1)], ALU.subtract, ALU.is_equal)
                    last.then_inc(onehot_s, 1)

                def indices(i, q, wait=True):
                    b = 2 * i + q
                    dve.wait_ge(meta_done, b + 1)
                    if wait:
                        dve.wait_ge(gathered[q], 16 * i)
                    dve.tensor_copy(meta[:, bass.ds(b, 1), :].rearrange("p o c -> p (o c)"), g.ps[0:S, MB + q, 0:3]).then_inc(meta_v, 1)
                    dve.tensor_scalar(gidx[q][:], g.ps[0:S, MB + q, 0:1], FAR, None, ALU.add).then_inc(idx_s, 1)

                def tokens(i, q):
                    b = 2 * i + q
                    dve.wait_ge(xT_turned, b + 1)
                    dve.tensor_copy(xT[:, q, KD // 2:KD, :], g.ps[:, XB + 1, 0:4 * S].rearrange("p (k c) -> p k c", c=S)).then_inc(xT_v, 1)

                def y_half(i, q, wait=True):
                    b = 2 * i + q
                    if wait:
                        dve.wait_ge(scattered[q], 16 * i)
                    dve.tensor_scalar(sidx[q][:], meta[:, bass.ds(b, 1), 2], FAR, None, ALU.add).then_inc(sidx_s, 1)
                    dve.wait_ge(y_done, b + 1)
                    dve.tensor_copy(ysb[q][:, 512:D], g.ps[0:S, YB + 1, :]).then_inc(y_v, 1)

                def step(i, q, first_y=False):
                    b = 2 * i + q
                    first = isinstance(i, int) and i == 0 and q == 0
                    dve.wait_ge(silued, b + 1)
                    dve.wait_ge(meta_v, b + 1)
                    if not first:
                        dve.wait_ge(hid_turned, b)
                    dve.scalar_tensor_tensor(hid[:], act_g[:], meta[:, bass.ds(b, 1), 1], g.ps[0:S, GU, FE:2 * FE],
                                             ALU.mult, ALU.mult).then_inc(hid_s, 1)
                    tokens(i + q, 1 - q)
                    if not first:
                        y_half(i - 1 + q, 1 - q, wait=not first_y)
                    pick(i + 2, q)
                    indices(i + 1 + q, 1 - q)

                pick(0, 0, wait=False)
                pick(0, 1, wait=False)
                indices(0, 0, wait=False)
                indices(0, 1, wait=False)
                pick(1, 0)
                indices(1, 0)
                pick(1, 1)
                tokens(0, 0)
                final = last_pair(dve)
                step(0, 0)
                step(0, 1, first_y=True)
                step(1, 0, first_y=True)
                step(1, 1)
                with dve.Fori(2, final + 1) as i:
                    step(i, 0)
                    step(i, 1)
                y_half(final, 1)


def combine_phase(g, layer, tiles):
    nc = g.nc
    tag = f"c{layer}"
    H = D // 2
    jobs = [(t, h) for t in range(tiles) for h in range(2)]
    with ExitStack() as st:
        sb = lambda n, s, d=F32: st.enter_context(nc.sbuf_tensor(f"{tag}_{n}", s, d))
        rows = sb("rows", [P, 2, TOPK, H])
        total = sb("total", [P, 2, H])
        rows_in = [g.sem(f"{tag}_rows_in{q}") for q in range(2)]
        summed, chain_s = g.sem(f"{tag}_summed"), g.sem(f"{tag}_chain")
        src = g.y_rows[0:tiles * P * TOPK, :].rearrange("(t p k) d -> t p k d", p=P, k=TOPK)
        with nc.Block() as block:
            @block.sync
            def _(sp):
                for n, (t, h) in enumerate(jobs):
                    if n >= 2:
                        sp.wait_ge(summed, n - 1)
                    sp.dma_start(rows[:, n % 2, :, :], src[t][:, :, h * H:(h + 1) * H]).then_inc(rows_in[n % 2], 16)

            @block.vector
            def _(dve):
                chain = Chain(dve, chain_s)
                for n, (t, h) in enumerate(jobs):
                    q = n % 2
                    x = g.x[:, t, h * H:(h + 1) * H]
                    dve.wait_ge(rows_in[q], 16 * (n // 2 + 1))
                    dve.tensor_reduce(total[:, q, :], rows[:, q, :, :].rearrange("p k d -> p d k"), AX.X, ALU.add).then_inc(summed, 1)
                    dve.wait_ge(summed, n + 1)
                    chain.link(dve.tensor_tensor(total[:, q, :], total[:, q, :], g.mod(t, GATE2)[:, h * H:(h + 1) * H], ALU.mult))
                    chain.link(dve.tensor_tensor(x, x, total[:, q, :], ALU.add))


BA, BX, LAM, CW, CB = 0, 2, 4, 6, 10


def lru_in_phase(g, par, uc, gate):
    nc, ins = g.nc, g.ins
    CH = 640
    PAD = SEQ + TAPS - 1
    with ExitStack() as st:
        sb = lambda n, s, d=F32: st.enter_context(nc.sbuf_tensor(n, s, d))
        norm = Norm(g, "n3", sb, TILES, lambda t: g.mod(t, SH1), lambda t: g.mod(t, SC1))
        w = sb("lru_w_in_sb", [P, 2, KD, CH])
        ut = sb("lru_ut", [P, TILES, RNN])
        upad = sb("lru_upad", [RW, 2, 2, PAD])
        praw = sb("lru_praw", [96, 2, RW])
        w_ready = [g.sem(f"li_w_ready{q}") for q in range(2)]
        par_in, par_turned, par_s = g.sem("li_par_in"), g.sem("li_par_turned"), g.sem("li_par_s")
        done, evac, turned, padded = g.sem("li_done"), g.sem("li_evac"), g.sem("li_turned"), g.sem("li_padded")
        conv, padz, chain_s = g.sem("li_conv"), g.sem("li_padz"), g.sem("li_chain")
        jobs = [(c, t) for c in (2, 3) for t in range(TILES)] + [(c, t) for c in (0, 1) for t in range(LAT_TILES)]
        order = [2, 3, 0, 1]
        last_job = {c: max(n for n, (cc, _) in enumerate(jobs) if cc == c) for c in order}

        with nc.Block() as block:
            @block.sync
            def _(sp):
                src = ins["lru_w_in"][0].rearrange("(p k) n -> p k n", k=KD)
                for i, c in enumerate(order):
                    if i >= 2:
                        sp.wait_ge(done, last_job[order[i - 2]] + 1)
                    sp.dma_start(w[:, i % 2, :, :], src[:, :, c * CH:(c + 1) * CH]).then_inc(w_ready[i % 2], 16)

            @block.gpsimd
            def _(pool):
                for i, name in enumerate(("lru_ba", "lru_bx", "lru_lam")):
                    pool.dma_start(praw[32 * i:32 * i + 32, 0, :], ins[name][0].rearrange("d (n c) -> (d n) c", c=RW)).then_inc(par_in, 16)
                pool.dma_start(praw[0:64, 1, :], ins["lru_conv_w"][0].rearrange("j (n c) -> (j n) c", c=RW)).then_inc(par_in, 16)
                pool.dma_start(praw[64:80, 1, :], ins["lru_conv_b"][0].rearrange("(n c) -> n c", c=RW)).then_inc(par_in, 16)
                pool.memset(upad[:], 0.0).then_inc(padz, 1)
                pool.wait_ge(padz, 1)
                pool.memset(uc[64:RP, :, :], 0.0).then_inc(padz, 1)

            @block.tensor
            def _(pe):
                pe.wait_ge(par_in, 80)
                pe.transpose(g.ps[0:RW, 6, 0:96], praw[:, 0, :], g.ident[0:96, 0:96])
                pe.transpose(g.ps[0:RW, 6, 96:176], praw[0:80, 1, :], g.ident[0:80, 0:80]).then_inc(par_turned, 1)
                for t in range(TILES):
                    norm.pe_turn(pe, t)

                def block_turn(n):
                    if n >= 2:
                        pe.wait_ge(padded, n - 1)
                    for t in range(TILES):
                        last = pe.transpose(g.ps[0:RW, 4 + n % 2, t * P:(t + 1) * P], ut[:, t, n * RW:(n + 1) * RW], g.ident)
                    last.then_inc(turned, 1)

                for n, (c, t) in enumerate(jobs):
                    if t == 0:
                        i = order.index(c)
                        pe.wait_ge(w_ready[i % 2], 16 * (i // 2 + 1))
                    norm.wait_hT(pe, TILES - 1 if n == 1 else t)
                    if n >= 2:
                        pe.wait_ge(evac, n - 1)
                    b = 2 if n % 2 == 0 else 0
                    for k in range(KD):
                        for j in range(2):
                            last = pe.matmul(g.ps[:, b + j, 0:CH // 2], norm.hT[:, k, t * P:(t + 1) * P],
                                             w[:, order.index(c) % 2, k, j * (CH // 2):(j + 1) * (CH // 2)],
                                             start=(k == 0), stop=(k == KD - 1))
                    last.then_inc(done, 1)
                    if 4 <= n < 8:
                        if n == 4:
                            pe.wait_ge(evac, 4)
                        for m in range(2):
                            block_turn(2 * (n - 4) + m)
                    if n >= 8:
                        if n == 8:
                            pe.wait_ge(evac, 8)
                        for m in range(2):
                            block_turn(8 + 2 * (n - 8) + m)

            @block.scalar
            def _(act):
                norm.act_stats(act)
                for t in range(TILES):
                    norm.act_evacuate(act, t)
                for n, (c, t) in enumerate(jobs):
                    act.wait_ge(done, n + 1)
                    b = 2 if n % 2 == 0 else 0
                    dst, c0, f = (ut, (c - 2) * CH, ACT.Copy) if c >= 2 else (gate, c * CH, ACT.Gelu_apprx_tanh)
                    act.activation(dst[:, t, c0:c0 + CH].rearrange("p (j c) -> p j c", j=2), g.ps[:, b:b + 2, 0:CH // 2], f).then_inc(evac, 1)

            @block.vector
            def _(dve):
                chain = Chain(dve, chain_s)
                dve.wait_ge(par_turned, 1)
                dve.tensor_copy(par[:], g.ps[0:RW, 6, 0:176]).then_inc(par_s, 1)
                dve.wait_ge(par_s, 1)
                norm.dve_rstd(dve)
                for t in range(TILES):
                    norm.dve_h(dve, t)
                    norm.dve_evacuate(dve, t)
                dve.wait_ge(padz, 2)
                col = lambda s, n: par[:, s * RB + n:s * RB + n + 1]
                for n in range(RB):
                    q = n % 2
                    dve.wait_ge(turned, n + 1)
                    dve.tensor_copy(upad[:, q, :, LEFT:LEFT + SEQ], g.ps[0:RW, 4 + q, :].rearrange("p (s c) -> p s c", s=2)).then_inc(padded, 1)
                    dve.wait_ge(padded, n + 1)
                    u = uc[0:RW, n, :].rearrange("p (s c) -> p s c", s=2)
                    chain.link(dve.tensor_scalar(u, upad[:, q, :, 0:SEQ], col(CW, n), col(CB, n), ALU.mult, ALU.add))
                    for j in range(1, TAPS):
                        chain.link(dve.scalar_tensor_tensor(u, upad[:, q, :, j:j + SEQ], col(CW + j, n), u, ALU.mult, ALU.add))


def lru_scan_phase(g, par, uc, gate, hsum):
    nc, ins = g.nc, g.ins
    HB = 4
    IG = 4
    groups = [(d, h) for d in range(2) for h in range(RB // HB)]
    GB = 3
    with ExitStack() as st:
        sb = lambda n, s, d=F32: st.enter_context(nc.sbuf_tensor("ls_" + n, s, d))
        sem = lambda n: g.sem("ls_" + n)
        wa = sb("wa", [RP, 2 * RB, RW])
        wx = sb("wx", [RP, 2 * RB, RW])
        z, w1, dd, lnw, m0 = (sb(n, [RW, 2 * RB]) for n in ("z", "w1", "dd", "lnw", "m0"))
        pos8, neg8 = sb("pos8", [RW, 2 * RB]), sb("neg8", [RW, 2 * RB])
        r = sb("r", [RW, 2 * HB, TOK])
        bu = sb("bu", [RW, 2 * HB, TOK])
        a = sb("a", [RW, 2 * HB, TOK])
        ig = sb("ig", [RW, IG, TOK])
        sq = sb("sq", [RW, 2, TOK])
        hc = sb("hc", [RW, 2, CTX])
        back = sb("back", [RW, 2, SEQ])
        w_in, w_done, zs, ln_s, chain_s = sem("w_in"), sem("w_done"), sem("zs"), sem("ln_s"), sem("chain")
        rates, sig, bus, exps, sqs, omts, roots, scans = (sem(n) for n in ("rates", "sig", "bus", "exps", "sqs", "omts", "roots", "scans"))
        gturned, gated, acts, padded = sem("gturned"), sem("gated"), sem("acts"), sem("padded")
        lam = par[:, LAM * RB:(LAM + 2) * RB]
        blocks = [(d, h, n) for d, h in groups for n in range(HB)]

        with nc.Block() as block:
            @block.sync
            def _(sp):
                sp.wait_ge(padded, 3)
                for dst, name in ((wa, "lru_wa"), (wx, "lru_wx")):
                    sp.dma_start(dst[0:RW, :, :], ins[name][0].rearrange("d n c f -> c (d n) f")).then_inc(w_in, 16)

            @block.tensor
            def _(pe):
                pe.wait_ge(w_in, 32)
                for j, (d, h, n) in enumerate(blocks):
                    ch = h * HB + n
                    if j >= GB:
                        pe.wait_ge(sig, 2 * (j - GB + 1))
                    b = 2 * (j % GB)
                    pe.matmul(g.ps[0:RW, b, :], wa[:, d * RB + ch, :], uc[:, ch, :], start=True, stop=True)
                    pe.matmul(g.ps[0:RW, b + 1, :], wx[:, d * RB + ch, :], uc[:, ch, :], start=True, stop=True).then_inc(w_done, 1)
                for n in range(RB):
                    if n >= 2:
                        pe.wait_ge(gated, n - 1)
                    for t in range(LAT_TILES):
                        last = pe.transpose(g.ps[0:RW, 6 + n % 2, t * P:(t + 1) * P], gate[:, t, n * RW:(n + 1) * RW], g.ident)
                    last.then_inc(gturned, 1)

            @block.scalar
            def _(act):
                act.activation(z[:], lam, ACT.Abs).then_inc(acts, 1)
                act.wait_ge(acts, 1)
                act.activation(z[:], z[:], ACT.Exp, scale=-1.0).then_inc(zs, 1)
                act.wait_ge(zs, 2)
                act.activation(lnw[:], w1[:], ACT.Ln).then_inc(ln_s, 1)

                def sigmoids(gi):
                    d, h = groups[gi]
                    for n in range(HB):
                        j, ch = gi * HB + n, h * HB + n
                        act.wait_ge(w_done, j + 1)
                        if gi >= 2:
                            act.wait_ge(scans, j - 2 * HB + 1)
                        col = lambda row: par[:, (row + d) * RB + ch:(row + d) * RB + ch + 1]
                        act.activation(r[:, j % (2 * HB), :], g.ps[0:RW, 2 * (j % GB), :], ACT.Sigmoid, bias=col(BA)).then_inc(sig, 1)
                        if j >= IG:
                            act.wait_ge(bus, j - IG + 1)
                        act.activation(ig[:, j % IG, :], g.ps[0:RW, 2 * (j % GB) + 1, :], ACT.Sigmoid, bias=col(BX)).then_inc(sig, 1)

                def decays(gi):
                    d, h = groups[gi]
                    for n in range(HB):
                        j = gi * HB + n
                        c = d * RB + h * HB + n
                        q = j % (2 * HB)
                        act.wait_ge(sig, 2 * (j + 1))
                        act.activation(a[:, q, :], r[:, q, :], ACT.Exp, scale=neg8[:, c:c + 1]).then_inc(exps, 1)
                        act.wait_ge(exps, 2 * j + 1)
                        act.activation(r[:, q, :], r[:, q, :], ACT.Tanh, scale=pos8[:, c:c + 1]).then_inc(exps, 1)

                def square_roots(gi):
                    for j in range(gi * HB, (gi + 1) * HB):
                        act.wait_ge(omts, j + 1)
                        act.activation(r[:, j % (2 * HB), :], r[:, j % (2 * HB), :], ACT.Sqrt).then_inc(roots, 1)

                sigmoids(0)
                act.wait_ge(rates, 1)
                for gi in range(len(groups)):
                    decays(gi)
                    if gi + 1 < len(groups):
                        sigmoids(gi + 1)
                    square_roots(gi)

            @block.gpsimd
            def _(pool):
                for n, t in enumerate((hsum, wa, wx)):
                    pool.memset(t[64:RP, :, :], 0.0).then_inc(padded, 1)
                    pool.wait_ge(padded, n + 1)
                for j in range(len(blocks)):
                    n = j % (2 * HB)
                    pool.wait_ge(exps, 2 * j + 1)
                    if j >= 2:
                        pool.wait_ge(omts, j - 1)
                    pool.tensor_tensor(sq[:, j % 2, :], a[:, n, :], a[:, n, :], ALU.mult).then_inc(sqs, 1)

            @block.vector
            def _(dve):
                chain = Chain(dve, chain_s)
                dve.wait_ge(zs, 1)
                dve.tensor_scalar(w1[:], z[:], 1.0, None, ALU.add).then_inc(zs, 1)
                dve.wait_ge(zs, 2)
                chain.link(dve.tensor_scalar(dd[:], w1[:], -1.0, None, ALU.add))
                chain.link(dve.tensor_scalar(m0[:], dd[:], 0.0, None, ALU.is_equal))
                chain.link(dve.tensor_tensor(dd[:], dd[:], m0[:], ALU.add))
                chain.link(dve.reciprocal(dd[:], dd[:]))
                dve.wait_ge(ln_s, 1)
                chain.link(dve.tensor_tensor(lnw[:], lnw[:], m0[:], ALU.add))
                chain.link(dve.tensor_tensor(lnw[:], lnw[:], dd[:], ALU.mult))
                chain.link(dve.tensor_tensor(lnw[:], lnw[:], z[:], ALU.mult))
                chain.link(dve.tensor_scalar(m0[:], lam, -1.0, 0.0, ALU.mult, ALU.max))
                chain.link(dve.tensor_tensor(m0[:], m0[:], lnw[:], ALU.add))
                chain.link(dve.tensor_scalar(pos8[:], m0[:], 8.0, None, ALU.mult))
                dve.tensor_scalar(neg8[:], m0[:], -8.0, None, ALU.mult).then_inc(rates, 1)
                dve.wait_ge(padded, 1)

                def inputs(gi):
                    for n in range(HB):
                        j = gi * HB + n
                        dve.wait_ge(sig, 2 * j + 2)
                        dve.tensor_tensor(bu[:, j % (2 * HB), :], ig[:, j % IG, :], uc[0:RW, groups[gi][1] * HB + n, :], ALU.mult).then_inc(bus, 1)

                def complements(gi):
                    for j in range(gi * HB, (gi + 1) * HB):
                        dve.wait_ge(exps, 2 * j + 2)
                        dve.wait_ge(sqs, j + 1)
                        dve.scalar_tensor_tensor(r[:, j % (2 * HB), :], sq[:, j % 2, :], 1.0, r[:, j % (2 * HB), :], ALU.add, ALU.mult).then_inc(omts, 1)

                def recur(gi):
                    d, h = groups[gi]
                    for n in range(HB):
                        j, ch = gi * HB + n, h * HB + n
                        A, B = a[:, j % (2 * HB), :], bu[:, j % (2 * HB), :]
                        dve.wait_ge(roots, j + 1)
                        dve.wait_ge(bus, j + 1)
                        chain.link(dve.tensor_tensor(B, B, r[:, j % (2 * HB), :], ALU.mult))
                        lat, ctx = slice(0, SEQ), slice(SEQ, TOK)
                        if d == 0:
                            chain.link(dve.tensor_tensor_scan(hc[:, j % 2, :], A[:, ctx], B[:, ctx], 0.0, ALU.mult, ALU.add))
                            dve.tensor_tensor_scan(hsum[0:RW, ch, :], A[:, lat], B[:, lat], hc[:, j % 2, CTX - 1:CTX], ALU.mult, ALU.add).then_inc(scans, 1)
                        else:
                            rev = lambda v: v[:, ::-1]
                            chain.link(dve.tensor_tensor_scan(rev(hc[:, j % 2, :]), rev(A[:, ctx]), rev(B[:, ctx]), 0.0, ALU.mult, ALU.add))
                            chain.link(dve.tensor_tensor_scan(rev(back[:, j % 2, :]), rev(A[:, lat]), rev(B[:, lat]), hc[:, j % 2, 0:1], ALU.mult, ALU.add))
                            dve.tensor_tensor(hsum[0:RW, ch, :], hsum[0:RW, ch, :], back[:, j % 2, :], ALU.add).then_inc(scans, 1)

                inputs(0)
                for gi in range(len(groups)):
                    complements(gi)
                    if gi + 1 < len(groups):
                        inputs(gi + 1)
                    recur(gi)
                dve.wait_ge(scans, len(blocks))
                for n in range(RB):
                    dve.wait_ge(gturned, n + 1)
                    dve.tensor_tensor(hsum[0:RW, n, :], hsum[0:RW, n, :], g.ps[0:RW, 6 + n % 2, 0:SEQ], ALU.mult).then_inc(gated, 1)


def load_mod_phase(g, layer, dsts):
    nc = g.nc
    mod_in = g.sem(f"mod_in{layer}")
    with nc.Block() as block:
        @block.sync
        def _(sp):
            for dst, stream, n in dsts:
                sp.dma_start(dst, g.mod_rows[layer, stream, 0:n * D].partition_broadcast(P).rearrange("p (m d) -> p m d", d=D)).then_inc(mod_in, 16)
            sp.wait_ge(mod_in, 16 * len(dsts))

        if layer == 0:
            @block.vector
            def _(dve):
                dve.tensor_copy(g.ident_bf[:], g.ident)
                dve.tensor_copy(g.mask_bf[:], g.field("mask"))
                dve.tensor_copy(g.before_bf[:], g.field("before"))
                dve.memset(g.ones_bf[:], 1.0)
                dve.memset(g.ones[:], 1.0)
                dve.memset(g.eps[:], EPS)


def final_phase(g):
    nc = g.nc
    with ExitStack() as st:
        sb = lambda n, s, d=F32: st.enter_context(nc.sbuf_tensor("f_" + n, s, d))
        gain = sb("gain", [P, D])
        y = sb("y", [P, LAT_TILES, D])
        sumsq, root, junk = sb("sumsq", [P, LAT_TILES]), sb("root", [P, LAT_TILES]), sb("junk", [P, D])
        gain_in, squares, rooted, recip, ready, stored = (g.sem("f_" + n) for n in ("gain_in", "squares", "rooted", "recip", "ready", "stored"))
        with nc.Block() as block:
            @block.sync
            def _(sp):
                sp.dma_start(gain[:], g.ins["final_g"].partition_broadcast(P)).then_inc(gain_in, 16)
                for t in range(LAT_TILES):
                    sp.wait_ge(ready, t + 1)
                    sp.dma_start(g.out[0, t * P:(t + 1) * P, :], y[:, t, :]).then_inc(stored, 16)
                sp.wait_ge(stored, 16 * LAT_TILES)

            @block.scalar
            def _(act):
                for t in range(LAT_TILES):
                    act.activation(junk[:], g.x[:, t, :], ACT.Square, accum_out=sumsq[:, t:t + 1]).then_inc(squares, 1)
                    act.wait_ge(squares, t + 1)
                act.activation(root[:], sumsq[:], ACT.Sqrt, bias=g.eps[:, 0:1], scale=1.0 / D).then_inc(rooted, 1)

            @block.vector
            def _(dve):
                dve.wait_ge(rooted, 1)
                dve.reciprocal(root[:], root[:]).then_inc(recip, 1)
                dve.wait_ge(recip, 1)
                dve.wait_ge(gain_in, 16)
                for t in range(LAT_TILES):
                    dve.scalar_tensor_tensor(y[:, t, :], g.x[:, t, :], root[:, t:t + 1], gain[:], ALU.mult, ALU.mult).then_inc(ready, 1)


def backbone(nc, ins, table, out):
    with ExitStack() as stack:
        g = Core(nc, stack, ins, table, out)
        sb = lambda n, s, d=F32: stack.enter_context(nc.sbuf_tensor(n, s, d))
        g.table = sb("table", [P, TABLE_W])
        g.x = sb("x_stream", [P, TILES, D])
        g.ident_bf, g.before_bf, g.ones_bf = (sb(n, [P, P], BF16) for n in ("ident_bf", "before_bf", "ones_bf"))
        g.mask_bf = sb("mask_bf", [P, LAT_TILES * SEQ], BF16)
        g.ones = sb("ones", [P, P])
        g.eps = sb("eps", [P, 1])
        g.ps = stack.enter_context(nc.psum_tensor("ps", [P, 8, 512], F32))
        g.ident = g.field("ident")
        ada_phase(g)

        with ExitStack() as layer:
            sb = lambda n, s, d=F32: layer.enter_context(nc.sbuf_tensor(n, s, d))
            mods = sb("mods0", [P, 2, NMOD, D])
            g.mod = lambda t, m: mods[:, t // LAT_TILES, m, :]
            load_mod_phase(g, 0, [(mods[:, s, :, :], s, NMOD) for s in range(2)])
            with ExitStack() as att:
                sb = lambda n, s, d=F32: att.enter_context(nc.sbuf_tensor(n, s, d))
                qT = sb("qT", [P, HEADS // 2, TOK])
                kT = sb("kT", [P, KV // 2, 2, TOK])
                v = sb("v", [P, TILES, KVD])
                qkv_phase(g, qT, kT, v)
                o = sb("o", [P, TILES, QD])
                attention_phase(g, qT, kT, v, o)
                project_phase(g, "ao", ins["attn_w_o"][0].rearrange("(p k) n -> p k n", k=KD), P, KD, TILES, src=o)
            with ExitStack() as moe:
                routes = Routes(lambda n, s, d=F32: moe.enter_context(nc.sbuf_tensor(n, s, d)), 0, TILES)
                route_phase(g, 0, TILES, routes)
                expert_phase(g, 0, TILES, routes)
            combine_phase(g, 0, TILES)
        g.recycle_semaphores()

        with ExitStack() as layer:
            sb = lambda n, s, d=F32: layer.enter_context(nc.sbuf_tensor(n, s, d))
            mod_lat = sb("mod1_lat", [P, NMOD, D])
            mod_ctx = sb("mod1_ctx", [P, 2, D])
            g.mod = lambda t, m: (mod_lat if t < LAT_TILES else mod_ctx)[:, m, :]
            load_mod_phase(g, 1, [(mod_lat[:], 0, NMOD), (mod_ctx[:], 1, 2)])
            with ExitStack() as lru:
                sb = lambda n, s, d=F32: lru.enter_context(nc.sbuf_tensor(n, s, d))
                hsum = sb("hsum", [RP, RB, SEQ])
                with ExitStack() as inner:
                    sb = lambda n, s, d=F32: inner.enter_context(nc.sbuf_tensor(n, s, d))
                    par = sb("par", [RW, 11 * RB])
                    uc = sb("uc", [RP, RB, TOK])
                    gate = sb("gate", [P, LAT_TILES, RNN])
                    lru_in_phase(g, par, uc, gate)
                    lru_scan_phase(g, par, uc, gate, hsum)
                project_phase(g, "lo", ins["lru_w_out"][0].rearrange("(n c) d -> c n d", c=RW), RW, RB, LAT_TILES, srcT=hsum)
            with ExitStack() as moe:
                routes = Routes(lambda n, s, d=F32: moe.enter_context(nc.sbuf_tensor(n, s, d)), 1, LAT_TILES)
                route_phase(g, 1, LAT_TILES, routes)
                expert_phase(g, 1, LAT_TILES, routes)
            combine_phase(g, 1, LAT_TILES)
        final_phase(g)


_INS = ["x", "c", "ctx", "c_ctx", "ada_w", "ada_b", "norm1_g", "norm2_g", "attn_w_qkv", "attn_w_o", "attn_sink",
        "lru_w_in", "lru_conv_w", "lru_conv_b", "lru_wa", "lru_ba", "lru_wx", "lru_bx", "lru_lam", "lru_w_out",
        "moe_router_w", "moe_router_bias", "moe_w_gate", "moe_w_up", "moe_w_down",
        "shared_w_gate", "shared_w_up", "shared_w_down", "final_g"]


def shape_table():
    import numpy as np

    f = np.float32
    tab = np.zeros((P, TABLE_W), f)

    def put(name, a):
        lo, hi = FIELD[name]
        a = np.asarray(a, f)
        tab[0:a.shape[0], lo:hi] = a

    r = np.arange(P)
    e = np.arange(EXPERTS)
    put("ident", np.eye(P))
    put("before", r[:, None] < r[None, :])
    put("iota", np.tile(r, (P, 1)))
    q, k = np.arange(SEQ), np.arange(SEQ)
    mask = np.where(np.abs(q[:, None] - k[None, :]) <= WINDOW, 0.0, NEG)
    put("mask", mask.reshape(LAT_TILES, P, SEQ).transpose(1, 0, 2).reshape(P, -1))
    put("before_e", np.concatenate([e[:, None] < e[None, :], np.ones((EXPERTS, 1), bool)], 1))
    put("upto_e", e[:, None] <= e[None, :])
    gg = np.arange(GROUPS)
    put("lower_g", np.tile((gg[None, :] < gg[:, None]).reshape(1, -1), (P, 1)))
    put("tok", r[:, None] + P * np.arange(TILES)[None, :])
    for layer, tiles in enumerate((TILES, LAT_TILES)):
        put(f"negbase{layer}", np.tile(-slots_of(tiles) * np.arange(NBMAX), (P, 1)))
    put("iota_b", np.tile(np.arange(NBMAX), (P, 1)))
    nf = HD // 4
    inv = np.exp(f(-math.log(ROPE_THETA)) * np.arange(nf, dtype=f) / f(nf)).astype(f)
    tok = np.arange(SEQ)
    row = (tok // GRID_W).astype(f)[:, None] * inv
    col = (tok % GRID_W).astype(f)[:, None] * inv
    cos = np.concatenate([np.cos(row), np.cos(row), np.cos(col), np.cos(col)], 1)
    sin = np.concatenate([-np.sin(row), np.sin(row), -np.sin(col), np.sin(col)], 1)
    tiled = lambda a: a.reshape(LAT_TILES, P, HD).transpose(1, 0, 2).reshape(P, -1)
    put("rope_c", tiled(cos))
    put("rope_s", tiled(sin))
    return tab


def kernel(**inputs):
    import numpy as _np
    import concourse.bacc as _bacc
    from concourse import mybir as _mybir
    from concourse.bass_utils import run_bass_kernel_spmd as _run

    nc = _bacc.Bacc("TRN2", target_bir_lowering=False, num_devices=1)
    arrays, ins = {}, {}
    for name in _INS:
        a = _np.ascontiguousarray(inputs[name])
        arrays[f"in_{name}"] = a
        ins[name] = nc.dram_tensor(f"in_{name}", a.shape, _mybir.dt.from_np(a.dtype), kind="ExternalInput").ap()
    arrays["in_table"] = shape_table()
    table = nc.dram_tensor("in_table", arrays["in_table"].shape, F32, kind="ExternalInput").ap()
    out = nc.dram_tensor("out_0", (1, SEQ, D), F32, kind="ExternalOutput").ap()
    backbone(nc, ins, table, out)
    r = _run(nc, [arrays], core_ids=[0])
    return r.results[0]["out_0"]
```

```python
import math

import concourse.bass as bass
from concourse import mybir
from contextlib import ExitStack

F32 = mybir.dt.float32
BF16 = mybir.dt.bfloat16
F32R = mybir.dt.float32r
I32 = mybir.dt.int32
U32 = mybir.dt.uint32
ALU = mybir.AluOpType
ACT = mybir.ActivationFunctionType
AX = mybir.AxisListType

P = 128
D = 1024
KD = D // P
SEQ = 256
CTX = 256
TOK = SEQ + CTX
LAT_TILES = SEQ // P
TILES = TOK // P
NMOD = 6
SH1, SC1, GATE1, SH2, SC2, GATE2 = range(NMOD)
EPS = 1e-6
GRID_W = 64
ROPE_THETA = 10000.0

HEADS = 16
KV = 4
GROUP = HEADS // KV
HD = 64
QD = HEADS * HD
KVD = KV * HD
QKV = QD + 2 * KVD
WINDOW = 128
SCALE = HD ** -0.5
NEG = -1e30

RNN = 1280
RB = 16
RW = RNN // RB
RP = 96
TAPS = 4
LEFT = 2

EXPERTS = 64
TOPK = 8
GROUPS = 8
PER_GROUP = EXPERTS // GROUPS
TOP_GROUPS = 4
FE = 256
KF = FE // P
ROUTED_SCALE = 2.5
FAR = 8192.0


def slots_of(tiles):
    return tiles * P // 4


def max_blocks(tiles):
    extra = (tiles * P * TOPK - EXPERTS) // slots_of(tiles)
    return (EXPERTS + extra + 1) // 2 * 2


NBMAX = max_blocks(TILES) + 8

_FIELDS = [("ident", P), ("before", P), ("iota", P), ("mask", LAT_TILES * SEQ), ("before_e", EXPERTS + 1),
           ("upto_e", EXPERTS), ("lower_g", GROUPS * GROUPS), ("tok", TILES), ("negbase0", NBMAX), ("negbase1", NBMAX),
           ("iota_b", NBMAX), ("first_b", NBMAX), ("rope_c", LAT_TILES * HD), ("rope_s", LAT_TILES * HD)]
FIELD = {}
_at = 0
for _name, _width in _FIELDS:
    FIELD[_name] = (_at, _at + _width)
    _at += _width
TABLE_W = _at


class Chain:

    def __init__(self, eng, sem):
        self.eng, self.sem, self.n = eng, sem, 0

    def done(self, ins):
        self.n += 1
        ins.then_inc(self.sem, 1)
        return self.n

    def link(self, ins):
        self.eng.wait_ge(self.sem, self.done(ins))


class Core:

    def __init__(self, nc, stack, ins, table, out):
        self.nc, self.stack, self.ins, self.out = nc, stack, ins, out
        self.table_dram = table
        self.mod_rows = nc.dram_tensor("mod_rows", (2, 2, NMOD * D), F32, kind="Internal").ap()
        self.h2_rows = nc.dram_tensor("h2_rows", (TOK, D), F32, kind="Internal").ap()
        self.y_rows = nc.dram_tensor("y_rows", (TOK * TOPK, D), F32, kind="Internal").ap()

        self.mod_layer = 0
        self.sems = []

    def sem(self, name):
        self.sems.append(self.nc.alloc_semaphore(name=name))
        return self.sems[-1]

    def recycle_semaphores(self):
        self.nc.clear_and_free_semaphores(self.sems)
        self.nc.all_engine_barrier()
        self.sems = []

    def mod_slots(self, first, n):
        return self.mods[:, first:first + n, :] if first < 8 else self.mods_rest[:, first - 8:first - 8 + n, :]

    def mod(self, t, m):
        return self.mod_slots(MOD_SLOT[self.mod_layer][t // LAT_TILES][m], 1)[:, 0, :]

    def mod_source(self, layer, stream, a, b):
        rows = self.mod_rows[layer, stream, a * D:b * D]
        return rows.partition_broadcast(P).rearrange("p (m d) -> p m d", d=D)

    def field(self, name, rows=P):
        a, b = FIELD[name]
        return self.table[0:rows, a:b]


def ada_phase(g):
    nc, ins = g.nc, g.ins
    HALF = NMOD * D // 2
    BUFS = 4
    NB = HALF // 512
    with ExitStack() as st:
        sb = lambda n, s, d=F32: st.enter_context(nc.sbuf_tensor(n, s, d))
        wbuf = sb("ada_wbuf", [P, BUFS, HALF])
        craw = sb("ada_craw", [P, 2, KD])
        cs = sb("ada_cs", [P, KD, 2])
        row = sb("ada_row", [2, 2, HALF])
        bias = sb("ada_bias", [2, 2, HALF])
        gains = sb("ada_gains", [2, 2, D])
        w_ready = [g.sem(f"ada_w_ready{i}") for i in range(BUFS)]
        small = [g.sem(f"ada_small{i}") for i in range(2)]
        c_ready, c_silu, used, bank_done = g.sem("ada_c_ready"), g.sem("ada_c_silu"), g.sem("ada_used"), g.sem("ada_bank_done")
        evac, row_ready, mod_in = g.sem("ada_evac"), g.sem("ada_row_ready"), g.sem("mod_in0")
        stored, x_in, consts = g.sem("ada_stored"), g.sem("x_in"), g.sem("consts")
        tiles = [(l, h, k) for l in range(2) for h in range(2) for k in range(KD)]
        halves = [(l, h) for l in range(2) for h in range(2)]
        part = lambda h: slice(h * HALF, (h + 1) * HALF)
        norm = NormRows(g, "n1", lambda t: g.mod(t, SH1), lambda t: g.mod(t, SC1))

        with nc.Block() as block:
            @block.sync
            def _(sp):
                sp.dma_start(craw[:, 0, :], ins["c"].rearrange("o (p k) -> p (o k)", k=KD)).then_inc(c_ready, 16)
                sp.dma_start(craw[:, 1, :], ins["c_ctx"].rearrange("(p k) -> p k", k=KD)).then_inc(c_ready, 16)
                for n, (l, h, k) in enumerate(tiles):
                    if n >= BUFS:
                        half, chunk = divmod(n - BUFS, KD)
                        if chunk == KD - 1:
                            sp.wait_ge(bank_done, NB * (half + 1))
                        else:
                            sp.wait_ge(used, (KD - 1) * half + chunk + 1)
                    src = ins["ada_w"][l].rearrange("(p k) n -> p k n", k=KD)[:, k, part(h)]
                    sp.dma_start(wbuf[:, n % BUFS, :], src).then_inc(w_ready[n % BUFS], 16)

            @block.gpsimd
            def _(pool):
                pool.dma_start(g.table[:], g.table_dram).then_inc(x_in, 16)
                for n, (l, h) in enumerate(halves):
                    if n == 2:
                        pool.dma_start(g.x[:, 0:LAT_TILES, :], ins["x"][0].rearrange("(t p) d -> p t d", p=P)).then_inc(x_in, 16)
                        pool.dma_start(g.x[:, LAT_TILES:TILES, :], ins["ctx"][0].rearrange("(t p) d -> p t d", p=P)).then_inc(x_in, 16)
                    if n >= 2:
                        pool.wait_ge(row_ready, n - 1)
                    pool.dma_start(bias[:, n % 2, :], ins["ada_b"][l, part(h)].partition_broadcast(2)).then_inc(small[n % 2], 16)
                    pool.dma_start(gains[:, n % 2, :], ins["norm2_g" if h else "norm1_g"][l].partition_broadcast(2)).then_inc(small[n % 2], 16)

            @block.scalar
            def _(act):
                act.wait_ge(c_ready, 32)
                for s in range(2):
                    act.activation(cs[:, :, s], craw[:, s, :], ACT.Silu).then_inc(c_silu, 1)
                act.wait_ge(consts, 1)
                act.wait_ge(x_in, 48)
                for t in range(TILES):
                    norm.act(act, t)
                for n, (l, h) in enumerate(halves):
                    act.wait_ge(row_ready, n + 1)
                    act.dma_start(g.mod_rows[l, :, part(h)], row[:, n % 2, :]).then_inc(stored, 16)
                    if l == 0:
                        act.wait_ge(stored, 16 * (n + 1))
                        for dst, stream, a, b in MOD_LOADS[h]:
                            act.dma_start(g.mod_slots(dst, b - a), g.mod_source(0, stream, a, b)).then_inc(mod_in, 16)
                act.wait_ge(stored, 16 * len(halves))
                act.wait_ge(mod_in, 16 * (len(MOD_LOADS[0]) + len(MOD_LOADS[1])))

            @block.tensor
            def _(pe):
                pe.wait_ge(c_silu, 2)
                for n, (l, h, k) in enumerate(tiles):
                    pe.wait_ge(w_ready[n % BUFS], 16 * (n // BUFS + 1))
                    for j in range(NB):
                        if k == 0 and n:
                            pe.wait_ge(evac, NB * (n // KD - 1) + j + 1)
                        last = pe.matmul(g.ps[0:2, j, :], cs[:, k, :], wbuf[:, n % BUFS, j * 512:(j + 1) * 512],
                                         start=(k == 0), stop=(k == KD - 1))
                        if k == KD - 1:
                            last.then_inc(bank_done, 1)
                    if k < KD - 1:
                        last.then_inc(used, 1)

            @block.vector
            def _(dve):
                dve.memset(g.eps[:], EPS).then_inc(consts, 1)
                dve.memset(g.ones_bf[:], 1.0)
                dve.memset(g.ones[:], 1.0)
                dve.wait_ge(x_in, 48)
                dve.tensor_copy(g.ident_bf[:], g.ident)
                dve.tensor_copy(g.mask_bf[:], g.field("mask"))
                dve.tensor_copy(g.before_bf[:], g.field("before"))
                for n in range(len(halves)):
                    dve.wait_ge(small[n % 2], 32 * (n // 2 + 1))
                    if n >= 2:
                        dve.wait_ge(stored, 16 * (n - 1))
                    for j in range(NB):
                        cols = slice(j * 512, (j + 1) * 512)
                        dve.wait_ge(bank_done, NB * n + j + 1)
                        dve.tensor_tensor(row[:, n % 2, cols], g.ps[0:2, j, :], bias[:, n % 2, cols], ALU.add).then_inc(evac, 1)
                    dve.wait_ge(evac, NB * (n + 1))
                    r = row[:, n % 2, D:2 * D]
                    dve.scalar_tensor_tensor(r, r, 1.0, gains[:, n % 2, :], ALU.add, ALU.mult).then_inc(row_ready, 1)
                    if n == 1:
                        dve.wait_ge(mod_in, 16 * (len(MOD_LOADS[0]) + len(MOD_LOADS[1])))
                        for t in range(TILES):
                            norm.dve(dve, t)


MOD_LOADS = [[(0, 0, 0, 3), (5, 1, 0, 3)], [(3, 0, 3, 5), (8, 0, 5, 6), (9, 1, 3, 6)]]
MOD_LOADS1 = [(0, 0, 0, 2), (6, 1, 0, 2), (2, 0, 2, 6)]
MOD_SLOT = [([0, 1, 2, 3, 4, 8], [5, 6, 7, 9, 10, 11]), ([0, 1, 2, 3, 4, 5], [6, 7])]


class NormRows:

    def __init__(self, g, tag, shift, gain):
        self.g, self.shift, self.gain = g, shift, gain
        self.squared, self.rooted = g.sem(tag + "_squared"), g.sem(tag + "_rooted")
        self.steps, self.ready = g.sem(tag + "_steps"), g.sem(tag + "_ready")

    def act(self, act, t):
        g = self.g
        act.activation(g.junk[:], g.x[:, t, :], ACT.Square, accum_out=g.sumsq[:, t:t + 1]).then_inc(self.squared, 1)
        act.wait_ge(self.squared, t + 1)
        act.activation(g.root[:, t:t + 1], g.sumsq[:, t:t + 1], ACT.Sqrt, bias=g.eps[:, 0:1], scale=1.0 / D).then_inc(self.rooted, 1)

    def dve(self, dve, t):
        g, h = self.g, self.g.h[:, t, :]
        dve.wait_ge(self.rooted, t + 1)
        dve.reciprocal(g.rstd[:, t:t + 1], g.root[:, t:t + 1]).then_inc(self.steps, 1)
        dve.wait_ge(self.steps, 2 * t + 1 if self.shift else t + 1)
        rows = dve.scalar_tensor_tensor(h, g.x[:, t, :], g.rstd[:, t:t + 1], self.gain(t), ALU.mult, ALU.mult)
        if self.shift is None:
            rows.then_inc(self.ready, 1)
            return
        rows.then_inc(self.steps, 1)
        dve.wait_ge(self.steps, 2 * t + 2)
        dve.tensor_tensor(h, h, self.shift(t), ALU.add).then_inc(self.ready, 1)


class Turned:

    def __init__(self, g, tag, sb, tiles):
        self.g, self.tiles = g, tiles
        self.hT = sb(tag + "_hT", [P, KD, tiles * P])
        self.turned, self.hT_act, self.hT_dve = g.sem(tag + "_turned"), g.sem(tag + "_hT_act"), g.sem(tag + "_hT_dve")

    def act_evacuate(self, act, t):
        act.wait_ge(self.turned, t + 1)
        act.activation(self.hT[:, 0:KD // 2, t * P:(t + 1) * P],
                       self.g.ps[:, 0, :].rearrange("p (k c) -> p k c", c=P), ACT.Copy).then_inc(self.hT_act, 1)

    def dve_evacuate(self, dve, t):
        dve.wait_ge(self.turned, t + 1)
        dve.tensor_copy(self.hT[:, KD // 2:KD, t * P:(t + 1) * P],
                        self.g.ps[:, 1, :].rearrange("p (k c) -> p k c", c=P)).then_inc(self.hT_dve, 1)

    def pe_turn(self, pe, t):
        if t:
            self.wait_hT(pe, t - 1)
        for k in range(KD):
            last = pe.transpose(self.g.ps[:, k // 4, (k % 4) * P:(k % 4 + 1) * P], self.g.h[:, t, k::KD], self.g.ident)
        last.then_inc(self.turned, 1)

    def wait_hT(self, eng, t):
        eng.wait_ge(self.hT_act, t + 1)
        eng.wait_ge(self.hT_dve, t + 1)


def qkv_phase(g, qT, kT, v):
    nc, ins = g.nc, g.ins
    PAIRS = HEADS // 2
    CH = 256
    NCH = QKV // CH
    HALF_Q = QD // 2
    with ExitStack() as st:
        sb = lambda n, s, d=F32: st.enter_context(nc.sbuf_tensor(n, s, d))
        h_hi = sb("n1_h_hi", [P, KD, TOK], F32R)
        h_lo = sb("n1_h_lo", [P, KD, TOK], F32R)
        w_hi = sb("qkv_w_hi", [P, 2, KD, CH], F32R)
        w_lo = sb("qkv_w_lo", [P, 2, KD, CH], F32R)
        w = qT[:].rearrange("p m c -> p (m c)").rearrange("p (q k c) -> p q k c", q=2, c=CH)
        qk = sb("qk", [P, TILES, QD + KVD])
        rot = g.h[:, 0, 0:CH]
        w_ready = [g.sem(f"qkv_w_ready{q}") for q in range(2)]
        WPARTS = 4
        KW = KD // WPARTS
        w_first = [g.sem(f"qkv_w_first{m}") for m in range(WPARTS)]
        hturned, h_high, h_split, hi_s, lo_s = (g.sem("qkv_" + n) for n in ("hturned", "h_high", "h_split", "hi_s", "lo_s"))
        projected, chain_s, kz = g.sem("qkv_projected"), g.sem("qkv_chain"), g.sem("k_zeroed")
        evac_a, evac_v = g.sem("qkv_evac_act"), g.sem("qkv_evac_dve")
        turned, turned_a, turned_v = g.sem("qk_turned"), g.sem("qk_turned_act"), g.sem("qk_turned_dve")
        jobs = [(c, t) for c in range(NCH) for t in range(TILES)]
        BANKS = 3
        on_dve = lambda n: jobs[n][1] < LAT_TILES and jobs[n][0] < NCH - 1
        count = lambda n, dve: sum(on_dve(m) == dve for m in range(n + 1))
        parts = [(0, m * KW, (m + 1) * KW) for m in range(WPARTS)] + [(c, 0, KD) for c in range(1, NCH)]
        part_of = lambda c: WPARTS + c - 1
        chunks = [("q", m) for m in range(PAIRS)] + [("k", m) for m in range(KV // 2)]

        def evacuated(eng, n):
            eng.wait_ge(evac_v if on_dve(n) else evac_a, count(n, on_dve(n)))

        with nc.Block() as block:
            @block.sync
            def _(sp):
                src = ins["attn_w_qkv"][0].rearrange("(p k) n -> p k n", k=KD)
                for n, (c, k0, k1) in enumerate(parts):
                    if c >= 2:
                        sp.wait_ge(lo_s, part_of(c - 2) + 1 if c > 2 else WPARTS)
                    done = w_first[n] if c == 0 else w_ready[c % 2]
                    if c < NCH - 2:
                        half, a = divmod(c, 2)
                        for s in range(2):
                            c0 = half * HALF_Q + s * (HALF_Q // 2) + a * (CH // 2)
                            sp.dma_start(w[:, c % 2, k0:k1, s * (CH // 2):(s + 1) * (CH // 2)],
                                         src[:, k0:k1, c0:c0 + CH // 2]).then_inc(done, 16)
                    else:
                        sp.dma_start(w[:, c % 2, k0:k1, :], src[:, k0:k1, c * CH:(c + 1) * CH]).then_inc(done, 16)

            def chunk_loaded(c):
                return 16 * sum((2 if b < NCH - 2 else 1) for b in range(1, c + 1) if b % 2 == c % 2)

            def turned_out(copy, m, done):
                kind, i = chunks[m]
                ps = g.ps[:, 6 + m % 2, :]
                if kind == "q":
                    copy(qT[:, i, :], ps).then_inc(done, 1)
                else:
                    copy(kT[0:HD, i, 0, :], ps[0:HD, :]).then_inc(done, 1)
                    copy(kT[HD:P, i, 1, :], ps[HD:P, :]).then_inc(done, 1)

            @block.scalar
            def _(act):
                def rows_high(t):
                    act.wait_ge(hturned, t + 1)
                    for b in range(2):
                        act.activation(h_hi[:, 4 * b:4 * b + 4, t * P:(t + 1) * P],
                                       g.ps[:, b, :].rearrange("p (k c) -> p k c", c=P), ACT.Copy).then_inc(h_high, 1)

                def weights_high(n):
                    c, k0, k1 = parts[n]
                    if c == 0:
                        act.wait_ge(w_first[n], 32)
                    else:
                        act.wait_ge(w_ready[c % 2], chunk_loaded(c))
                    if c >= 2:
                        act.wait_ge(projected, TILES * (c - 1))
                    act.activation(w_hi[:, c % 2, k0:k1, :], w[:, c % 2, k0:k1, :], ACT.Copy).then_inc(hi_s, 1)

                rows_high(0)
                for n in range(WPARTS):
                    weights_high(n)
                for t in range(1, TILES):
                    rows_high(t)
                    if t == 2:
                        weights_high(part_of(1))
                for n, (c, t) in enumerate(jobs):
                    if not on_dve(n):
                        act.wait_ge(projected, n + 1)
                        dst = v[:, t, :] if c == NCH - 1 else qk[:, t, c * CH:(c + 1) * CH]
                        act.activation(dst, g.ps[:, 2 + n % BANKS, 0:CH], ACT.Copy).then_inc(evac_a, 1)
                    if t == TILES - 1 and c + 2 < NCH:
                        weights_high(part_of(c + 2))
                act.wait_ge(kz, 1)
                for m in range(1, len(chunks), 2):
                    act.wait_ge(turned, m + 1)
                    turned_out(lambda o, i: act.activation(o, i, ACT.Copy), m, turned_a)

            @block.vector
            def _(dve):
                chain = Chain(dve, chain_s)

                def rows_low(t):
                    for b in range(2):
                        dve.wait_ge(h_high, 2 * t + b + 1)
                        part = (slice(None), slice(4 * b, 4 * b + 4), slice(t * P, (t + 1) * P))
                        dve.tensor_tensor(h_lo[part], g.ps[:, b, :].rearrange("p (k c) -> p k c", c=P),
                                          h_hi[part].bitcast(F32), ALU.subtract).then_inc(h_split, 1)

                def weights_low(n):
                    c, k0, k1 = parts[n]
                    dve.wait_ge(hi_s, n + 1)
                    dve.tensor_tensor(w_lo[:, c % 2, k0:k1, :], w[:, c % 2, k0:k1, :],
                                      w_hi[:, c % 2, k0:k1, :].bitcast(F32), ALU.subtract).then_inc(lo_s, 1)

                rows_low(0)
                for n in range(WPARTS):
                    weights_low(n)
                for t in range(1, TILES):
                    rows_low(t)
                    if t == 2:
                        weights_low(part_of(1))
                nh = CH // HD
                heads = lambda a: a.rearrange("p (h d) -> p h d", d=HD)
                halves = lambda a: a.rearrange("p (h x s f) -> p h x s f", x=2, s=2, f=HD // 4)
                for n, (c, t) in enumerate(jobs):
                    if c and t == 0 and c + 1 < NCH:
                        weights_low(part_of(c + 1))
                    if not on_dve(n):
                        continue
                    ps, out = g.ps[:, 2 + n % BANKS, 0:CH], qk[:, t, c * CH:(c + 1) * CH]
                    c0, s0 = (FIELD[f][0] + t * HD for f in ("rope_c", "rope_s"))
                    cos = g.table[:, c0:c0 + HD][:, None, :].to_broadcast([P, nh, HD])
                    sin = g.table[:, s0:s0 + HD].rearrange("p (x s f) -> p x s f", x=2, s=2)
                    dve.wait_ge(projected, n + 1)
                    chain.done(dve.tensor_tensor(heads(out), heads(ps), cos, ALU.mult))
                    for s in range(2):
                        last = chain.done(dve.tensor_tensor(halves(rot)[:, :, :, s, :], halves(ps)[:, :, :, 1 - s, :],
                                                            sin[:, None, :, s, :].to_broadcast([P, nh, 2, HD // 4]), ALU.mult))
                    dve.wait_ge(chain_s, last)
                    dve.tensor_tensor(out, out, rot, ALU.add).then_inc(evac_v, 1)
                    dve.wait_ge(evac_v, count(n, True))
                dve.wait_ge(kz, 1)
                for m in range(0, len(chunks), 2):
                    dve.wait_ge(turned, m + 1)
                    turned_out(dve.tensor_copy, m, turned_v)

            @block.gpsimd
            def _(pool):
                pool.memset(kT[:], 0.0).then_inc(kz, 1)

            @block.tensor
            def _(pe):
                def turn_rows(t):
                    if t:
                        pe.wait_ge(h_split, 2 * t)
                    for k in range(KD):
                        last = pe.transpose(g.ps[:, k // 4, (k % 4) * P:(k % 4 + 1) * P], g.h[:, t, k::KD], g.ident)
                    last.then_inc(hturned, 1)

                turn_rows(0)
                for n, (c, t) in enumerate(jobs):
                    if n + 1 < TILES:
                        turn_rows(n + 1)
                    pe.wait_ge(h_split, 2 * t + 2)
                    if n >= BANKS:
                        evacuated(pe, n - BANKS)
                    for k in range(KD):
                        if n == 0 and k % KW == 0:
                            pe.wait_ge(lo_s, k // KW + 1)
                        elif k == 0 and t == 0:
                            pe.wait_ge(lo_s, part_of(c) + 1)
                        tok = slice(t * P, (t + 1) * P)
                        for m, (h, wp) in enumerate(((h_hi, w_hi), (h_lo, w_hi), (h_hi, w_lo))):
                            cols = wp[:, c % 2, k, :]
                            if c < NCH - 2:
                                cols = cols.rearrange("p (s g d) -> p g s d", s=2, d=HD)
                            last = pe.matmul(g.ps[:, 2 + n % BANKS, 0:CH], h[:, k, tok], cols,
                                             start=(k == 0 and m == 0), stop=(k == KD - 1 and m == 2))
                    last.then_inc(projected, 1)
                pe.wait_ge(evac_a, count(len(jobs) - 1, False))
                pe.wait_ge(evac_v, count(len(jobs) - 1, True))
                for m, (kind, i) in enumerate(chunks):
                    if m >= 2:
                        pe.wait_ge(turned_a if m % 2 else turned_v, m // 2)
                    for t in range(TILES):
                        src = qk[:, t, (QD if kind == "k" else 0) + i * P:(QD if kind == "k" else 0) + (i + 1) * P]
                        last = pe.transpose(g.ps[:, 6 + m % 2, t * P:(t + 1) * P], src, g.ident)
                    last.then_inc(turned, 1)


def attention_phase(g, qT, kT, v, o):
    nc, ins = g.nc, g.ins
    units = [(t, m, s) for t in range(TILES) for m in range(HEADS // 2) for s in range(2)]
    head = lambda m, s: (2 * (m // GROUP) + s) * GROUP + m % GROUP
    first_key = lambda t: 0 if t < LAT_TILES else SEQ
    S_BANKS, AHEAD, LAG = 4, 3, 2
    T_BANK, O_BANK = 4, 6
    with ExitStack() as st:
        sb = lambda n, s, d=F32: st.enter_context(nc.sbuf_tensor(n, s, d))
        prob = sb("prob", [P, S_BANKS, TOK])
        probT = sb("probT", [P, 2, TOK])
        sink = sb("sink", [P, HEADS])
        negsink = sb("negsink", [P, HEADS])
        top = sb("top", [P, len(units)])
        nbias = sb("nbias", [P, TILES, HEADS])
        rowsum = sb("rowsum", [P, TILES, HEADS])
        sinkexp = sb("sinkexp", [P, TILES, HEADS])
        sink_in, scored, biased, exped = g.sem("sink_in"), g.sem("scored"), g.sem("biased"), g.sem("exped")
        turned, evac_a, evac_v, mixed = g.sem("prob_turned"), g.sem("probT_act"), g.sem("probT_dve"), g.sem("mixed")
        chain_s, o_evac, sink_arg, sink_exp = g.sem("att_chain"), g.sem("o_evac"), g.sem("sink_arg"), g.sem("sink_exp")
        HALF = HEADS // 2

        with nc.Block() as block:
            @block.sync
            def _(sp):
                sp.dma_start(sink[:], ins["attn_sink"][0].partition_broadcast(P)).then_inc(sink_in, 16)

            @block.tensor
            def _(pe):
                def scores(u):
                    t, m, s = units[u]
                    if u >= S_BANKS:
                        pe.wait_ge(exped, u - S_BANKS + 1)
                    ps = g.ps[:, u % S_BANKS, :]
                    query, jp = qT[:, m, t * P:(t + 1) * P], m // GROUP
                    if t < LAT_TILES:
                        pe.matmul(ps[:, 0:SEQ], query, kT[:, jp, s, 0:SEQ], start=True, stop=False)
                        pe.matmul(ps[:, 0:SEQ], g.ident_bf[:], g.mask_bf[:, t * SEQ:(t + 1) * SEQ], start=False, stop=True)
                    pe.matmul(ps[:, SEQ:TOK], query, kT[:, jp, s, SEQ:TOK], start=True, stop=True).then_inc(scored, 1)

                def turn(u):
                    t, m, s = units[u]
                    pe.wait_ge(exped, u + 1)
                    if u >= 2:
                        pe.wait_ge(evac_a if u % 2 else evac_v, u // 2)
                    for j in range(first_key(t) // P, TILES):
                        last = pe.transpose(g.ps[:, T_BANK + u % 2, j * P:(j + 1) * P], prob[:, u % S_BANKS, j * P:(j + 1) * P], g.ident)
                    last.then_inc(turned, 1)

                def mix(u):
                    t, m, s = units[u]
                    hd = head(m, s)
                    kvh = hd // GROUP
                    pe.wait_ge(evac_a if u % 2 else evac_v, u // 2 + 1)
                    if t and u % HALF == 0:
                        pe.wait_ge(o_evac, u // HALF - 1)
                    j0 = first_key(t) // P
                    for j in range(j0, TILES):
                        last = pe.matmul(g.ps[:, O_BANK + hd // HALF, (hd % HALF) * HD:(hd % HALF + 1) * HD],
                                         probT[:, u % 2, j * P:(j + 1) * P], v[:, j, kvh * HD:(kvh + 1) * HD],
                                         start=(j == j0), stop=(j == TILES - 1))
                    last.then_inc(mixed, 1)

                for u in range(AHEAD):
                    scores(u)
                for u in range(len(units)):
                    if u + AHEAD < len(units):
                        scores(u + AHEAD)
                    turn(u)
                    if u:
                        mix(u - 1)
                mix(len(units) - 1)

            @block.vector
            def _(dve):
                chain = Chain(dve, chain_s)
                dve.wait_ge(sink_in, 16)
                chain.link(dve.tensor_scalar(negsink[:], sink[:], -1.0, None, ALU.mult))

                def finish(n):
                    t, hs = n // 2, slice(n % 2 * HALF, (n % 2 + 1) * HALF)
                    dve.wait_ge(biased, HALF * (n + 1))
                    dve.tensor_tensor(sinkexp[:, t, hs], nbias[:, t, hs], sink[:, hs], ALU.add).then_inc(sink_arg, 1)
                    dve.wait_ge(sink_exp, n + 1)
                    dve.wait_ge(exped, HALF * (n + 1))
                    chain.link(dve.tensor_tensor(rowsum[:, t, hs], rowsum[:, t, hs], sinkexp[:, t, hs], ALU.add))
                    chain.link(dve.reciprocal(rowsum[:, t, hs], rowsum[:, t, hs]))
                    dve.wait_ge(mixed, HALF * (n + 1))
                    dve.tensor_tensor(o[:, t, n % 2 * 512:(n % 2 + 1) * 512].rearrange("p (h d) -> p h d", d=HD),
                                      g.ps[:, O_BANK + n % 2, :].rearrange("p (h d) -> p h d", d=HD),
                                      rowsum[:, t, hs, None].to_broadcast([P, HALF, HD]), ALU.mult).then_inc(o_evac, 1)

                def copy(w):
                    dve.wait_ge(turned, w + 1)
                    if w >= 2:
                        dve.wait_ge(mixed, w - 1)
                    k0 = first_key(units[w][0])
                    dve.tensor_copy(probT[:, w % 2, k0:TOK], g.ps[:, T_BANK + w % 2, k0:TOK]).then_inc(evac_v, 1)

                for u in range(len(units) + AHEAD):
                    if u < len(units):
                        t, m, s = units[u]
                        hd = head(m, s)
                        dve.wait_ge(scored, u + 1)
                        chain.link(dve.reduce_max(top[:, u:u + 1], g.ps[:, u % S_BANKS, first_key(t):TOK], AX.X))
                        dve.tensor_scalar(nbias[:, t, hd:hd + 1], top[:, u:u + 1], -SCALE, negsink[:, hd:hd + 1],
                                          ALU.mult, ALU.min).then_inc(biased, 1)
                    if u >= LAG and (u - LAG) % 2 == 0 and u - LAG < len(units):
                        copy(u - LAG)
                    if u % HALF == 4 and u >= HALF and u < len(units):
                        finish(u // HALF - 1)
                finish(len(units) // HALF - 1)

            @block.scalar
            def _(act):
                def copy(w):
                    act.wait_ge(turned, w + 1)
                    if w >= 2:
                        act.wait_ge(mixed, w - 1)
                    k0 = first_key(units[w][0])
                    act.activation(probT[:, w % 2, k0:TOK], g.ps[:, T_BANK + w % 2, k0:TOK], ACT.Copy).then_inc(evac_a, 1)

                def sink_terms(n):
                    t, hs = n // 2, slice(n % 2 * HALF, (n % 2 + 1) * HALF)
                    act.wait_ge(sink_arg, n + 1)
                    act.activation(sinkexp[:, t, hs], sinkexp[:, t, hs], ACT.Exp).then_inc(sink_exp, 1)

                for u in range(len(units) + AHEAD):
                    if u < len(units):
                        t, m, s = units[u]
                        hd = head(m, s)
                        k0 = first_key(t)
                        act.wait_ge(biased, u + 1)
                        if u >= S_BANKS:
                            act.wait_ge(turned, u - S_BANKS + 1)
                        act.activation(prob[:, u % S_BANKS, k0:TOK], g.ps[:, u % S_BANKS, k0:TOK], ACT.Exp,
                                       bias=nbias[:, t, hd:hd + 1], scale=SCALE, accum_out=rowsum[:, t, hd:hd + 1]).then_inc(exped, 1)
                    if u >= LAG and (u - LAG) % 2 == 1 and u - LAG < len(units):
                        copy(u - LAG)
                    if u % HALF == 4 and u >= HALF and u < len(units):
                        sink_terms(u // HALF - 1)
                sink_terms(len(units) // HALF - 1)


def project_phase(g, tag, w_dram, kp, nk, tiles, srcT=None, src=None):
    rows = kp if srcT is None else srcT.shape[0]
    nc = g.nc
    with ExitStack() as st:
        sb = lambda n, s, d=F32: st.enter_context(nc.sbuf_tensor(n, s, d))
        w = sb(tag + "_w", [rows, nk, D])
        if srcT is None:
            srcT = sb(tag + "_srcT", [P, KD, tiles * P])
        gated = sb(tag + "_gated", [P, 2, D])
        WG = 2
        late_mods = MOD_LOADS1[2:] if g.mod_layer else []
        mod_in = g.sem(tag + "_mod_in")
        w_ready = [g.sem(f"{tag}_w_ready{i}") for i in range(nk // WG)]
        turned, done, h_stored = g.sem(tag + "_turned"), g.sem(tag + "_done"), g.sem(tag + "_h_stored")
        norm = NormRows(g, tag + "_n2", lambda t: g.mod(t, SH2), lambda t: g.mod(t, SC2))
        turned_a, turned_v = g.sem(tag + "_turned_act"), g.sem(tag + "_turned_dve")
        gated_s, added, padded = g.sem(tag + "_gated_s"), g.sem(tag + "_added"), g.sem(tag + "_padded")

        with nc.Block() as block:
            if rows > kp:
                @block.gpsimd
                def _(pool):
                    pool.memset(w[64:rows, :, :], 0.0).then_inc(padded, 1)

            @block.sync
            def _(sp):
                if rows > kp:
                    sp.wait_ge(padded, 1)
                for i in range(nk // WG):
                    sp.dma_start(w[0:kp, WG * i:WG * (i + 1), :], w_dram[:, WG * i:WG * (i + 1), :]).then_inc(w_ready[i], 16)
                for t in range(tiles):
                    sp.wait_ge(norm.ready, t + 1)
                    sp.dma_start(g.h2_rows[t * P:(t + 1) * P, :], g.h[:, t, :]).then_inc(h_stored, 16)
                sp.wait_ge(h_stored, 16 * tiles)

            @block.tensor
            def _(pe):
                if src is not None:
                    for t in range(tiles):
                        if t:
                            pe.wait_ge(turned_a, t)
                            pe.wait_ge(turned_v, t)
                        for k in range(KD):
                            last = pe.transpose(g.ps[:, k // 4, (k % 4) * P:(k % 4 + 1) * P], src[:, t, k::KD], g.ident)
                        last.then_inc(turned, 1)
                for t in range(tiles):
                    if src is not None:
                        pe.wait_ge(turned_a, t + 1)
                        pe.wait_ge(turned_v, t + 1)
                    if t >= 2:
                        pe.wait_ge(gated_s, t - 1)
                    for k in range(nk):
                        if t == 0 and k % WG == 0:
                            pe.wait_ge(w_ready[k // WG], 16)
                        for j in range(2):
                            last = pe.matmul(g.ps[:, 4 + 2 * (t % 2) + j, :], srcT[:, k, t * P:(t + 1) * P],
                                             w[:, k, j * 512:(j + 1) * 512], start=(k == 0), stop=(k == nk - 1))
                    last.then_inc(done, 1)

            @block.scalar
            def _(act):
                for dst, stream, r0, r1 in late_mods:
                    act.dma_start(g.mod_slots(dst, r1 - r0), g.mod_source(g.mod_layer, stream, r0, r1)).then_inc(mod_in, 16)
                if src is not None:
                    for t in range(tiles):
                        act.wait_ge(turned, t + 1)
                        act.activation(srcT[:, 0:KD // 2, t * P:(t + 1) * P],
                                       g.ps[:, 0, :].rearrange("p (k c) -> p k c", c=P), ACT.Copy).then_inc(turned_a, 1)
                for t in range(tiles):
                    act.wait_ge(added, t + 1)
                    norm.act(act, t)

            @block.vector
            def _(dve):
                if src is not None:
                    for t in range(tiles):
                        dve.wait_ge(turned, t + 1)
                        dve.tensor_copy(srcT[:, KD // 2:KD, t * P:(t + 1) * P],
                                        g.ps[:, 1, :].rearrange("p (k c) -> p k c", c=P)).then_inc(turned_v, 1)
                if late_mods:
                    dve.wait_ge(mod_in, 16 * len(late_mods))
                for t in range(tiles):
                    dve.wait_ge(done, t + 1)
                    if t >= 2:
                        dve.wait_ge(added, t - 1)
                    y = g.ps[:, 4 + 2 * (t % 2):6 + 2 * (t % 2), :].rearrange("p a b -> p (a b)")
                    dve.tensor_tensor(gated[:, t % 2, :], y, g.mod(t, GATE1), ALU.mult).then_inc(gated_s, 1)
                    dve.wait_ge(gated_s, t + 1)
                    dve.tensor_tensor(g.x[:, t, :], g.x[:, t, :], gated[:, t % 2, :], ALU.add).then_inc(added, 1)
                    if t:
                        norm.dve(dve, t - 1)
                norm.dve(dve, tiles - 1)


class Routes:

    def __init__(self, sb, layer, tiles):
        n = f"l{layer}_"
        self.slot = sb(n + "slot", [P, tiles, EXPERTS])
        self.entry = sb(n + "entry", [P, tiles, EXPERTS, 3])
        self.expert = sb(n + "expert", [1, NBMAX], I32)
        self.count = sb(n + "count", [1, 1], I32)


class ExpertWeights:

    def __init__(self, g, sb, layer):
        ins, tag = g.ins, f"m{layer}_"
        self.wgu = sb(tag + "wgu", [P, 2, 2, KD, FE])
        self.wd = sb(tag + "wd", [P, 2, KF, D])
        self.wgu_in = [g.sem(f"{tag}wgu_in{q}") for q in range(2)]
        self.wd_in = [g.sem(f"{tag}wd_in{q}") for q in range(2)]
        self.gate_up_w = [ins[n][layer].rearrange("e (p k) f -> e p k f", k=KD) for n in ("moe_w_gate", "moe_w_up")]
        self.down_w = ins["moe_w_down"][layer].rearrange("e (p j) d -> e p j d", j=KF)

    def gate_up(self, sp, e, q):
        for a, w in enumerate(self.gate_up_w):
            sp.dma_start(self.wgu[:, q, a, :, :], w[bass.ds(e, 1)].rearrange("o p k f -> p (o k) f")).then_inc(self.wgu_in[q], 16)

    def down(self, sp, e, q):
        sp.dma_start(self.wd[:, q, :, :], self.down_w[bass.ds(e, 1)].rearrange("o p j d -> p (o j) d")).then_inc(self.wd_in[q], 16)


def route_phase(g, layer, tiles, routes, weights):
    nc, ins = g.nc, g.ins
    tag = f"r{layer}"
    E, S = EXPERTS, slots_of(tiles)
    full = tiles * P // S
    with ExitStack() as st:
        sb = lambda n, s, d=F32: st.enter_context(nc.sbuf_tensor(f"{tag}_{n}", s, d))
        sem = lambda n: g.sem(f"{tag}_{n}")
        norm = Turned(g, f"n2_{layer}", lambda n, s, d=F32: st.enter_context(nc.sbuf_tensor(n, s, d)), tiles)
        wr = sb("wr", [P, KD, E])
        wgu = sb("wgu", [P, 2, KD, FE])
        wd = sb("wd", [P, KF, D])
        rbias = sb("rbias", [P, E])
        act_g = g.h[:, 0, :].rearrange("p (t f) -> p t f", f=FE)
        hid = g.h[:, 1, :].rearrange("p (t f) -> p t f", f=FE)
        hidT = sb("hidT", [P, 2, KF, P])
        gated = g.h[:, 2, :]
        score = sb("score", [P, tiles, E])
        sel = sb("sel", [P, tiles, E])
        best = sb("best", [P, tiles, GROUPS, 8])
        gscore = sb("gscore", [P, tiles, GROUPS])
        beats = sb("beats", [P, tiles, GROUPS, GROUPS])
        ties = sb("ties", [P, tiles, GROUPS, GROUPS])
        rank = sb("rank", [P, tiles, GROUPS])
        pen = sb("pen", [P, tiles, GROUPS])
        top8 = sb("top8", [P, tiles, 8])
        chosen = sb("chosen", [P, tiles, E])
        chosen_bf = sb("chosen_bf", [P, tiles, E], BF16)
        weight = sb("weight", [P, tiles, E])
        wsum = sb("wsum", [P, tiles])
        kth = sb("kth", [P, tiles, E])
        nblk = sb("nblk", [E, 1])
        over = sb("over", [E, full])
        blkend = sb("blkend", [E, 1])
        covers = sb("covers", [E, NBMAX])
        blkstart = sb("blkstart", [P, E + 1])
        slots_before = sb("slots_before", [P, E])
        w_in, wgu_in, wd_in = sem("w_in"), sem("wgu_in"), sem("wd_in")
        routed, scored, gu_done, silued, hid_s = sem("routed"), sem("scored"), sem("gu_done"), sem("silued"), sem("hid_s")
        turned, hidT_s, y_done, gated_s = sem("hid_turned"), sem("hidT_s"), sem("y_done"), sem("gated_s")
        chain_s, masks, pos_done, nblk_s, ends = sem("chain"), sem("masks"), sem("pos_done"), sem("nblk_s"), sem("ends")
        covers_s, owners, blkstart_s, xadd = sem("covers_s"), sem("owners"), sem("blkstart_s"), sem("xadd")
        GU, POS, ROUTER = 2, 6, 7
        Y = (0, 2 if tiles == TILES else 4)
        ENDS, COUNT = (5 if tiles == TILES else 2), TILES * E

        with nc.Block() as block:
            @block.sync
            def _(sp):
                sp.dma_start(wr[:], ins["moe_router_w"][layer].rearrange("(p k) e -> p k e", k=KD)).then_inc(w_in, 16)
                sp.dma_start(rbias[:], ins["moe_router_bias"][layer].partition_broadcast(P)).then_inc(w_in, 16)
                sp.dma_start(wgu[:, 0, :, :], ins["shared_w_gate"][layer].rearrange("(p k) f -> p k f", k=KD)).then_inc(wgu_in, 16)
                sp.dma_start(wgu[:, 1, :, :], ins["shared_w_up"][layer].rearrange("(p k) f -> p k f", k=KD)).then_inc(wgu_in, 16)
                sp.dma_start(wd[:], ins["shared_w_down"][layer].rearrange("(p j) d -> p j d", j=KF)).then_inc(wd_in, 16)
                for q in range(2):
                    weights.gate_up(sp, q, q)
                    weights.down(sp, q, q)

            @block.tensor
            def _(pe):
                for t in range(tiles):
                    norm.pe_turn(pe, t)
                pe.wait_ge(w_in, 32)
                for t in range(tiles):
                    norm.wait_hT(pe, t)
                    for k in range(KD):
                        last = pe.matmul(g.ps[:, ROUTER, t * E:(t + 1) * E], norm.hT[:, k, t * P:(t + 1) * P], wr[:, k, :],
                                         start=(k == 0), stop=(k == KD - 1))
                last.then_inc(routed, 1)
                pe.wait_ge(wgu_in, 32)
                for t in range(tiles):
                    for k in range(KD):
                        last = pe.matmul(g.ps[:, GU + t, :].rearrange("p (a f) -> p a f", a=2), norm.hT[:, k, t * P:(t + 1) * P],
                                         wgu[:, :, k, :], start=(k == 0), stop=(k == KD - 1))
                    last.then_inc(gu_done, 1)
                pe.wait_ge(masks, 1)
                for t in range(tiles):
                    for t0 in range(t + 1):
                        pe.matmul(g.ps[:, POS, t * E:(t + 1) * E], g.before_bf[:] if t0 == t else g.ones_bf[:],
                                  chosen_bf[:, t0, :], start=(t0 == 0), stop=(t0 == t))
                for t in range(tiles):
                    last = pe.matmul(g.ps[0:E, POS, COUNT:COUNT + 1], chosen_bf[:, t, :], g.ones_bf[:, 0:1], start=(t == 0), stop=(t == tiles - 1))
                last.then_inc(pos_done, 1)

                def turn_hidden(t):
                    pe.wait_ge(hid_s, t + 1)
                    if t == 0:
                        pe.wait_ge(scored, 1)
                    else:
                        pe.wait_ge(hidT_s, t)
                    for j in range(KF):
                        last = pe.transpose(g.ps[:, ROUTER, j * P:(j + 1) * P], hid[:, t, j::KF], g.ident)
                    last.then_inc(turned, 1)

                turn_hidden(0)
                for t in range(tiles):
                    pe.wait_ge(hidT_s, t + 1)
                    if t + 1 < tiles:
                        turn_hidden(t + 1)
                    if t == 0:
                        pe.wait_ge(wd_in, 16)
                    if t >= 2:
                        pe.wait_ge(gated_s, t - 1)
                    for j in range(KF):
                        for n in range(2):
                            last = pe.matmul(g.ps[:, Y[t % 2] + n, :], hidT[:, t % 2, j, :], wd[:, j, n * 512:(n + 1) * 512],
                                             start=(j == 0), stop=(j == KF - 1))
                    last.then_inc(y_done, 1)
                    if t == 0:
                        pe.wait_ge(nblk_s, 1)
                        pe.wait_ge(hid_s, tiles)
                        pe.matmul(g.ps[:, ENDS, 0:E + 1], nblk[:, 0:1].to_broadcast([E, P]), g.field("before_e", E), start=True, stop=True)
                        pe.matmul(g.ps[0:E, ENDS, 128:129], g.field("upto_e", E), nblk[:], start=True, stop=True).then_inc(ends, 1)
                    if t == tiles - 2:
                        pe.wait_ge(covers_s, 1)
                        pe.wait_ge(blkstart_s, 1)
                        pe.matmul(g.ps[:, ENDS, 0:NBMAX], g.ones[0:E, :], covers[:], start=True, stop=True).then_inc(owners, 1)

            @block.scalar
            def _(act):
                for t in range(tiles):
                    norm.act_evacuate(act, t)
                act.wait_ge(routed, 1)
                act.activation(score[:], g.ps[:, ROUTER, 0:tiles * E].rearrange("p (t e) -> p t e", e=E), ACT.Sigmoid).then_inc(scored, 1)
                for t in range(tiles):
                    act.wait_ge(gu_done, t + 1)
                    act.activation(act_g[:, t, :], g.ps[:, GU + t, 0:FE], ACT.Silu).then_inc(silued, 1)
                for t in range(tiles):
                    act.wait_ge(turned, t + 1)
                    if t >= 2:
                        act.wait_ge(y_done, t - 1)
                    act.activation(hidT[:, t % 2, :, :], g.ps[:, ROUTER, 0:FE].rearrange("p (j c) -> p j c", c=P), ACT.Copy).then_inc(hidT_s, 1)

            @block.vector
            def _(dve):
                chain = Chain(dve, chain_s)
                for t in range(tiles):
                    norm.dve_evacuate(dve, t)

                def hidden(t):
                    dve.wait_ge(silued, t + 1)
                    dve.tensor_tensor(hid[:, t, :], act_g[:, t, :], g.ps[:, GU + t, FE:2 * FE], ALU.mult).then_inc(hid_s, 1)

                def shared_out(t):
                    dve.wait_ge(y_done, t + 1)
                    if t:
                        dve.wait_ge(xadd, t)
                    y = g.ps[:, Y[t % 2]:Y[t % 2] + 2, :].rearrange("p a b -> p (a b)")
                    dve.tensor_tensor(gated, y, g.mod(t, GATE2), ALU.mult).then_inc(gated_s, 1)
                    dve.wait_ge(gated_s, t + 1)
                    dve.tensor_tensor(g.x[:, t, :], g.x[:, t, :], gated, ALU.add).then_inc(xadd, 1)

                dve.wait_ge(scored, 1)
                dve.wait_ge(w_in, 32)
                by_group = lambda a: a.rearrange("p t (g e) -> p t g e", e=PER_GROUP)
                chain.link(dve.tensor_tensor(sel[:], score[:], rbias[:, None, :].to_broadcast([P, tiles, E]), ALU.add))
                for t in range(tiles):
                    for gr in range(GROUPS):
                        last = dve.max(best[:, t, gr, :], sel[:, t, gr * PER_GROUP:(gr + 1) * PER_GROUP])
                        n = chain.done(last)
                dve.wait_ge(chain_s, n)
                chain.link(dve.tensor_tensor(gscore[:], best[:, :, :, 0], best[:, :, :, 1], ALU.add))
                mine = gscore[:, :, :, None].to_broadcast([P, tiles, GROUPS, GROUPS])
                other = gscore[:, :, None, :].to_broadcast([P, tiles, GROUPS, GROUPS])
                lower = g.field("lower_g").rearrange("p (a b) -> p a b", b=GROUPS)
                chain.done(dve.tensor_tensor(beats[:], other, mine, ALU.is_gt))
                chain.link(dve.tensor_tensor(ties[:], other, mine, ALU.is_equal))
                chain.link(dve.tensor_tensor(ties[:], ties[:], lower[:, None, :, :].to_broadcast([P, tiles, GROUPS, GROUPS]), ALU.mult))
                chain.link(dve.tensor_tensor(beats[:], beats[:], ties[:], ALU.add))
                chain.link(dve.tensor_reduce(rank[:], beats[:], AX.X, ALU.add))
                chain.link(dve.tensor_scalar(rank[:], rank[:], float(TOP_GROUPS), None, ALU.is_lt))
                chain.link(dve.tensor_scalar(pen[:], rank[:], -NEG, NEG, ALU.mult, ALU.add))
                wide = lambda a: a[:, :, :, None].to_broadcast([P, tiles, GROUPS, PER_GROUP])
                chain.link(dve.tensor_tensor(by_group(sel[:]), by_group(sel[:]), wide(rank[:]), ALU.mult))
                chain.link(dve.tensor_tensor(by_group(sel[:]), by_group(sel[:]), wide(pen[:]), ALU.add))
                for t in range(tiles):
                    n = chain.done(dve.max(top8[:, t, :], sel[:, t, :]))
                dve.wait_ge(chain_s, n)
                for t in range(tiles):
                    n = chain.done(dve.match_replace(chosen[:, t, :], top8[:, t, :], sel[:, t, :], -3e38))
                dve.wait_ge(chain_s, n)
                chain.link(dve.tensor_scalar(chosen[:], chosen[:], -2e38, None, ALU.is_lt))
                dve.tensor_copy(chosen_bf[:], chosen[:]).then_inc(masks, 1)
                for t in range(tiles):
                    hidden(t)
                dve.wait_ge(pos_done, 1)
                for j in range(1, full):
                    chain.link(dve.tensor_scalar(over[:, j:j + 1], g.ps[0:E, POS, COUNT:COUNT + 1], float(S * j), None, ALU.is_gt))
                dve.tensor_reduce(nblk[:], over[:, 1:full], AX.X, ALU.add).then_inc(nblk_s, 1)
                chain.link(dve.tensor_tensor(weight[:], score[:], chosen[:], ALU.mult))
                chain.link(dve.tensor_reduce(wsum[:], weight[:], AX.X, ALU.add))
                chain.link(dve.reciprocal(wsum[:], wsum[:]))
                chain.link(dve.tensor_scalar(wsum[:], wsum[:], ROUTED_SCALE, None, ALU.mult))
                chain.done(dve.tensor_tensor(routes.entry[:, :, :, 1], weight[:], wsum[:, :, None].to_broadcast([P, tiles, E]), ALU.mult))
                for t in range(tiles):
                    n = chain.done(dve.tensor_tensor_scan(kth[:, t, :], g.ones[:, 0:E], chosen[:, t, :], 0.0, ALU.mult, ALU.add))
                tok = g.field("tok")[:, 0:tiles]
                chain.done(dve.tensor_scalar(routes.entry[:, :, :, 0], tok[:, :, None].to_broadcast([P, tiles, E]), -FAR, None, ALU.add))
                dve.wait_ge(chain_s, n)
                for t in range(tiles):
                    chain.link(dve.tensor_scalar(wsum[:, t:t + 1], tok[:, t:t + 1], float(TOPK), -1.0 - FAR, ALU.mult, ALU.add))
                    chain.done(dve.tensor_scalar(routes.entry[:, t, :, 2], kth[:, t, :], wsum[:, t:t + 1], None, ALU.add))
                shared_out(0)
                dve.wait_ge(ends, 1)
                dve.tensor_copy(blkstart[:], g.ps[:, ENDS, 0:E + 1]).then_inc(blkstart_s, 1)
                chain.link(dve.tensor_scalar(blkend[:], g.ps[0:E, ENDS, 128:129], float(E), None, ALU.add))
                dve.tensor_scalar(covers[:], g.field("iota_b", E), blkend[:, 0:1], None, ALU.is_ge).then_inc(covers_s, 1)
                dve.wait_ge(blkstart_s, 1)
                chain.link(dve.tensor_scalar(routes.count[:], blkstart[0:1, E:E + 1], float(E - 3), None, ALU.add))
                pos = g.ps[:, POS, 0:tiles * E].rearrange("p (t e) -> p t e", e=E)
                per_expert = lambda a: a[:, None, 0:E].to_broadcast([P, tiles, E])
                chain.done(dve.tensor_scalar(slots_before[:], g.field("iota")[:, 0:E], float(S), 1.0, ALU.mult, ALU.add))
                chain.link(dve.tensor_tensor(blkstart[:, 0:E], blkstart[:, 0:E], g.field("iota")[:, 0:E], ALU.subtract))
                chain.done(dve.tensor_scalar(routes.slot[:], pos, float(S), None, ALU.is_ge))
                chain.link(dve.tensor_scalar(blkstart[:, 0:E], blkstart[:, 0:E], float(S), float(S * (E - 1)), ALU.mult, ALU.add))
                chain.link(dve.tensor_tensor(routes.slot[:], routes.slot[:], per_expert(blkstart), ALU.mult))
                chain.link(dve.tensor_tensor(routes.slot[:], routes.slot[:], pos, ALU.add))
                chain.link(dve.tensor_tensor(routes.slot[:], routes.slot[:], per_expert(slots_before), ALU.add))
                chain.link(dve.tensor_tensor(routes.slot[:], routes.slot[:], chosen[:], ALU.mult))
                chain.link(dve.tensor_scalar(routes.slot[:], routes.slot[:], -1.0, None, ALU.add))
                for t in range(1, tiles - 1):
                    shared_out(t)
                dve.wait_ge(owners, 1)
                chain.link(dve.scalar_tensor_tensor(routes.expert[:], g.ps[0:1, ENDS, 0:NBMAX], float(E - 1),
                                                    g.field("first_b", 1), ALU.min, ALU.add))
                shared_out(tiles - 1)


def expert_phase(g, layer, tiles, routes, weights):
    nc, ins = g.nc, g.ins
    tag = f"m{layer}"
    S = slots_of(tiles)
    last_token, last_row = tiles * P - 1, tiles * P * TOPK - 1
    with ExitStack() as st:
        sb = lambda n, s, d=F32: st.enter_context(nc.sbuf_tensor(f"{tag}_{n}", s, d))
        sem = lambda n: g.sem(f"{tag}_{n}")
        wgu, wd, wgu_in, wd_in = weights.wgu, weights.wd, weights.wgu_in, weights.wd_in
        xg = [g.h[0:S, q, :] for q in range(2)]
        CHUNKS = 4
        KC = KD // CHUNKS
        w_hi = sb("w_hi", [P, 2, KD, FE], F32R)
        w_lo = sb("w_lo", [P, 2, KD, FE], F32R)
        x_hi = sb("x_hi", [P, 2, KD, S], F32R)
        x_lo = sb("x_lo", [P, 2, KD, S], F32R)
        onehot = sb("onehot", [P, 2, tiles, S])
        meta = sb("meta", [S, NBMAX, 3])
        gidx = [sb(f"gidx{q}", [S, 1], U32) for q in range(2)]
        sidx = [sb(f"sidx{q}", [S, 1], U32) for q in range(2)]
        act_g = sb("act_g", [S, FE])
        hid = sb("hid", [S, FE])
        hidT = sb("hidT", [P, KF, S])
        ysb = [g.h[0:S, 2 + q, :] for q in range(2)]
        pair = lambda n: [sem(n + "0"), sem(n + "1")]
        gathered, scattered = pair("gathered"), pair("scattered")
        onehot_s, meta_done, idx_s, xT_turned, x_high, x_split = (sem(n) for n in ("onehot_s", "meta_done", "idx_s", "xT_turned", "x_high", "x_split"))
        silued, hid_s, hid_turned, hidT_s = (sem(n) for n in ("silued", "hid_s", "hid_turned", "hidT_s"))
        y_done, y_a, y_v, sidx_s, zeroed, issue, meta_v = (sem(n) for n in ("y_done", "y_a", "y_v", "sidx_s", "zeroed", "issue", "meta_v"))
        hi_s, lo_s, chunk_used = (sem(n) for n in ("hi_s", "lo_s", "chunk_used"))
        GU, YB, XB, HB, MB = 0, 1, 3, 5, 6

        def last_pair(eng):
            return (eng.value_load(routes.count[0:1, 0:1], min_val=EXPERTS - 3, max_val=max_blocks(tiles) - 3) >> 1) + 1

        def owner(eng, b):
            return eng.value_load(routes.expert[0:1, bass.ds(b, 1)], min_val=0, max_val=EXPERTS - 1)

        def after_wait(eng):
            eng.sem_inc(issue, 1)

        with nc.Block() as block:
            @block.sync
            def _(sp):
                def gate_up(i, q):
                    b = 2 * i + q
                    e = owner(sp, b)
                    sp.wait_ge(lo_s, CHUNKS * b - CHUNKS)
                    after_wait(sp)
                    weights.gate_up(sp, e, q)

                def down(i, q):
                    b = 2 * i + q
                    e = owner(sp, b)
                    sp.wait_ge(y_done, b - 1)
                    after_wait(sp)
                    weights.down(sp, e, q)

                final = last_pair(sp)
                gate_up(1, 0)
                gate_up(1, 1)
                down(1, 0)
                with sp.Fori(2, final + 1) as i:
                    gate_up(i, 0)
                    down(i - 1, 1)
                    gate_up(i, 1)
                    down(i, 0)
                down(final, 1)

            @block.gpsimd
            def _(pool):
                def gather(i, q):
                    b = 2 * i + q
                    pool.wait_ge(idx_s, b + 1)
                    if not (isinstance(i, int) and i == 0):
                        pool.wait_ge(xT_turned, b - 1)
                    after_wait(pool)
                    pool.indirect_dma_start(xg[q], None, g.h2_rows[0:tiles * P, :], bass.IndirectOffsetOnAxis(ap=gidx[q][:, 0:1], axis=0),
                                            bounds_check=last_token, oob_is_err=False).then_inc(gathered[q], 16)

                def scatter(i, q):
                    b = 2 * i + q
                    pool.wait_ge(y_a, b + 1)
                    pool.wait_ge(y_v, b + 1)
                    pool.wait_ge(sidx_s, b + 1)
                    after_wait(pool)
                    pool.indirect_dma_start(g.y_rows[0:tiles * P * TOPK, :], bass.IndirectOffsetOnAxis(ap=sidx[q][:, 0:1], axis=0), ysb[q], None,
                                            bounds_check=last_row, oob_is_err=False).then_inc(scattered[q], 16)

                for q in range(2):
                    pool.memset(xg[q], 0.0).then_inc(zeroed, 1)
                pool.wait_ge(zeroed, 2)
                final = last_pair(pool)
                gather(0, 0)
                gather(0, 1)
                gather(1, 0)
                gather(1, 1)
                scatter(0, 0)
                gather(2, 0)
                with pool.Fori(1, final + 1) as i:
                    scatter(i - 1, 1)
                    gather(i + 1, 1)
                    scatter(i, 0)
                    gather(i + 2, 0)
                scatter(final, 1)
                for q in range(2):
                    pool.wait_ge(scattered[q], 16 * final + 16)
                    after_wait(pool)
                    pool.wait_ge(gathered[q], 16 * final + (32 if q else 48))
                    after_wait(pool)

            @block.tensor
            def _(pe):
                def slots(i, q):
                    b = 2 * i + q
                    e = owner(pe, b)
                    pe.wait_ge(onehot_s, b + 1)
                    if not (isinstance(i, int) and i == 0):
                        pe.wait_ge(idx_s, b - 1)
                    for t in range(tiles):
                        last = pe.matmul(g.ps[0:S, MB + q, 0:3], onehot[:, q, t, :],
                                         routes.entry[:, t, bass.ds(e, 1), :].rearrange("p o c -> p (o c)"),
                                         start=(t == 0), stop=(t == tiles - 1))
                    last.then_inc(meta_done, 1)

                def turn_tokens(i, q, first=False):
                    b = 2 * i + q
                    pe.wait_ge(gathered[q], 16 * (i + 1))
                    if not first:
                        pe.wait_ge(x_split, 2 * b)
                    after_wait(pe)
                    for k in range(KD):
                        last = pe.transpose(g.ps[:, XB + k // 4, (k % 4) * S:(k % 4 + 1) * S], xg[q][:, k::KD], g.ident[0:S, 0:S])
                    last.then_inc(xT_turned, 1)

                def down(i, q, first=False):
                    b = 2 * i + q
                    pe.wait_ge(hidT_s, b + 1)
                    pe.wait_ge(wd_in[q], 16 * (i + 1))
                    if not first:
                        pe.wait_ge(y_a, b)
                        pe.wait_ge(y_v, b)
                    for j in range(KF):
                        for n in range(2):
                            last = pe.matmul(g.ps[0:S, YB + n, :], hidT[:, j, :], wd[:, q, j, n * 512:(n + 1) * 512],
                                             start=(j == 0), stop=(j == KF - 1))
                    last.then_inc(y_done, 1)

                def step(i, q):
                    b = 2 * i + q
                    first = isinstance(i, int) and i == 0 and q == 0
                    pe.wait_ge(x_split, 2 * b + 2)
                    if not first:
                        pe.wait_ge(hid_s, b)
                    for c in range(CHUNKS):
                        pe.wait_ge(lo_s, CHUNKS * b + (c + 1))
                        after_wait(pe)
                        for k in range(KC * c, KC * (c + 1)):
                            for n, (x, w) in enumerate(((x_hi, w_hi), (x_lo, w_hi), (x_hi, w_lo))):
                                last = pe.matmul(g.ps[0:S, GU, :].rearrange("p (a f) -> p a f", a=2), x[:, q, k, :],
                                                 w[:, :, k, :], start=(k == 0 and n == 0), stop=(k == KD - 1 and n == 2))
                        last.then_inc(chunk_used, 1)
                    turn_tokens(i + q, 1 - q)
                    if not first:
                        down(i - 1 + q, 1 - q, first=(isinstance(i, int) and i == 0 and q == 1))
                    pe.wait_ge(hid_s, b + 1)
                    if not first:
                        pe.wait_ge(hidT_s, b)
                    after_wait(pe)
                    for j in range(KF):
                        last = pe.transpose(g.ps[:, HB, j * S:(j + 1) * S], hid[:, j::KF], g.ident[0:S, 0:S])
                    last.then_inc(hid_turned, 1)
                    slots(i + 1 + q, 1 - q)

                slots(0, 0)
                slots(0, 1)
                slots(1, 0)
                turn_tokens(0, 0, first=True)
                final = last_pair(pe)
                step(0, 0)
                step(0, 1)
                with pe.Fori(1, final + 1) as i:
                    step(i, 0)
                    step(i, 1)
                down(final, 1)

            @block.scalar
            def _(act):
                def tokens(i, q):
                    b = 2 * i + q
                    act.wait_ge(xT_turned, b + 1)
                    for n in range(2):
                        act.activation(x_hi[:, q, 4 * n:4 * n + 4, :], g.ps[:, XB + n, 0:4 * S].rearrange("p (k c) -> p k c", c=S), ACT.Copy).then_inc(x_high, 1)

                def split_high(i, q, chunks, first=False):
                    b = 2 * i + q
                    if 0 in chunks:
                        act.wait_ge(wgu_in[q], 32 * (i + 1))
                    for c in chunks:
                        if not first:
                            act.wait_ge(chunk_used, CHUNKS * b + (c + 1 - CHUNKS))
                        k = slice(KC * c, KC * (c + 1))
                        act.activation(w_hi[:, :, k, :], wgu[:, q, :, k, :], ACT.Copy).then_inc(hi_s, 1)

                def y_half(i, q, wait=True):
                    b = 2 * i + q
                    act.wait_ge(y_done, b + 1)
                    if wait:
                        act.wait_ge(scattered[q], 16 * i)
                    act.activation(ysb[q][:, 0:512], g.ps[0:S, YB, :], ACT.Copy).then_inc(y_a, 1)

                def step(i, q, wait_y=True, split=True):
                    b = 2 * i + q
                    peeled = isinstance(i, int) and i == 0
                    if split:
                        split_high(i + q, 1 - q, range(CHUNKS - 1))
                    act.wait_ge(chunk_used, CHUNKS * (b + 1))
                    if not (peeled and q == 0):
                        act.wait_ge(hid_s, b)
                    act.activation(act_g[:], g.ps[0:S, GU, 0:FE], ACT.Silu).then_inc(silued, 1)
                    if split:
                        split_high(i + q, 1 - q, range(CHUNKS - 1, CHUNKS))
                    tokens(i + q, 1 - q)
                    if not (peeled and q == 0):
                        y_half(i - 1 + q, 1 - q, wait=wait_y)
                    act.wait_ge(hid_turned, b + 1)
                    act.activation(hidT[:], g.ps[:, HB, 0:KF * S].rearrange("p (j c) -> p j c", c=S), ACT.Copy).then_inc(hidT_s, 1)

                split_high(0, 0, range(CHUNKS), first=True)
                tokens(0, 0)
                final = last_pair(act)
                step(0, 0)
                step(0, 1, wait_y=False)
                step(1, 0, wait_y=False)
                step(1, 1)
                with act.Fori(2, final) as i:
                    step(i, 0)
                    step(i, 1)
                step(final, 0)
                step(final, 1, split=False)
                y_half(final, 1)

            @block.vector
            def _(dve):
                def pick(i, q, wait=True):
                    b = 2 * i + q
                    e = owner(dve, b)
                    if wait:
                        dve.wait_ge(meta_done, b - 1)
                    for t in range(tiles):
                        last = dve.tensor_scalar(onehot[:, q, t, :], g.field("iota")[:, 0:S], routes.slot[:, t, bass.ds(e, 1)],
                                                 g.table[:, bass.ds(b + FIELD[f"negbase{layer}"][0], 1)], ALU.subtract, ALU.is_equal)
                    last.then_inc(onehot_s, 1)

                def indices(i, q, wait=True):
                    b = 2 * i + q
                    dve.wait_ge(meta_done, b + 1)
                    if wait:
                        dve.wait_ge(gathered[q], 16 * i)
                    dve.tensor_copy(meta[:, bass.ds(b, 1), :].rearrange("p o c -> p (o c)"), g.ps[0:S, MB + q, 0:3]).then_inc(meta_v, 1)
                    dve.tensor_scalar(gidx[q][:], g.ps[0:S, MB + q, 0:1], FAR, None, ALU.add).then_inc(idx_s, 1)

                def tokens(i, q):
                    b = 2 * i + q
                    dve.wait_ge(xT_turned, b + 1)
                    for n in range(2):
                        ks = slice(4 * n, 4 * n + 4)
                        dve.wait_ge(x_high, 2 * b + (n + 1))
                        dve.tensor_tensor(x_lo[:, q, ks, :], g.ps[:, XB + n, 0:4 * S].rearrange("p (k c) -> p k c", c=S),
                                          x_hi[:, q, ks, :].bitcast(F32), ALU.subtract).then_inc(x_split, 1)

                def split_low(i, q, chunks):
                    b = 2 * i + q
                    for c in chunks:
                        k = slice(KC * c, KC * (c + 1))
                        dve.wait_ge(hi_s, CHUNKS * b + (c + 1))
                        dve.tensor_tensor(w_lo[:, :, k, :], wgu[:, q, :, k, :], w_hi[:, :, k, :].bitcast(F32), ALU.subtract).then_inc(lo_s, 1)

                def y_half(i, q, wait=True):
                    b = 2 * i + q
                    if wait:
                        dve.wait_ge(scattered[q], 16 * i)
                    dve.tensor_scalar(sidx[q][:], meta[:, bass.ds(b, 1), 2], FAR, None, ALU.add).then_inc(sidx_s, 1)
                    dve.wait_ge(y_done, b + 1)
                    dve.tensor_copy(ysb[q][:, 512:D], g.ps[0:S, YB + 1, :]).then_inc(y_v, 1)

                def step(i, q, first_y=False, split=True):
                    b = 2 * i + q
                    if split:
                        split_low(i + q, 1 - q, range(CHUNKS - 1))
                    first = isinstance(i, int) and i == 0 and q == 0
                    dve.wait_ge(silued, b + 1)
                    dve.wait_ge(meta_v, b + 1)
                    if not first:
                        dve.wait_ge(hid_turned, b)
                    dve.scalar_tensor_tensor(hid[:], act_g[:], meta[:, bass.ds(b, 1), 1], g.ps[0:S, GU, FE:2 * FE],
                                             ALU.mult, ALU.mult).then_inc(hid_s, 1)
                    if split:
                        split_low(i + q, 1 - q, range(CHUNKS - 1, CHUNKS))
                    tokens(i + q, 1 - q)
                    if not first:
                        y_half(i - 1 + q, 1 - q, wait=not first_y)
                    pick(i + 2, q)
                    indices(i + 1 + q, 1 - q)

                pick(0, 0, wait=False)
                pick(0, 1, wait=False)
                indices(0, 0, wait=False)
                indices(0, 1, wait=False)
                pick(1, 0)
                indices(1, 0)
                pick(1, 1)
                split_low(0, 0, range(CHUNKS))
                tokens(0, 0)
                final = last_pair(dve)
                step(0, 0)
                step(0, 1, first_y=True)
                step(1, 0, first_y=True)
                step(1, 1)
                with dve.Fori(2, final) as i:
                    step(i, 0)
                    step(i, 1)
                step(final, 0)
                step(final, 1, split=False)
                y_half(final, 1)


def combine_phase(g, layer, tiles):
    nc = g.nc
    tag = f"c{layer}"
    H = D // 2
    jobs = [(t, h) for t in range(tiles) for h in range(2)]
    with ExitStack() as st:
        sb = lambda n, s, d=F32: st.enter_context(nc.sbuf_tensor(f"{tag}_{n}", s, d))
        rows = sb("rows", [P, 4, TOPK, H])
        total = sb("total", [P, 2, H])
        rows_in = [g.sem(f"{tag}_rows_in{q}") for q in range(4)]
        summed, pe_summed, scaled = g.sem(f"{tag}_summed"), g.sem(f"{tag}_pe_summed"), g.sem(f"{tag}_scaled")
        src = g.y_rows[0:tiles * P * TOPK, :].rearrange("(t p k) d -> t p k d", p=P, k=TOPK)
        added, mod_in, stored = g.sem(f"{tag}_added"), g.sem(f"{tag}_mod_in"), g.sem(f"{tag}_stored")
        gate2 = [g.mod(t, GATE2) for t in range(tiles)]
        if layer == 0:
            g.mod_layer = 1
            norm = NormRows(g, "n3", lambda t: g.mod(t, SH1), lambda t: g.mod(t, SC1))
        else:
            gain = sb("gain", [P, D])
            norm = NormRows(g, "nf", None, lambda t: gain[:])
        with nc.Block() as block:
            @block.sync
            def _(sp):
                def load_mods():
                    for dst, stream, a, b in MOD_LOADS1[0:2]:
                        sp.dma_start(g.mod_slots(dst, b - a), g.mod_source(1, stream, a, b)).then_inc(mod_in, 16)

                for n, (t, h) in enumerate(jobs):
                    if n >= 4:
                        sp.wait_ge(pe_summed if h == 0 else summed, t - 1)
                    sp.dma_start(rows[:, n % 4, :, :], src[t][:, :, h * H:(h + 1) * H]).then_inc(rows_in[n % 4], 16)
                    if n == 1 and layer == 0:
                        load_mods()
                    if n == 1 and layer == 1:
                        sp.dma_start(gain[:], g.ins["final_g"].partition_broadcast(P)).then_inc(mod_in, 16)
                if layer == 1:
                    for t in range(tiles):
                        sp.wait_ge(norm.ready, t + 1)
                        sp.dma_start(g.out[0, t * P:(t + 1) * P, :], g.h[:, t, :]).then_inc(stored, 16)
                    sp.wait_ge(stored, 16 * tiles)

            @block.tensor
            def _(pe):
                for t in range(tiles):
                    pe.wait_ge(rows_in[2 * (t % 2)], 16 * (t // 2 + 1))
                    if t >= 2:
                        pe.wait_ge(scaled, 2 * (t - 1))
                    for k in range(TOPK):
                        last = pe.matmul(g.ps[:, t % 2, :], g.ident, rows[:, 2 * (t % 2), k, :], start=(k == 0), stop=(k == TOPK - 1))
                    last.then_inc(pe_summed, 1)

            @block.scalar
            def _(act):
                for t in range(tiles):
                    act.wait_ge(added, 2 * (t + 1))
                    norm.act(act, t)

            @block.vector
            def _(dve):
                for n, (t, h) in enumerate((t, h) for t in range(tiles) for h in (1, 0)):
                    q = n % 2
                    x = g.x[:, t, h * H:(h + 1) * H]
                    gate = gate2[t][:, h * H:(h + 1) * H]
                    if h == 0:
                        dve.wait_ge(pe_summed, t + 1)
                        sums = g.ps[:, t % 2, :]
                    else:
                        b = 2 * (t % 2) + 1
                        dve.wait_ge(rows_in[b], 16 * (t // 2 + 1))
                        sums = total[:, q, :]
                        dve.tensor_reduce(sums, rows[:, b, :, :].rearrange("p k d -> p d k"), AX.X, ALU.add).then_inc(summed, 1)
                        dve.wait_ge(summed, t + 1)
                    dve.tensor_tensor(total[:, q, :], sums, gate, ALU.mult).then_inc(scaled, 1)
                    dve.wait_ge(scaled, n + 1)
                    dve.tensor_tensor(x, x, total[:, q, :], ALU.add).then_inc(added, 1)
                    if h == 0 and t + 1 < tiles:
                        dve.wait_ge(mod_in, 32 if layer == 0 else 16)
                        norm.dve(dve, t)
                norm.dve(dve, tiles - 1)


BA, BX, LAM, CW, CB = 0, 2, 4, 6, 10


def lru_in_phase(g, par, uc, gate, hsum):
    nc, ins = g.nc, g.ins
    CH = 320
    CB_BLOCKS = CH // RW
    PAD = SEQ + TAPS - 1
    WPARTS = 4
    KW = KD // WPARTS
    with ExitStack() as st:
        sb = lambda n, s, d=F32: st.enter_context(nc.sbuf_tensor(n, s, d))
        h_hi = sb("n3_h_hi", [P, KD, TOK], F32R)
        h_lo = sb("n3_h_lo", [P, KD, TOK], F32R)
        w_hi = sb("lru_w_hi", [P, 2, KD, CH], F32R)
        w_lo = sb("lru_w_lo", [P, 2, KD, CH], F32R)
        spare = g.mods[:].rearrange("p m d -> p (m d)")
        w = spare[:, 0:2 * KD * CH].rearrange("p (q k c) -> p q k c", q=2, c=CH)
        normed = g.h[:].rearrange("p t d -> p (t d)")
        ut = [normed[:, t * RNN:(t + 1) * RNN] for t in range(TILES - 1)] + [spare[:, 2 * KD * CH:2 * KD * CH + RNN]]
        upad = hsum[0:RW, 0:5, :].rearrange("p n c -> p (n c)")[:, 0:4 * PAD].rearrange("p (q s c) -> p q s c", q=2, s=2)
        praw = sb("lru_praw", [96, 2, RW])
        w_ready = [g.sem(f"li_w_ready{q}") for q in range(2)]
        w_first = [g.sem(f"li_w_first{m}") for m in range(WPARTS)]
        hturned, h_high, h_split, hi_s, lo_s = (g.sem("li_" + n) for n in ("hturned", "h_high", "h_split", "hi_s", "lo_s"))
        par_in, par_turned, par_s = g.sem("li_par_in"), g.sem("li_par_turned"), g.sem("li_par_s")
        done, evac, turned, padded = g.sem("li_done"), g.sem("li_evac"), g.sem("li_turned"), g.sem("li_padded")
        padz, chain_s, conv, tap0 = g.sem("li_padz"), g.sem("li_chain"), g.sem("li_conv"), g.sem("li_tap0")
        order = list(range(RNN // CH, 2 * RNN // CH)) + list(range(RNN // CH))
        U = RNN // CH
        jobs = [(i, t) for i in range(len(order)) for t in range(TILES if i < U else LAT_TILES)]
        last_job = [max(n for n, (ii, _) in enumerate(jobs) if ii == i) for i in range(len(order))]
        blocks_after = [[] for _ in jobs]
        for n, (i, t) in enumerate(jobs):
            if 1 <= i <= U:
                per_job = CB_BLOCKS // (TILES if i < U else LAT_TILES)
                first = CB_BLOCKS * (i - 1) + per_job * t
                blocks_after[n] = list(range(first, first + per_job))
        col = lambda s, n: par[:, s * RB + n:s * RB + n + 1]
        parts = [(0, m * KW, (m + 1) * KW) for m in range(WPARTS)] + [(i, 0, KD) for i in range(1, len(order))]
        part_of = lambda i: WPARTS + i - 1

        with nc.Block() as block:
            @block.sync
            def _(sp):
                src = ins["lru_w_in"][0].rearrange("(p k) n -> p k n", k=KD)
                for n, (i, k0, k1) in enumerate(parts):
                    if i >= 2:
                        sp.wait_ge(lo_s, part_of(i - 2) + 1 if i > 2 else WPARTS)
                    sp.dma_start(w[:, i % 2, k0:k1, :], src[:, k0:k1, order[i] * CH:(order[i] + 1) * CH]).then_inc(
                        w_first[n] if i == 0 else w_ready[i % 2], 16)

            @block.gpsimd
            def _(pool):
                for i, name in enumerate(("lru_ba", "lru_bx", "lru_lam")):
                    pool.dma_start(praw[32 * i:32 * i + 32, 0, :], ins[name][0].rearrange("d (n c) -> (d n) c", c=RW)).then_inc(par_in, 16)
                pool.dma_start(praw[0:64, 1, :], ins["lru_conv_w"][0].rearrange("j (n c) -> (j n) c", c=RW)).then_inc(par_in, 16)
                pool.dma_start(praw[64:80, 1, :], ins["lru_conv_b"][0].rearrange("(n c) -> n c", c=RW)).then_inc(par_in, 16)
                pool.memset(upad, 0.0).then_inc(padz, 1)
                pool.wait_ge(padz, 1)
                pool.memset(uc[64:RP, :, :], 0.0).then_inc(padz, 1)

            @block.tensor
            def _(pe):
                def turn_rows(t):
                    if t:
                        pe.wait_ge(h_split, 2 * t)
                    for k in range(KD):
                        last = pe.transpose(g.ps[:, k // 4, (k % 4) * P:(k % 4 + 1) * P], g.h[:, t, k::KD], g.ident)
                    last.then_inc(hturned, 1)

                def turn_block(n):
                    if n >= 2:
                        pe.wait_ge(padded, n - 1)
                    for t in range(TILES):
                        last = pe.transpose(g.ps[0:RW, 4 + n % 2, t * P:(t + 1) * P], ut[t][:, n * RW:(n + 1) * RW], g.ident)
                    last.then_inc(turned, 1)

                turn_rows(0)
                for n, (i, t) in enumerate(jobs):
                    if n + 1 < TILES:
                        turn_rows(n + 1)
                    pe.wait_ge(h_split, 2 * t + 2)
                    if n >= 2:
                        pe.wait_ge(evac, n - 1)
                    for k in range(KD):
                        if n == 0 and k % KW == 0:
                            pe.wait_ge(lo_s, k // KW + 1)
                        elif k == 0 and t == 0:
                            pe.wait_ge(lo_s, part_of(i) + 1)
                        tok = slice(t * P, (t + 1) * P)
                        for m, (h, wp) in enumerate(((h_hi, w_hi), (h_lo, w_hi), (h_hi, w_lo))):
                            last = pe.matmul(g.ps[:, 2 + n % 2, 0:CH], h[:, k, tok], wp[:, i % 2, k, :],
                                             start=(k == 0 and m == 0), stop=(k == KD - 1 and m == 2))
                    last.then_inc(done, 1)
                    if i == 1 and t == 0:
                        pe.wait_ge(par_in, 80)
                        pe.transpose(g.ps[0:RW, 6, 0:96], praw[:, 0, :], g.ident[0:96, 0:96])
                        pe.transpose(g.ps[0:RW, 6, 96:176], praw[0:80, 1, :], g.ident[0:80, 0:80]).then_inc(par_turned, 1)
                    if 1 <= i <= U and t == 0:
                        pe.wait_ge(evac, last_job[i - 1] + 1)
                    for m in blocks_after[n]:
                        turn_block(m)

            @block.scalar
            def _(act):
                def rows_high(t):
                    act.wait_ge(hturned, t + 1)
                    for b in range(2):
                        act.activation(h_hi[:, 4 * b:4 * b + 4, t * P:(t + 1) * P],
                                       g.ps[:, b, :].rearrange("p (k c) -> p k c", c=P), ACT.Copy).then_inc(h_high, 1)

                def weights_high(n):
                    i, k0, k1 = parts[n]
                    act.wait_ge(w_first[n] if i == 0 else w_ready[i % 2], 16 if i == 0 else 16 * (i // 2 + i % 2))
                    if i >= 2:
                        act.wait_ge(done, last_job[i - 2] + 1)
                    act.activation(w_hi[:, i % 2, k0:k1, :], w[:, i % 2, k0:k1, :], ACT.Copy).then_inc(hi_s, 1)

                rows_high(0)
                for n in range(WPARTS):
                    weights_high(n)
                for t in range(1, TILES):
                    rows_high(t)
                    if t == 2:
                        weights_high(part_of(1))
                for n, (i, t) in enumerate(jobs):
                    act.wait_ge(done, n + 1)
                    c0 = (order[i] * CH) % RNN
                    dst, f = (ut[t], ACT.Copy) if i < U else (gate[:, t, :], ACT.Gelu_apprx_tanh)
                    act.activation(dst[:, c0:c0 + CH], g.ps[:, 2 + n % 2, 0:CH], f).then_inc(evac, 1)
                    if n == last_job[i] and i + 2 < len(order):
                        weights_high(part_of(i + 2))
                    if n == last_job[0] + 1:
                        act.wait_ge(par_s, 1)
                        act.wait_ge(padz, 2)
                    for m in blocks_after[n]:
                        q = m % 2
                        act.wait_ge(turned, m + 1)
                        if m >= 2:
                            act.wait_ge(conv, m - 1)
                        act.activation(upad[:, q, :, LEFT:LEFT + SEQ], g.ps[0:RW, 4 + q, :].rearrange("p (s c) -> p s c", s=2), ACT.Copy).then_inc(padded, 1)
                        act.wait_ge(padded, m + 1)
                        act.activation(uc[0:RW, m, :].rearrange("p (s c) -> p s c", s=2), upad[:, q, :, 0:SEQ], ACT.Identity,
                                       bias=col(CB, m), scale=col(CW, m)).then_inc(tap0, 1)

            @block.vector
            def _(dve):
                chain = Chain(dve, chain_s)

                def rows_low(t):
                    for b in range(2):
                        dve.wait_ge(h_high, 2 * t + b + 1)
                        part = (slice(None), slice(4 * b, 4 * b + 4), slice(t * P, (t + 1) * P))
                        dve.tensor_tensor(h_lo[part], g.ps[:, b, :].rearrange("p (k c) -> p k c", c=P),
                                          h_hi[part].bitcast(F32), ALU.subtract).then_inc(h_split, 1)

                def weights_low(n):
                    i, k0, k1 = parts[n]
                    dve.wait_ge(hi_s, n + 1)
                    dve.tensor_tensor(w_lo[:, i % 2, k0:k1, :], w[:, i % 2, k0:k1, :],
                                      w_hi[:, i % 2, k0:k1, :].bitcast(F32), ALU.subtract).then_inc(lo_s, 1)

                rows_low(0)
                for n in range(WPARTS):
                    weights_low(n)
                for t in range(1, TILES):
                    rows_low(t)
                    if t == 2:
                        weights_low(part_of(1))
                dve.wait_ge(par_turned, 1)
                dve.tensor_copy(par[:], g.ps[0:RW, 6, 0:176]).then_inc(par_s, 1)
                dve.wait_ge(par_s, 1)
                for n in range(RB):
                    if n % CB_BLOCKS == 0:
                        weights_low(part_of(n // CB_BLOCKS + 2))
                    q = n % 2
                    dve.wait_ge(tap0, n + 1)
                    u = uc[0:RW, n, :].rearrange("p (s c) -> p s c", s=2)
                    for j in range(1, TAPS):
                        tap = dve.scalar_tensor_tensor(u, upad[:, q, :, j:j + SEQ], col(CW + j, n), u, ALU.mult, ALU.add)
                        if j < TAPS - 1:
                            chain.link(tap)
                    tap.then_inc(conv, 1)
                for i in range(RB // CB_BLOCKS + 2, len(order)):
                    weights_low(part_of(i))


def lru_scan_phase(g, par, uc, gate, hsum):
    nc, ins = g.nc, g.ins
    HB = 4
    IG = 4
    groups = [(d, h) for d in range(2) for h in range(RB // HB)]
    GB = 3
    with ExitStack() as st:
        sb = lambda n, s, d=F32: st.enter_context(nc.sbuf_tensor("ls_" + n, s, d))
        sem = lambda n: g.sem("ls_" + n)
        wa = sb("wa", [RP, 2 * RB, RW])
        wx = sb("wx", [RP, 2 * RB, RW])
        z, w1, dd, lnw, m0 = (sb(n, [RW, 2 * RB]) for n in ("z", "w1", "dd", "lnw", "m0"))
        pos8, neg8 = sb("pos8", [RW, 2 * RB]), sb("neg8", [RW, 2 * RB])
        r = sb("r", [RW, 2 * HB, TOK])
        bu = sb("bu", [RW, 2 * HB, TOK])
        a = sb("a", [RW, 2 * HB, TOK])
        ig = g.h[0:RW, 0:2, :].rearrange("p a (b c) -> p (a b) c", c=TOK)
        sq = g.h[0:RW, 2, :].rearrange("p (b c) -> p b c", c=TOK)
        hc = g.h[0:RW, 3, 0:2 * CTX].rearrange("p (b c) -> p b c", c=CTX)
        back = g.h[0:RW, 3, 2 * CTX:D].rearrange("p (b c) -> p b c", c=SEQ)
        w_in, wa_padded = [sem("w_in0"), sem("w_in1")], sem("wa_padded")
        w_done, zs, ln_s, chain_s = sem("w_done"), sem("zs"), sem("ln_s"), sem("chain")
        rates, sig, bus, exps, sqs, omts, roots, scans = (sem(n) for n in ("rates", "sig", "bus", "exps", "sqs", "omts", "roots", "scans"))
        gturned, gated, acts, padded = sem("gturned"), sem("gated"), sem("acts"), sem("padded")
        lam = par[:, LAM * RB:(LAM + 2) * RB]
        blocks = [(d, h, n) for d, h in groups for n in range(HB)]

        with nc.Block() as block:
            @block.sync
            def _(sp):
                for d in range(2):
                    for dst, name, zeroed in ((wa, "lru_wa", wa_padded), (wx, "lru_wx", padded)):
                        if d == 0:
                            sp.wait_ge(zeroed, 1)
                        sp.dma_start(dst[0:RW, d * RB:(d + 1) * RB, :], ins[name][0, d].rearrange("n c f -> c n f")).then_inc(w_in[d], 16)

            @block.tensor
            def _(pe):
                for j, (d, h, n) in enumerate(blocks):
                    ch = h * HB + n
                    if h == 0 and n == 0:
                        pe.wait_ge(w_in[d], 32)
                    if j >= GB:
                        pe.wait_ge(sig, 2 * (j - GB + 1))
                    b = 2 * (j % GB)
                    pe.matmul(g.ps[0:RW, b, :], wa[:, d * RB + ch, :], uc[:, ch, :], start=True, stop=True)
                    pe.matmul(g.ps[0:RW, b + 1, :], wx[:, d * RB + ch, :], uc[:, ch, :], start=True, stop=True).then_inc(w_done, 1)
                for n in range(RB):
                    if n >= 2:
                        pe.wait_ge(gated, n - 1)
                    for t in range(LAT_TILES):
                        last = pe.transpose(g.ps[0:RW, 6 + n % 2, t * P:(t + 1) * P], gate[:, t, n * RW:(n + 1) * RW], g.ident)
                    last.then_inc(gturned, 1)

            @block.scalar
            def _(act):
                act.activation(z[:], lam, ACT.Abs).then_inc(acts, 1)
                act.wait_ge(acts, 1)
                act.activation(z[:], z[:], ACT.Exp, scale=-1.0).then_inc(zs, 1)
                act.wait_ge(zs, 2)
                act.activation(lnw[:], w1[:], ACT.Ln).then_inc(ln_s, 1)

                def sigmoids(gi):
                    d, h = groups[gi]
                    for n in range(HB):
                        j, ch = gi * HB + n, h * HB + n
                        act.wait_ge(w_done, j + 1)
                        if gi >= 2:
                            act.wait_ge(scans, j - 2 * HB + 1)
                        col = lambda row: par[:, (row + d) * RB + ch:(row + d) * RB + ch + 1]
                        act.activation(r[:, j % (2 * HB), :], g.ps[0:RW, 2 * (j % GB), :], ACT.Sigmoid, bias=col(BA)).then_inc(sig, 1)
                        if j >= IG:
                            act.wait_ge(bus, j - IG + 1)
                        act.activation(ig[:, j % IG, :], g.ps[0:RW, 2 * (j % GB) + 1, :], ACT.Sigmoid, bias=col(BX)).then_inc(sig, 1)

                def decays(gi):
                    d, h = groups[gi]
                    for n in range(HB):
                        j = gi * HB + n
                        c = d * RB + h * HB + n
                        q = j % (2 * HB)
                        act.wait_ge(sig, 2 * (j + 1))
                        act.activation(a[:, q, :], r[:, q, :], ACT.Exp, scale=neg8[:, c:c + 1]).then_inc(exps, 1)
                        act.wait_ge(exps, 2 * j + 1)
                        act.activation(r[:, q, :], r[:, q, :], ACT.Tanh, scale=pos8[:, c:c + 1]).then_inc(exps, 1)

                def square_roots(gi):
                    for j in range(gi * HB, (gi + 1) * HB):
                        act.wait_ge(omts, j + 1)
                        act.activation(r[:, j % (2 * HB), :], r[:, j % (2 * HB), :], ACT.Sqrt).then_inc(roots, 1)

                sigmoids(0)
                act.wait_ge(rates, 1)
                for gi in range(len(groups)):
                    decays(gi)
                    if gi + 1 < len(groups):
                        sigmoids(gi + 1)
                    square_roots(gi)

            @block.gpsimd
            def _(pool):
                for n, t in enumerate((wx, hsum)):
                    pool.memset(t[64:RP, :, :], 0.0).then_inc(padded, 1)
                    pool.wait_ge(padded, n + 1)
                for j in range(len(blocks)):
                    n = j % (2 * HB)
                    pool.wait_ge(exps, 2 * j + 1)
                    if j >= 2:
                        pool.wait_ge(omts, j - 1)
                    pool.tensor_tensor(sq[:, j % 2, :], a[:, n, :], a[:, n, :], ALU.mult).then_inc(sqs, 1)

            @block.vector
            def _(dve):
                chain = Chain(dve, chain_s)
                dve.memset(wa[64:RP, :, :], 0.0).then_inc(wa_padded, 1)
                dve.wait_ge(wa_padded, 1)
                dve.wait_ge(zs, 1)
                dve.tensor_scalar(w1[:], z[:], 1.0, None, ALU.add).then_inc(zs, 1)
                dve.wait_ge(zs, 2)
                chain.link(dve.tensor_scalar(dd[:], w1[:], -1.0, None, ALU.add))
                chain.link(dve.tensor_scalar(m0[:], dd[:], 0.0, None, ALU.is_equal))
                chain.link(dve.tensor_tensor(dd[:], dd[:], m0[:], ALU.add))
                chain.link(dve.reciprocal(dd[:], dd[:]))
                dve.wait_ge(ln_s, 1)
                chain.link(dve.tensor_tensor(lnw[:], lnw[:], m0[:], ALU.add))
                chain.link(dve.tensor_tensor(lnw[:], lnw[:], dd[:], ALU.mult))
                chain.link(dve.tensor_tensor(lnw[:], lnw[:], z[:], ALU.mult))
                chain.link(dve.tensor_scalar(m0[:], lam, -1.0, 0.0, ALU.mult, ALU.max))
                chain.link(dve.tensor_tensor(m0[:], m0[:], lnw[:], ALU.add))
                chain.link(dve.tensor_scalar(pos8[:], m0[:], 8.0, None, ALU.mult))
                dve.tensor_scalar(neg8[:], m0[:], -8.0, None, ALU.mult).then_inc(rates, 1)
                dve.wait_ge(padded, 2)

                def inputs(gi):
                    for n in range(HB):
                        j = gi * HB + n
                        dve.wait_ge(sig, 2 * j + 2)
                        dve.tensor_tensor(bu[:, j % (2 * HB), :], ig[:, j % IG, :], uc[0:RW, groups[gi][1] * HB + n, :], ALU.mult).then_inc(bus, 1)

                def complements(gi):
                    for j in range(gi * HB, (gi + 1) * HB):
                        dve.wait_ge(exps, 2 * j + 2)
                        dve.wait_ge(sqs, j + 1)
                        dve.scalar_tensor_tensor(r[:, j % (2 * HB), :], sq[:, j % 2, :], 1.0, r[:, j % (2 * HB), :], ALU.add, ALU.mult).then_inc(omts, 1)

                def recur(gi):
                    d, h = groups[gi]
                    for n in range(HB):
                        j, ch = gi * HB + n, h * HB + n
                        A, B = a[:, j % (2 * HB), :], bu[:, j % (2 * HB), :]
                        dve.wait_ge(roots, j + 1)
                        dve.wait_ge(bus, j + 1)
                        chain.link(dve.tensor_tensor(B, B, r[:, j % (2 * HB), :], ALU.mult))
                        lat, ctx = slice(0, SEQ), slice(SEQ, TOK)
                        if d == 0:
                            chain.link(dve.tensor_tensor_scan(hc[:, j % 2, :], A[:, ctx], B[:, ctx], 0.0, ALU.mult, ALU.add))
                            dve.tensor_tensor_scan(hsum[0:RW, ch, :], A[:, lat], B[:, lat], hc[:, j % 2, CTX - 1:CTX], ALU.mult, ALU.add).then_inc(scans, 1)
                        else:
                            rev = lambda v: v[:, ::-1]
                            chain.link(dve.tensor_tensor_scan(rev(hc[:, j % 2, :]), rev(A[:, ctx]), rev(B[:, ctx]), 0.0, ALU.mult, ALU.add))
                            chain.link(dve.tensor_tensor_scan(rev(back[:, j % 2, :]), rev(A[:, lat]), rev(B[:, lat]), hc[:, j % 2, 0:1], ALU.mult, ALU.add))
                            dve.tensor_tensor(hsum[0:RW, ch, :], hsum[0:RW, ch, :], back[:, j % 2, :], ALU.add).then_inc(scans, 1)

                inputs(0)
                for gi in range(len(groups)):
                    complements(gi)
                    if gi + 1 < len(groups):
                        inputs(gi + 1)
                    recur(gi)
                dve.wait_ge(scans, len(blocks))
                for n in range(RB):
                    dve.wait_ge(gturned, n + 1)
                    dve.tensor_tensor(hsum[0:RW, n, :], hsum[0:RW, n, :], g.ps[0:RW, 6 + n % 2, 0:SEQ], ALU.mult).then_inc(gated, 1)


def backbone(nc, ins, table, out):
    with ExitStack() as stack:
        g = Core(nc, stack, ins, table, out)
        sb = lambda n, s, d=F32: stack.enter_context(nc.sbuf_tensor(n, s, d))
        g.table = sb("table", [P, TABLE_W])
        g.x = sb("x_stream", [P, TILES, D])
        g.ident_bf, g.before_bf, g.ones_bf = (sb(n, [P, P], BF16) for n in ("ident_bf", "before_bf", "ones_bf"))
        g.mask_bf = sb("mask_bf", [P, LAT_TILES * SEQ], BF16)
        g.ones = sb("ones", [P, P])
        g.eps = sb("eps", [P, 1])
        g.ps = stack.enter_context(nc.psum_tensor("ps", [P, 8, 512], F32))
        g.ident = g.field("ident")
        g.h = sb("h", [P, TILES, D])
        g.junk = sb("squares", [P, D], BF16)
        g.sumsq, g.root, g.rstd = (sb(n, [P, TILES]) for n in ("sumsq", "root", "rstd"))
        g.mods = sb("mods", [P, 8, D])

        with ExitStack() as layer:
            g.mods_rest = layer.enter_context(nc.sbuf_tensor("mods_rest", [P, 4, D], F32))
            ada_phase(g)
            with ExitStack() as att:
                sb = lambda n, s, d=F32: att.enter_context(nc.sbuf_tensor(n, s, d))
                qT = sb("qT", [P, HEADS // 2, TOK])
                kT = sb("kT", [P, KV // 2, 2, TOK])
                v = sb("v", [P, TILES, KVD])
                qkv_phase(g, qT, kT, v)
                o = sb("o", [P, TILES, QD])
                attention_phase(g, qT, kT, v, o)
                project_phase(g, "ao", ins["attn_w_o"][0].rearrange("(p k) n -> p k n", k=KD), P, KD, TILES, src=o)
            with ExitStack() as moe:
                sb = lambda n, s, d=F32: moe.enter_context(nc.sbuf_tensor(n, s, d))
                routes, weights = Routes(sb, 0, TILES), ExpertWeights(g, sb, 0)
                route_phase(g, 0, TILES, routes, weights)
                expert_phase(g, 0, TILES, routes, weights)
            combine_phase(g, 0, TILES)
        g.recycle_semaphores()

        with ExitStack() as layer:
            with ExitStack() as lru:
                sb = lambda n, s, d=F32: lru.enter_context(nc.sbuf_tensor(n, s, d))
                hsum = sb("hsum", [RP, RB, SEQ])
                with ExitStack() as inner:
                    sb = lambda n, s, d=F32: inner.enter_context(nc.sbuf_tensor(n, s, d))
                    par = sb("par", [RW, 11 * RB])
                    uc = sb("uc", [RP, RB, TOK])
                    gate = sb("gate", [P, LAT_TILES, RNN])
                    lru_in_phase(g, par, uc, gate, hsum)
                    lru_scan_phase(g, par, uc, gate, hsum)
                project_phase(g, "lo", ins["lru_w_out"][0].rearrange("(n c) d -> c n d", c=RW), RW, RB, LAT_TILES, srcT=hsum)
            with ExitStack() as moe:
                sb = lambda n, s, d=F32: moe.enter_context(nc.sbuf_tensor(n, s, d))
                routes, weights = Routes(sb, 1, LAT_TILES), ExpertWeights(g, sb, 1)
                route_phase(g, 1, LAT_TILES, routes, weights)
                expert_phase(g, 1, LAT_TILES, routes, weights)
            combine_phase(g, 1, LAT_TILES)


_INS = ["x", "c", "ctx", "c_ctx", "ada_w", "ada_b", "norm1_g", "norm2_g", "attn_w_qkv", "attn_w_o", "attn_sink",
        "lru_w_in", "lru_conv_w", "lru_conv_b", "lru_wa", "lru_ba", "lru_wx", "lru_bx", "lru_lam", "lru_w_out",
        "moe_router_w", "moe_router_bias", "moe_w_gate", "moe_w_up", "moe_w_down",
        "shared_w_gate", "shared_w_up", "shared_w_down", "final_g"]


def shape_table():
    import numpy as np

    f = np.float32
    tab = np.zeros((P, TABLE_W), f)

    def put(name, a):
        lo, hi = FIELD[name]
        a = np.asarray(a, f)
        tab[0:a.shape[0], lo:hi] = a

    r = np.arange(P)
    e = np.arange(EXPERTS)
    put("ident", np.eye(P))
    put("before", r[:, None] < r[None, :])
    put("iota", np.tile(r, (P, 1)))
    q, k = np.arange(SEQ), np.arange(SEQ)
    mask = np.where(np.abs(q[:, None] - k[None, :]) <= WINDOW, 0.0, NEG)
    put("mask", mask.reshape(LAT_TILES, P, SEQ).transpose(1, 0, 2).reshape(P, -1))
    put("before_e", np.concatenate([e[:, None] < e[None, :], np.ones((EXPERTS, 1), bool)], 1))
    put("upto_e", e[:, None] <= e[None, :])
    gg = np.arange(GROUPS)
    put("lower_g", np.tile((gg[None, :] < gg[:, None]).reshape(1, -1), (P, 1)))
    put("tok", r[:, None] + P * np.arange(TILES)[None, :])
    for layer, tiles in enumerate((TILES, LAT_TILES)):
        put(f"negbase{layer}", np.tile(-slots_of(tiles) * np.arange(NBMAX), (P, 1)))
    b = np.arange(NBMAX)
    put("iota_b", np.tile(b, (P, 1)))
    put("first_b", np.tile(np.where(b < EXPERTS, b, 0), (P, 1)))
    nf = HD // 4
    inv = np.exp(f(-math.log(ROPE_THETA)) * np.arange(nf, dtype=f) / f(nf)).astype(f)
    tok = np.arange(SEQ)
    row = (tok // GRID_W).astype(f)[:, None] * inv
    col = (tok % GRID_W).astype(f)[:, None] * inv
    cos = np.concatenate([np.cos(row), np.cos(row), np.cos(col), np.cos(col)], 1)
    sin = np.concatenate([-np.sin(row), np.sin(row), -np.sin(col), np.sin(col)], 1)
    tiled = lambda a: a.reshape(LAT_TILES, P, HD).transpose(1, 0, 2).reshape(P, -1)
    put("rope_c", tiled(cos))
    put("rope_s", tiled(sin))
    return tab


def kernel(**inputs):
    import numpy as _np
    import concourse.bacc as _bacc
    from concourse import mybir as _mybir
    from concourse.bass_utils import run_bass_kernel_spmd as _run

    nc = _bacc.Bacc("TRN2", target_bir_lowering=False, num_devices=1)
    arrays, ins = {}, {}
    for name in _INS:
        a = _np.ascontiguousarray(inputs[name])
        arrays[f"in_{name}"] = a
        ins[name] = nc.dram_tensor(f"in_{name}", a.shape, _mybir.dt.from_np(a.dtype), kind="ExternalInput").ap()
    arrays["in_table"] = shape_table()
    table = nc.dram_tensor("in_table", arrays["in_table"].shape, F32, kind="ExternalInput").ap()
    out = nc.dram_tensor("out_0", (1, SEQ, D), F32, kind="ExternalOutput").ap()
    backbone(nc, ins, table, out)
    r = _run(nc, [arrays], core_ids=[0])
    return r.results[0]["out_0"]
```
